# Optimizing a Trainium2 kernel written in Bass

```python
import math
import jax
import jax.numpy as jnp
from jax import lax
import numpy as np
import jax, jax.numpy as jnp

D_MODEL = 1024
BATCH = 1
SEQ = 256
DEPTH = 2

N_EVEN = (DEPTH + 1) // 2
N_ODD = DEPTH // 2
RMS_EPS = 1e-6

A_HEADS = 8
A_KV_HEADS = 2
A_HEAD_DIM = 64
A_WINDOW = 128
B_HEADS = 4
B_KEY_DIM = 64
B_VAL_DIM = 128
B_GATE_RANK = 16
B_GATE_TAU = 16.0
B_CHUNK = 64
C_HEADS = 8
C_HEAD_DIM = 128
C_BLOCK = 256
C_TOPK = 3
C_ROW_BLOCK = 128
REL_BUCKETS = 32
REL_MAX_DIST = 128
REL_HEADS = 8
MOE_GROUPS = 4
MOE_EXPERTS_PER_GROUP = 8
MOE_EXPERTS = MOE_GROUPS * MOE_EXPERTS_PER_GROUP
MOE_TOPK = 2
MOE_HIDDEN = 512
MOE_ROW_BLOCK = 128

EVEN_SPLITS = (A_HEADS * A_HEAD_DIM, A_KV_HEADS * A_HEAD_DIM, A_KV_HEADS * A_HEAD_DIM,
               B_HEADS * B_KEY_DIM, B_HEADS * B_KEY_DIM, B_HEADS * B_VAL_DIM,
               B_HEADS * B_VAL_DIM, B_GATE_RANK)
EVEN_IN = sum(EVEN_SPLITS)
EVEN_MIX = A_HEADS * A_HEAD_DIM + B_HEADS * B_VAL_DIM
ODD_MIX = C_HEADS * C_HEAD_DIM


def _rms(x, w):
    xf = x.astype(jnp.float32)
    y = xf * lax.rsqrt(jnp.mean(xf * xf, axis=-1, keepdims=True) + RMS_EPS)
    return (y * w.astype(jnp.float32)).astype(x.dtype)

def _rel_bucket(dist):
    exact = REL_BUCKETS // 2
    d = jnp.maximum(dist, 0)
    logd = jnp.log(jnp.maximum(d, 1).astype(jnp.float32) / exact) / math.log(REL_MAX_DIST / exact)
    far = jnp.minimum(exact + (logd * (REL_BUCKETS - exact)).astype(jnp.int32), REL_BUCKETS - 1)
    return jnp.where(d < exact, d, far)

def _group_rows(ids, n_groups, rows):
    n = ids.shape[0]
    n_rows = ((n + rows - 1) // rows) * rows + n_groups * rows
    counts = jnp.zeros((n_groups + 1,), jnp.int32).at[ids].add(1)[:n_groups]
    padded = ((counts + rows - 1) // rows) * rows
    start = jnp.cumsum(counts) - counts
    pend = jnp.cumsum(padded)
    pstart = pend - padded
    order = jnp.argsort(ids)
    sid = ids[order]
    gid = jnp.minimum(sid, n_groups - 1)
    dest = jnp.where(sid < n_groups, pstart[gid] + jnp.arange(n) - start[gid], n_rows)
    src = jnp.full((n_rows,), n, jnp.int32).at[dest].set(order.astype(jnp.int32), mode='drop')
    blk_group = jnp.searchsorted(pend, jnp.arange(n_rows // rows) * rows, side='right')
    return src, jnp.minimum(blk_group, n_groups - 1)

def _swa_sink_attention(q, k, v, sinks, rel_bias):
    B, S, _, hd = q.shape
    W = A_WINDOW
    nb = S // W
    G = A_HEADS // A_KV_HEADS
    f32 = jnp.float32
    qb = q.reshape(B, nb, W, A_KV_HEADS, G, hd)

    def band(t):
        tb = t.reshape(B, nb, W, A_KV_HEADS, hd)
        prev = jnp.pad(tb, ((0, 0), (1, 0), (0, 0), (0, 0), (0, 0)))[:, :-1]
        return jnp.concatenate([prev, tb], axis=2)

    kband, vband = band(k), band(v)
    lg = jnp.einsum('bnqkgd,bnskd->bkgnqs', qb, kband, preferred_element_type=f32) * hd ** -0.5
    dist = jnp.arange(W)[:, None] + W - jnp.arange(2 * W)[None, :]
    mask = ((dist >= 0) & (dist < W)
            & ((jnp.arange(nb)[:, None, None] > 0) | (jnp.arange(2 * W) >= W)[None, None, :]))
    bias = rel_bias[_rel_bucket(dist)].transpose(2, 0, 1).reshape(A_KV_HEADS, G, 1, W, 2 * W)
    lg = jnp.where(mask, lg + bias, -jnp.inf)
    sink = sinks.astype(f32).reshape(A_KV_HEADS, G, 1, 1, 1)
    m = jnp.maximum(lg.max(-1, keepdims=True), sink)
    p = jnp.exp(lg - m)
    probs = p / (p.sum(-1, keepdims=True) + jnp.exp(sink - m))
    o = jnp.einsum('bkgnqs,bnskd->bnqkgd', probs.astype(v.dtype), vband, preferred_element_type=f32)
    return o.reshape(B, S, A_HEADS * hd)

def _gla(q, k, v, log_a):
    B, S, H, dk = q.shape
    dv = v.shape[-1]
    C = B_CHUNK
    n = S // C

    def chunks(t):
        return t.reshape(B, n, C, H, t.shape[-1]).transpose(0, 3, 1, 2, 4)

    q, k, v, g = chunks(q * dk ** -0.5), chunks(k), chunks(v), chunks(log_a)
    b = jnp.cumsum(g, axis=3)
    b_last = b[:, :, :, -1:]
    q_dec = q * jnp.exp(b)
    att = jnp.einsum('bhnid,bhnjd->bhnij', q_dec, k * jnp.exp(-b))
    att = jnp.where(jnp.tril(jnp.ones((C, C), bool)), att, 0.0)
    o_intra = jnp.einsum('bhnij,bhnjv->bhniv', att, v)
    upd = jnp.einsum('bhnjd,bhnjv->bhndv', k * jnp.exp(b_last - b), v)
    decay = jnp.exp(b_last[:, :, :, 0])

    def step(state, inp):
        dec, u = inp
        return state * dec[..., None] + u, state

    _, s_in = lax.scan(step, jnp.zeros((B, H, dk, dv), q.dtype),
                       (decay.transpose(2, 0, 1, 3), upd.transpose(2, 0, 1, 3, 4)))
    o_inter = jnp.einsum('bhnid,bhndv->bhniv', q_dec, s_in.transpose(1, 2, 0, 3, 4))
    return (o_intra + o_inter).transpose(0, 2, 3, 1, 4).reshape(B, S, H, dv)

def _moba(q, k, v, rel_bias):
    B, S, H, hd = q.shape
    L = C_BLOCK
    nb = -(-S // L)
    Sp = nb * L
    k_sel = min(C_TOPK, nb)
    scale = hd ** -0.5
    f32 = jnp.float32
    q, k, v = [jnp.pad(t, ((0, 0), (0, Sp - S), (0, 0), (0, 0))).transpose(0, 2, 1, 3) for t in (q, k, v)]
    qb = q.reshape(B, H, nb, L, hd)
    kb = k.reshape(B, H, nb, L, hd)
    vb = v.reshape(B, H, nb, L, hd)
    li = jnp.arange(L)
    d_own = li[:, None] - li[None, :]
    bias_own = rel_bias[_rel_bucket(d_own)].transpose(2, 0, 1)[None, :, None]
    lg = jnp.einsum('bhnqd,bhnsd->bhnqs', qb, kb, preferred_element_type=f32) * scale + bias_own
    lg = jnp.where(d_own >= 0, lg, -jnp.inf)
    lse_own = jax.nn.logsumexp(lg, axis=-1)
    o_own = jnp.einsum('bhnqs,bhnsd->bhnqd', jnp.exp(lg - lse_own[..., None]).astype(v.dtype), vb,
                       preferred_element_type=f32)
    pos = jnp.arange(Sp)
    qblk = pos // L
    score = jnp.einsum('bhtd,bhjd->bhtj', q.astype(f32), kb.astype(f32).mean(axis=3))
    score = jnp.where(jnp.arange(nb)[None, :] < qblk[:, None], score, -jnp.inf)
    _, sel = lax.top_k(score, k_sel)
    valid = (jnp.arange(k_sel)[None, :] < jnp.minimum(qblk, k_sel)[:, None]) & (pos < S)[:, None]
    n_groups = B * H * nb
    grp = jnp.arange(B * H).reshape(B, H, 1, 1) * nb + sel
    grp = jnp.where(valid, grp, n_groups).reshape(-1)
    src, blk_grp = _group_rows(grp, n_groups, C_ROW_BLOCK)
    n_pairs = grp.shape[0]
    row_ok = src < n_pairs
    row_tok = jnp.minimum(src, n_pairs - 1) // k_sel
    n_tok = B * H * Sp
    q_rows = q.reshape(n_tok, hd)
    k_grp = kb.reshape(n_groups, L, hd)
    v_grp = vb.reshape(n_groups, L, hd)

    def attend_block(args):
        tok, g = args
        qr = q_rows[tok]
        dist = (tok % Sp)[:, None] - ((g % nb) * L + li)[None, :]
        bias = rel_bias[_rel_bucket(dist), (g // nb) % H]
        lg_r = jnp.einsum('rd,sd->rs', qr, k_grp[g], preferred_element_type=f32) * scale + bias
        lse_r = jax.nn.logsumexp(lg_r, axis=-1)
        o_r = jnp.einsum('rs,sd->rd', jnp.exp(lg_r - lse_r[:, None]).astype(v.dtype), v_grp[g],
                         preferred_element_type=f32)
        return o_r, lse_r

    o_sel, lse_sel = lax.map(attend_block, (row_tok.reshape(-1, C_ROW_BLOCK), blk_grp))
    o_sel = o_sel.reshape(-1, hd)
    lse_sel = lse_sel.reshape(-1)
    seg = jnp.where(row_ok, row_tok, n_tok)
    lse_own = lse_own.reshape(n_tok)
    m_sel = jax.ops.segment_max(jnp.where(row_ok, lse_sel, -jnp.inf), seg, num_segments=n_tok + 1)[:n_tok]
    m = jnp.maximum(lse_own, m_sel)
    w_sel = jnp.where(row_ok, jnp.exp(lse_sel - m[jnp.minimum(seg, n_tok - 1)]), 0.0)
    w_own = jnp.exp(lse_own - m)
    num = (w_own[:, None] * o_own.reshape(n_tok, hd)
           + jax.ops.segment_sum(w_sel[:, None] * o_sel, seg, num_segments=n_tok + 1)[:n_tok])
    den = w_own + jax.ops.segment_sum(w_sel, seg, num_segments=n_tok + 1)[:n_tok]
    o = (num / den[:, None]).reshape(B, H, Sp, hd)[:, :, :S]
    return o.transpose(0, 2, 1, 3).reshape(B, S, H * hd).astype(q.dtype)

def _even_mixer(h, w_in, w_out, q_norm, k_norm, sinks, gate_up, gate_bias, out_norm, rel_bias):
    B, S, _ = h.shape
    f32 = jnp.float32
    qa, ka, va, qb, kb, vb, rb, ab = jnp.split(h @ w_in, np.cumsum(EVEN_SPLITS)[:-1].tolist(), axis=-1)
    qa = _rms(qa.reshape(B, S, A_HEADS, A_HEAD_DIM), q_norm)
    ka = _rms(ka.reshape(B, S, A_KV_HEADS, A_HEAD_DIM), k_norm)
    va = va.reshape(B, S, A_KV_HEADS, A_HEAD_DIM)
    oa = _swa_sink_attention(qa, ka, va, sinks, rel_bias).astype(h.dtype)
    log_a = jax.nn.log_sigmoid((ab @ gate_up + gate_bias).astype(f32)) / B_GATE_TAU
    ob = _gla(qb.reshape(B, S, B_HEADS, B_KEY_DIM).astype(f32),
              kb.reshape(B, S, B_HEADS, B_KEY_DIM).astype(f32),
              vb.reshape(B, S, B_HEADS, B_VAL_DIM).astype(f32),
              log_a.reshape(B, S, B_HEADS, B_KEY_DIM))
    ob = _rms(ob, out_norm).astype(h.dtype) * jax.nn.silu(rb).reshape(B, S, B_HEADS, B_VAL_DIM)
    return jnp.concatenate([oa, ob.reshape(B, S, B_HEADS * B_VAL_DIM)], axis=-1) @ w_out

def _odd_mixer(h, w_in, w_out, q_norm, k_norm, rel_bias):
    B, S, _ = h.shape
    q, k, v = jnp.split(h @ w_in, 3, axis=-1)
    q = _rms(q.reshape(B, S, C_HEADS, C_HEAD_DIM), q_norm)
    k = _rms(k.reshape(B, S, C_HEADS, C_HEAD_DIM), k_norm)
    v = v.reshape(B, S, C_HEADS, C_HEAD_DIM)
    return _moba(q, k, v, rel_bias) @ w_out

def _hier_moe(h, w_group, b_group, w_expert, b_expert, w1, w3, w2):
    B, S, D = h.shape
    N = B * S
    f32 = jnp.float32
    xt = h.reshape(N, D)
    g_logits = (xt @ w_group).astype(f32) + b_group.astype(f32)
    g_sel = jnp.argmax(g_logits, axis=-1)
    p_g = jnp.take_along_axis(jax.nn.softmax(g_logits, axis=-1), g_sel[:, None], axis=-1)
    e_logits = ((xt @ w_expert).astype(f32) + b_expert.astype(f32)).reshape(N, MOE_GROUPS, MOE_EXPERTS_PER_GROUP)
    e_in = jnp.take_along_axis(e_logits, g_sel[:, None, None], axis=1)[:, 0]
    top_v, top_i = lax.top_k(e_in, MOE_TOPK)
    gate = (p_g * jax.nn.softmax(top_v, axis=-1)).reshape(-1)
    ids = (g_sel[:, None] * MOE_EXPERTS_PER_GROUP + top_i).reshape(-1)
    src, blk_e = _group_rows(ids, MOE_EXPERTS, MOE_ROW_BLOCK)
    n_pairs = ids.shape[0]
    row_ok = src < n_pairs
    pair = jnp.minimum(src, n_pairs - 1)
    row_tok = pair // MOE_TOPK

    def expert_block(args):
        tok, e = args
        xr = xt[tok]
        return (jax.nn.silu(xr @ w1[e]) * (xr @ w3[e])) @ w2[e]

    y = lax.map(expert_block, (row_tok.reshape(-1, MOE_ROW_BLOCK), blk_e)).reshape(-1, D)
    w_row = jnp.where(row_ok, gate[pair], 0.0).astype(y.dtype)
    seg = jnp.where(row_ok, row_tok, N)
    out = jax.ops.segment_sum(y * w_row[:, None], seg, num_segments=N + 1)[:N]
    return out.reshape(B, S, D)

def first_inputs(seed: int = 0) -> dict:
    key = jax.random.key(seed)
    ks = iter(jax.random.split(key, 32))
    D = D_MODEL

    def nrm(shape, s):
        return jax.random.normal(next(ks), shape, jnp.float32) * s

    return {
        'x': nrm((BATCH, SEQ, D), 1.0),
        'c': nrm((BATCH, D), 1.0),
        'rel_bias': nrm((REL_BUCKETS, REL_HEADS), 0.5),
        'ada_w': nrm((DEPTH, D, 6 * D), 0.5 * D ** -0.5),
        'ada_b': nrm((DEPTH, 6 * D), 0.02),
        'norm1_w': 1.0 + nrm((DEPTH, D), 0.05),
        'norm2_w': 1.0 + nrm((DEPTH, D), 0.05),
        'even_w_in': nrm((N_EVEN, D, EVEN_IN), D ** -0.5),
        'even_w_out': nrm((N_EVEN, EVEN_MIX, D), EVEN_MIX ** -0.5),
        'a_q_norm': 1.0 + nrm((N_EVEN, A_HEAD_DIM), 0.05),
        'a_k_norm': 1.0 + nrm((N_EVEN, A_HEAD_DIM), 0.05),
        'a_sinks': nrm((N_EVEN, A_HEADS), 0.5),
        'b_gate_up': nrm((N_EVEN, B_GATE_RANK, B_HEADS * B_KEY_DIM), B_GATE_RANK ** -0.5),
        'b_gate_bias': nrm((N_EVEN, B_HEADS * B_KEY_DIM), 0.1),
        'b_out_norm': 1.0 + nrm((N_EVEN, B_VAL_DIM), 0.05),
        'odd_w_in': nrm((N_ODD, D, 3 * ODD_MIX), D ** -0.5),
        'odd_w_out': nrm((N_ODD, ODD_MIX, D), ODD_MIX ** -0.5),
        'c_q_norm': 1.0 + nrm((N_ODD, C_HEAD_DIM), 0.05),
        'c_k_norm': 1.0 + nrm((N_ODD, C_HEAD_DIM), 0.05),
        'moe_w_group': nrm((DEPTH, D, MOE_GROUPS), D ** -0.5),
        'moe_b_group': nrm((DEPTH, MOE_GROUPS), 0.01),
        'moe_w_expert': nrm((DEPTH, D, MOE_EXPERTS), D ** -0.5),
        'moe_b_expert': nrm((DEPTH, MOE_EXPERTS), 0.01),
        'moe_w1': nrm((DEPTH, MOE_EXPERTS, D, MOE_HIDDEN), D ** -0.5),
        'moe_w3': nrm((DEPTH, MOE_EXPERTS, D, MOE_HIDDEN), D ** -0.5),
        'moe_w2': nrm((DEPTH, MOE_EXPERTS, MOE_HIDDEN, D), MOE_HIDDEN ** -0.5),
    }

def first_block(x, c, rel_bias, ada_w, ada_b, norm1_w, norm2_w, even_w_in, even_w_out, a_q_norm,
              a_k_norm, a_sinks, b_gate_up, b_gate_bias, b_out_norm, odd_w_in, odd_w_out, c_q_norm,
              c_k_norm, moe_w_group, moe_b_group, moe_w_expert, moe_b_expert, moe_w1, moe_w3, moe_w2):
    cond = jax.nn.silu(c)
    for layer in range(DEPTH):
        mod = (cond @ ada_w[layer] + ada_b[layer])[:, None, :]
        shift1, scale1, gate1, shift2, scale2, gate2 = jnp.split(mod, 6, axis=-1)
        h = _rms(x, norm1_w[layer]) * (1 + scale1) + shift1
        j = layer // 2
        if layer % 2 == 0:
            y = _even_mixer(h, even_w_in[j], even_w_out[j], a_q_norm[j], a_k_norm[j], a_sinks[j],
                            b_gate_up[j], b_gate_bias[j], b_out_norm[j], rel_bias)
        else:
            y = _odd_mixer(h, odd_w_in[j], odd_w_out[j], c_q_norm[j], c_k_norm[j], rel_bias)
        x = x + gate1 * y
        h = _rms(x, norm2_w[layer]) * (1 + scale2) + shift2
        x = x + gate2 * _hier_moe(h, moe_w_group[layer], moe_b_group[layer], moe_w_expert[layer],
                                  moe_b_expert[layer], moe_w1[layer], moe_w3[layer], moe_w2[layer])
    return x


DEPTH_2 = 1

NSA_HEADS = 8
NSA_KV_GROUPS = 2
NSA_HEAD_DIM = 64
NSA_HEADS_PER_GROUP = NSA_HEADS // NSA_KV_GROUPS
NSA_WIDTH = NSA_HEADS * NSA_HEAD_DIM
NSA_KV_WIDTH = NSA_KV_GROUPS * NSA_HEAD_DIM
CMP_LEN = 32
CMP_STRIDE = 16
SLC_LEN = 64
SLC_TOPN = 16
WINDOW = 512
Q_BLOCK = 128
ROPE_THETA = 500000.0
ROPE_DIM = NSA_HEAD_DIM // 4
HG_HEADS = 4
HG_KEY_DIM = 128
HG_VAL_DIM = 128
HG_WIDTH = HG_HEADS * HG_VAL_DIM
HG_CHUNK = 64
N_GROUPS = 4
EXPERTS_PER_GROUP = 8
N_EXPERTS = N_GROUPS * EXPERTS_PER_GROUP
TOP_K_IN_GROUP = 2
D_FF_EXPERT = 512
NEG_INF = -1e30
FORCE_SCORE = 1e4

IN_SPLITS = [NSA_WIDTH, 6 * NSA_KV_WIDTH, 3 * NSA_HEADS,
             HG_HEADS * HG_KEY_DIM, HG_HEADS * HG_KEY_DIM, HG_WIDTH, HG_WIDTH, 2 * D_MODEL]
IN_COLS = sum(IN_SPLITS)


def rmsnorm(x, g):
    x32 = x.astype(jnp.float32)
    y = x32 * lax.rsqrt(jnp.mean(x32 * x32, axis=-1, keepdims=True) + RMS_EPS)
    return (y * g.astype(jnp.float32)).astype(x.dtype)

def partial_rope(t, pos):
    half = ROPE_DIM // 2
    inv_freq = ROPE_THETA ** (-jnp.arange(half, dtype=jnp.float32) / half)
    ang = pos.astype(jnp.float32)[:, None] * inv_freq[None, :]
    cos = jnp.cos(ang)[:, None, :]
    sin = jnp.sin(ang)[:, None, :]
    t1 = t[..., :half]
    t2 = t[..., half:ROPE_DIM]
    return jnp.concatenate([t1 * cos - t2 * sin, t2 * cos + t1 * sin, t[..., ROPE_DIM:]], axis=-1)

def masked_softmax(s, mask):
    s = jnp.where(mask, s, NEG_INF)
    return jax.nn.softmax(s, axis=-1) * mask

def nsa_mixer(q, k_cmp_in, v_cmp_in, k_slc, v_slc, k_win, v_win, gate_logits, w_cmp_k, w_cmp_v, cmp_pos):
    f32 = jnp.float32
    b, s = q.shape[0], q.shape[1]
    G, R, dk = NSA_KV_GROUPS, NSA_HEADS_PER_GROUP, NSA_HEAD_DIM
    pos = jnp.arange(s)
    scale = dk ** -0.5
    q = partial_rope(q.astype(f32), pos).reshape(b, s, G, R, dk)
    k_slc = partial_rope(k_slc.astype(f32), pos)
    k_win = partial_rope(k_win.astype(f32), pos)
    v_slc = v_slc.astype(f32)
    v_win = v_win.astype(f32)
    gates = jax.nn.sigmoid(gate_logits.astype(f32)).reshape(b, s, G, R, 3)

    n_cmp = (s - CMP_LEN) // CMP_STRIDE + 1
    cmp_start = jnp.arange(n_cmp) * CMP_STRIDE
    cmp_end = cmp_start + CMP_LEN - 1
    cmp_idx = cmp_start[:, None] + jnp.arange(CMP_LEN)[None, :]

    def compress(t, w):
        blk = t.astype(f32)[:, cmp_idx] + cmp_pos.astype(f32)[None, None, :, None, :]
        blk = blk.transpose(0, 1, 3, 2, 4).reshape(b, n_cmp, G, CMP_LEN * dk)
        return jnp.einsum('bngc,cd->bngd', blk, w.astype(f32))

    k_cmp = partial_rope(compress(k_cmp_in, w_cmp_k), cmp_start)
    v_cmp = compress(v_cmp_in, w_cmp_v)

    n_sel = s // SLC_LEN
    top_n = min(SLC_TOPN, n_sel)
    sel_start = jnp.arange(n_sel) * SLC_LEN
    blk_ids = jnp.arange(n_sel)
    overlap = ((cmp_start[:, None] < sel_start[None, :] + SLC_LEN) &
               (cmp_end[:, None] >= sel_start[None, :])).astype(f32)
    k_sel_blocks = k_slc.reshape(b, n_sel, SLC_LEN, G, dk).transpose(0, 3, 1, 2, 4)
    v_sel_blocks = v_slc.reshape(b, n_sel, SLC_LEN, G, dk).transpose(0, 3, 1, 2, 4)
    gather_blocks = jax.vmap(jax.vmap(lambda blocks, ids: blocks[ids]))
    slc_offsets = jnp.arange(SLC_LEN)

    k_win_pad = jnp.pad(k_win, ((0, 0), (WINDOW, 0), (0, 0), (0, 0)))
    v_win_pad = jnp.pad(v_win, ((0, 0), (WINDOW, 0), (0, 0), (0, 0)))
    win_offsets = jnp.arange(WINDOW + Q_BLOCK) - WINDOW
    q_offsets = jnp.arange(Q_BLOCK)

    def query_block(c):
        t0 = c * Q_BLOCK
        tpos = t0 + q_offsets
        qb = lax.dynamic_slice_in_dim(q, t0, Q_BLOCK, axis=1)
        gb = lax.dynamic_slice_in_dim(gates, t0, Q_BLOCK, axis=1)
        cmask = cmp_end[None, :] <= tpos[:, None]
        p_cmp = masked_softmax(jnp.einsum('bqgrd,bngd->bgrqn', qb, k_cmp) * scale, cmask)
        o_cmp = jnp.einsum('bgrqn,bngd->bqgrd', p_cmp, v_cmp)
        imp = jnp.einsum('bgrqn,nj->bgqj', p_cmp, overlap)
        force = (blk_ids[None, :] == (tpos // SLC_LEN)[:, None]) | (blk_ids[None, :] == 0)
        valid = sel_start[None, :] <= tpos[:, None]
        score = jnp.where(force, FORCE_SCORE, jnp.where(valid, imp, -1.0))
        _, sel_idx = lax.top_k(score, top_n)
        k_sel = gather_blocks(k_sel_blocks, sel_idx).reshape(b, G, Q_BLOCK, top_n * SLC_LEN, dk)
        v_sel = gather_blocks(v_sel_blocks, sel_idx).reshape(b, G, Q_BLOCK, top_n * SLC_LEN, dk)
        sel_pos = (sel_idx[..., None] * SLC_LEN + slc_offsets).reshape(b, G, Q_BLOCK, top_n * SLC_LEN)
        smask = (sel_pos <= tpos[None, None, :, None])[:, :, None]
        p_slc = masked_softmax(jnp.einsum('bqgrd,bgqmd->bgrqm', qb, k_sel) * scale, smask)
        o_slc = jnp.einsum('bgrqm,bgqmd->bqgrd', p_slc, v_sel)
        kw = lax.dynamic_slice_in_dim(k_win_pad, t0, WINDOW + Q_BLOCK, axis=1)
        vw = lax.dynamic_slice_in_dim(v_win_pad, t0, WINDOW + Q_BLOCK, axis=1)
        kpos = t0 + win_offsets
        rel = tpos[:, None] - kpos[None, :]
        wmask = (rel >= 0) & (rel < WINDOW) & (kpos[None, :] >= 0)
        p_win = masked_softmax(jnp.einsum('bqgrd,bmgd->bgrqm', qb, kw) * scale, wmask)
        o_win = jnp.einsum('bgrqm,bmgd->bqgrd', p_win, vw)
        return gb[..., 0:1] * o_cmp + gb[..., 1:2] * o_slc + gb[..., 2:3] * o_win

    out = lax.map(query_block, jnp.arange(s // Q_BLOCK))
    return out.transpose(1, 0, 2, 3, 4, 5).reshape(b, s, NSA_WIDTH)

def hgrn2_mixer(q, f_logit, i_in, lb):
    f32 = jnp.float32
    b, s = q.shape[0], q.shape[1]
    q = q.astype(f32).reshape(b, s, HG_HEADS, HG_KEY_DIM)
    f = lb + (1.0 - lb) * jax.nn.sigmoid(f_logit.astype(f32).reshape(b, s, HG_HEADS, HG_KEY_DIM))
    log_f = jnp.log(f)
    k = 1.0 - f
    v = i_in.astype(f32).reshape(b, s, HG_HEADS, HG_VAL_DIM)
    n_ch = s // HG_CHUNK

    def to_chunks(t):
        return t.reshape(b, n_ch, HG_CHUNK, HG_HEADS, t.shape[-1]).transpose(1, 0, 3, 2, 4)

    causal = jnp.tril(jnp.ones((HG_CHUNK, HG_CHUNK), dtype=bool))

    def chunk_step(state, inp):
        qc, kc, vc, gc = inp
        bcum = jnp.cumsum(gc, axis=2)
        o_inter = jnp.einsum('bhtk,bhkv->bhtv', qc * jnp.exp(bcum), state)
        rel = jnp.where(causal[:, :, None], bcum[:, :, :, None, :] - bcum[:, :, None, :, :], -jnp.inf)
        attn = jnp.einsum('bhtk,bhsk,bhtsk->bhts', qc, kc, jnp.exp(rel))
        o_intra = jnp.einsum('bhts,bhsv->bhtv', attn, vc)
        b_last = bcum[:, :, -1:, :]
        new_state = (jnp.exp(b_last[:, :, 0, :])[..., None] * state +
                     jnp.einsum('bhsk,bhsv->bhkv', kc * jnp.exp(b_last - bcum), vc))
        return new_state, o_inter + o_intra

    state0 = jnp.zeros((b, HG_HEADS, HG_KEY_DIM, HG_VAL_DIM), f32)
    _, o = lax.scan(chunk_step, state0, (to_chunks(q), to_chunks(k), to_chunks(v), to_chunks(log_f)))
    return o.transpose(1, 0, 3, 2, 4).reshape(b, s, HG_HEADS, HG_VAL_DIM)

def hier_moe(h, w_grp, b_grp, w_rtr, b_rtr, w_gate, w_up, w_down):
    f32 = jnp.float32
    b, s, d = h.shape
    t = h.reshape(b * s, d)
    grp_logits = (t @ w_grp).astype(f32) + b_grp.astype(f32)
    grp_sel = jnp.argmax(grp_logits, axis=-1)
    grp_prob = jnp.take_along_axis(jax.nn.softmax(grp_logits, axis=-1), grp_sel[:, None], axis=1)
    exp_logits = ((t @ w_rtr).astype(f32) + b_rtr.astype(f32)).reshape(-1, N_GROUPS, EXPERTS_PER_GROUP)
    in_grp = jnp.take_along_axis(exp_logits, grp_sel[:, None, None], axis=1)[:, 0]
    top_logits, top_idx = lax.top_k(in_grp, TOP_K_IN_GROUP)
    top_w = jax.nn.softmax(top_logits, axis=-1) * grp_prob
    expert_ids = grp_sel[:, None] * EXPERTS_PER_GROUP + top_idx
    combine = jnp.sum(jax.nn.one_hot(expert_ids, N_EXPERTS, dtype=f32) * top_w[..., None], axis=1)
    out = jnp.zeros((b * s, d), f32)
    for e in range(N_EXPERTS):
        hid = jax.nn.silu(t @ w_gate[e]) * (t @ w_up[e])
        out = out + combine[:, e:e + 1] * (hid @ w_down[e]).astype(f32)
    return out.reshape(b, s, d).astype(h.dtype)

def second_inputs(seed: int = 0) -> dict:
    key = jax.random.key(seed)
    ks = jax.random.split(key, 24)
    f32 = jnp.float32
    nrm = lambda k, shape, scale: jax.random.normal(k, shape, f32) * scale
    return {
        'x': nrm(ks[0], (BATCH, SEQ, D_MODEL), 1.0),
        'attn_norm': 1.0 + nrm(ks[1], (DEPTH_2, D_MODEL), 0.01),
        'w_in': nrm(ks[2], (DEPTH_2, D_MODEL, IN_COLS), D_MODEL ** -0.5),
        'w_cmp_k': nrm(ks[3], (DEPTH_2, CMP_LEN * NSA_HEAD_DIM, NSA_HEAD_DIM), (CMP_LEN * NSA_HEAD_DIM) ** -0.5),
        'w_cmp_v': nrm(ks[4], (DEPTH_2, CMP_LEN * NSA_HEAD_DIM, NSA_HEAD_DIM), (CMP_LEN * NSA_HEAD_DIM) ** -0.5),
        'cmp_pos': nrm(ks[5], (DEPTH_2, CMP_LEN, NSA_HEAD_DIM), 0.02),
        'hg_lb_logits': nrm(ks[6], (DEPTH_2 + 1, HG_HEADS * HG_KEY_DIM), 0.5),
        'hg_norm': 1.0 + nrm(ks[7], (DEPTH_2, HG_VAL_DIM), 0.01),
        'w_br_nsa': nrm(ks[8], (DEPTH_2, NSA_WIDTH, D_MODEL), NSA_WIDTH ** -0.5),
        'w_br_hg': nrm(ks[9], (DEPTH_2, HG_WIDTH, D_MODEL), HG_WIDTH ** -0.5),
        'w_out': nrm(ks[10], (DEPTH_2, D_MODEL, D_MODEL), D_MODEL ** -0.5),
        'ffn_norm': 1.0 + nrm(ks[11], (DEPTH_2, D_MODEL), 0.01),
        'w_grp': nrm(ks[12], (DEPTH_2, D_MODEL, N_GROUPS), D_MODEL ** -0.5),
        'b_grp': nrm(ks[13], (DEPTH_2, N_GROUPS), 0.01),
        'w_rtr': nrm(ks[14], (DEPTH_2, D_MODEL, N_EXPERTS), D_MODEL ** -0.5),
        'b_rtr': nrm(ks[15], (DEPTH_2, N_EXPERTS), 0.01),
        'w_gate': nrm(ks[16], (DEPTH_2, N_EXPERTS, D_MODEL, D_FF_EXPERT), D_MODEL ** -0.5),
        'w_up': nrm(ks[17], (DEPTH_2, N_EXPERTS, D_MODEL, D_FF_EXPERT), D_MODEL ** -0.5),
        'w_down': nrm(ks[18], (DEPTH_2, N_EXPERTS, D_FF_EXPERT, D_MODEL), D_FF_EXPERT ** -0.5),
        'final_norm': 1.0 + nrm(ks[19], (D_MODEL,), 0.01),
    }

def second_block(x, attn_norm, w_in, w_cmp_k, w_cmp_v, cmp_pos, hg_lb_logits, hg_norm, w_br_nsa, w_br_hg,
              w_out, ffn_norm, w_grp, b_grp, w_rtr, b_rtr, w_gate, w_up, w_down, final_norm):
    b, s, _ = x.shape
    lower_bounds = jnp.cumsum(jax.nn.softmax(hg_lb_logits.astype(jnp.float32), axis=0), axis=0)
    split_points = np.cumsum(IN_SPLITS)[:-1].tolist()
    for layer in range(DEPTH_2):
        h = rmsnorm(x, attn_norm[layer])
        proj = h @ w_in[layer]
        nsa_q, nsa_kv, nsa_gate, hg_q, hg_f, hg_i, hg_g, merge_logits = jnp.split(proj, split_points, axis=-1)
        kv = nsa_kv.reshape(b, s, 6, NSA_KV_GROUPS, NSA_HEAD_DIM)
        o_nsa = nsa_mixer(nsa_q.reshape(b, s, NSA_HEADS, NSA_HEAD_DIM),
                          kv[:, :, 0], kv[:, :, 1], kv[:, :, 2], kv[:, :, 3], kv[:, :, 4], kv[:, :, 5],
                          nsa_gate.reshape(b, s, NSA_HEADS, 3),
                          w_cmp_k[layer], w_cmp_v[layer], cmp_pos[layer])
        lb = lower_bounds[layer].reshape(HG_HEADS, HG_KEY_DIM)
        o_hg = hgrn2_mixer(hg_q, hg_f, hg_i, lb)
        o_hg = rmsnorm(o_hg, hg_norm[layer]) * jax.nn.silu(
            hg_g.astype(jnp.float32).reshape(b, s, HG_HEADS, HG_VAL_DIM))
        o_hg = o_hg.reshape(b, s, HG_WIDTH).astype(x.dtype)
        gate_nsa, gate_hg = jnp.split(jax.nn.sigmoid(merge_logits), 2, axis=-1)
        mixed = (gate_nsa * (o_nsa.astype(x.dtype) @ w_br_nsa[layer]) +
                 gate_hg * (o_hg @ w_br_hg[layer]))
        x = x + mixed @ w_out[layer]
        x = x + hier_moe(rmsnorm(x, ffn_norm[layer]), w_grp[layer], b_grp[layer], w_rtr[layer], b_rtr[layer],
                         w_gate[layer], w_up[layer], w_down[layer])
    return rmsnorm(x, final_norm)


def setup_inputs(seed=0):
    out = dict(first_inputs(seed))
    for name, value in second_inputs(seed + 1).items():
        if name != "x":
            out[name + "_2"] = value
    return out


def reference(
    x, c, rel_bias, ada_w, ada_b, norm1_w, norm2_w, even_w_in, even_w_out, a_q_norm, a_k_norm,
    a_sinks, b_gate_up, b_gate_bias, b_out_norm, odd_w_in, odd_w_out, c_q_norm, c_k_norm,
    moe_w_group, moe_b_group, moe_w_expert, moe_b_expert, moe_w1, moe_w3, moe_w2, attn_norm_2,
    w_in_2, w_cmp_k_2, w_cmp_v_2, cmp_pos_2, hg_lb_logits_2, hg_norm_2, w_br_nsa_2, w_br_hg_2,
    w_out_2, ffn_norm_2, w_grp_2, b_grp_2, w_rtr_2, b_rtr_2, w_gate_2, w_up_2, w_down_2,
    final_norm_2,
):
    x = first_block(
        x, c, rel_bias, ada_w, ada_b, norm1_w, norm2_w, even_w_in, even_w_out, a_q_norm,
        a_k_norm, a_sinks, b_gate_up, b_gate_bias, b_out_norm, odd_w_in, odd_w_out, c_q_norm,
        c_k_norm, moe_w_group, moe_b_group, moe_w_expert, moe_b_expert, moe_w1, moe_w3, moe_w2,
    )
    return second_block(
        x, attn_norm_2, w_in_2, w_cmp_k_2, w_cmp_v_2, cmp_pos_2, hg_lb_logits_2, hg_norm_2,
        w_br_nsa_2, w_br_hg_2, w_out_2, ffn_norm_2, w_grp_2, b_grp_2, w_rtr_2, b_rtr_2,
        w_gate_2, w_up_2, w_down_2, final_norm_2,
    )


_drawn_inputs = setup_inputs


def setup_inputs(seed=0):
    import zlib

    import numpy as np

    out = dict(_drawn_inputs(seed))
    spreads = {}
    factors = {'a_q_norm': 3.801,
     'a_k_norm': 2.677,
     'a_sinks': 3.364,
     'c_q_norm': 8.0,
     'c_k_norm': 5.949,
     'moe_b_group': 4.232,
     'moe_b_expert': 3.59,
     'attn_norm_2': 5.194,
     'cmp_pos_2': 28.352,
     'hg_norm_2': 32.728,
     'ffn_norm_2': 11.629,
     'b_grp_2': 9.439,
     'b_rtr_2': 35.191,
     'final_norm_2': 26.838}
    for name, (base, spread) in spreads.items():
        noise = np.random.default_rng([zlib.crc32(name.encode()), seed]).standard_normal(out[name].shape)
        drawn = base * np.exp(spread * noise) if base else spread * noise
        out[name] = jnp.asarray(drawn.astype(out[name].dtype))
    for name, factor in factors.items():
        out[name] = (out[name] * factor).astype(out[name].dtype)
    return out
```

```python
import math

import concourse.bass as bass
from concourse import mybir

F32 = mybir.dt.float32
I32 = mybir.dt.int32
ALU = mybir.AluOpType
ACT = mybir.ActivationFunctionType
AX = mybir.AxisListType

P = 128
TOK = 256
TILES = TOK // P
D = 1024
DC = D // P
E = 32
FF = 512
GROUPS = 4
PER_GROUP = 8
BLOCK = 64
ROUNDS = TOK // BLOCK
BIG = 1.0e30
EPS = 1e-6
CHUNK = 64
CHUNKS = TOK // CHUNK
REL_BUCKETS = 32
REL_MAX_DIST = 128
A_WINDOW = 128
SKEW = 384
LEVELS = (32, 16, 8, 4, 2, 1)
ROPE_DIM = 16
ROPE_THETA = 500000.0
CMP_LEN, CMP_STRIDE = 32, 16
N_CMP = (TOK - CMP_LEN) // CMP_STRIDE + 1
HEADS = 8


class Stage:

    def __init__(self, nc, name):
        self.nc, self.name, self.sems = nc, name, []

    def sem(self, name):
        self.sems.append(self.nc.alloc_semaphore(name=f"{self.name}_{name}"))
        return self.sems[-1]

    def close(self):
        self.nc.clear_and_free_semaphores(self.sems)
        self.nc.all_engine_barrier()


class Chain:

    def __init__(self, eng, sem):
        self.eng, self.sem, self.n = eng, sem, 0

    def __call__(self, ins):
        self.n += 1
        ins.then_inc(self.sem, 1)
        self.eng.wait_ge(self.sem, self.n)


def moe_stage(nc, tag, x, h, hT, gate2, w_grp, b_grp, w_rtr, b_rtr, w1, w3, w2, consts, mem, ps):
    stage = Stage(nc, tag)
    sem = stage.sem
    rt, rb = mem["rt"], mem["rb"]
    ident, tri, ones, iota2, order = (consts[k] for k in ("ident", "tri", "ones", "iota2", "order"))
    small = mem["small"]
    slots, comb, nsteps = mem["slots"], mem["comb"], mem["nsteps"]
    sel, selw, selT, xg, hm, hTs, y = (mem[k] for k in ("sel", "selw", "selT", "xg", "hm", "hTs", "y"))
    w1b, w3b, w2b, sil = mem["w1b"], mem["w3b"], mem["w2b"], mem["sil"]
    bank_acc, bank_H, bank_T, bank_G, bank_Y = ps[0:4], ps[4], ps[5], ps[6], ps[7]

    rt_landed, w1_landed, w3_landed, w2_landed = sem("rt"), [sem("w1_0"), sem("w1_1")], [sem("w3_0"), sem("w3_1")], [sem("w2_0"), sem("w2_1")]
    logits_done, mask_ready, pos_done, steps_ready = sem("logits"), sem("mask"), sem("pos"), sem("steps")
    exp_done, exp_asked, acc_zeroed = sem("exp_done"), sem("exp_asked"), sem("acc_zeroed")
    sel_built, gathered, xg_copied, selT_copied = sem("sel_built"), sem("gathered"), sem("xg_copied"), sem("selT_copied")
    up_done, silu_done, hm_ready, turned, hT_copied = sem("up"), sem("silu"), sem("hm"), sem("turned"), sem("hT_copied")
    down_done, y_copied, scattered, dve_step = sem("down"), sem("y_copied"), sem("scattered"), sem("dve_step")

    H1, H3 = bank_H[:, 0:256], bank_H[:, 256:512]
    HT = bank_T[:, 0:256].rearrange("p (c n) -> p c n", c=2)
    ST = bank_T[:, 256:512].rearrange("p (t n) -> p t n", t=2)
    XG = bank_G[:, :].rearrange("p (c n) -> p c n", c=DC)

    def steps(eng):
        return eng.value_load(nsteps[0:1, 0:1], min_val=1, max_val=ROUNDS)

    with nc.Block() as block:
        @block.sync
        def _(sp):
            sp.dma_start(rt[:, :, 0:GROUPS], w_grp.rearrange("(c p) n -> p c n", p=P)).then_inc(rt_landed, 16)
            sp.dma_start(rt[:, :, GROUPS:], w_rtr.rearrange("(c p) n -> p c n", p=P)).then_inc(rt_landed, 16)
            sp.dma_start(rb[:, 0:GROUPS], b_grp.partition_broadcast(P)).then_inc(rt_landed, 16)
            sp.dma_start(rb[:, GROUPS:], b_rtr.partition_broadcast(P)).then_inc(rt_landed, 16)

            def load(u, pair):
                for buf, w, landed in ((w1b, w1, w1_landed), (w3b, w3, w3_landed), (w2b, w2, w2_landed)):
                    sp.dma_start(buf[:, u], w.rearrange("(j two) (c p) n -> two j p c n", two=2, p=P)[u, pair]).then_inc(landed[u], 16)

            load(0, 0)
            load(1, 0)
            sp.wait_ge(steps_ready, 1)
            rounds = steps(sp)
            with sp.Fori(0, rounds) as r:
                with sp.Fori(1, E // 2) as pair:
                    for u in range(2):
                        sp.wait_ge(down_done, r * E + pair * 2 + (u - 1))
                        load(u, pair)
                with sp.If(rounds > r + 1):
                    for u in range(2):
                        sp.wait_ge(down_done, r * E + E - 1 + u)
                        load(u, 0)

        @block.tensor
        def _(pe):
            pe.wait_ge(rt_landed, 64)
            for t in range(TILES):
                for c in range(DC):
                    m = nc.tensor.matmul(bank_H[:, t * 64:t * 64 + 36], hT[:, c, t * P:(t + 1) * P], rt[:, c, :],
                                         start=(c == 0), stop=(c == DC - 1))
            m.then_inc(logits_done, 1)
            for b in range(4):
                m = nc.tensor.matmul(bank_acc[b][:, :], consts["zeros"][:, 0:P], consts["zeros"][:, :], start=True, stop=True)
            pe.wait_ge(mask_ready, 1)
            M = mem["mask"]
            nc.tensor.matmul(bank_T[:, 0:E], tri[:, :], M[:, 0, :], start=True, stop=True)
            nc.tensor.matmul(bank_T[:, E:2 * E], ones[:, :], M[:, 0, :], start=True, stop=False)
            nc.tensor.matmul(bank_T[:, E:2 * E], tri[:, :], M[:, 1, :], start=False, stop=True)
            nc.tensor.matmul(bank_T[:, 2 * E:3 * E], ones[:, :], M[:, 0, :], start=True, stop=False)
            nc.tensor.matmul(bank_T[:, 2 * E:3 * E], ones[:, :], M[:, 1, :], start=False, stop=True).then_inc(pos_done, 1)
            pe.wait_ge(steps_ready, 1)

            def gather(u):
                for c in range(DC):
                    for t in range(TILES):
                        nc.tensor.matmul(XG[:, c, :], h[:, t, c * P:(c + 1) * P], sel[:, u, t, :],
                                         start=(t == 0), stop=(t == 1))

            def turn_sel(u):
                for t in range(TILES):
                    m = nc.tensor.transpose(ST[:, t, :], selw[:, u, t, :], ident[:, :])
                m.then_inc(gathered, 1)

            def scatter(u):
                for t in range(TILES):
                    for half in range(2):
                        m = nc.tensor.matmul(bank_acc[2 * t + half][:, :],
                                             selT[64 * half:64 * half + 64, u, t * P:(t + 1) * P],
                                             y[64 * half:64 * half + 64, u, :], start=False, stop=False,
                                             skip_group_check=True)
                return m

            pe.wait_ge(sel_built, 1)
            gather(0)
            turn_sel(0)
            rounds = steps(pe)
            with pe.Fori(0, rounds) as r:
                with pe.Fori(0, E, 2) as e:
                    for u in range(2):
                        g = r * E + e + u
                        pe.wait_ge(xg_copied, g + 1)
                        for w, out, landed in ((w1b, H1, w1_landed), (w3b, H3, w3_landed)):
                            pe.wait_ge(landed[u], (r * E + e) * 8 + 16)
                            for c in range(DC):
                                for half in range(2):
                                    m = nc.tensor.matmul(out[64 * half:64 * half + 64, :], xg[:, u, c, :],
                                                         w[:, u, c, half * 256:half * 256 + 256],
                                                         start=(c == 0), stop=(c == DC - 1), skip_group_check=True)
                        m.then_inc(up_done, 1)
                        pe.wait_ge(y_copied, g + 1)
                        scatter(1 - u).then_inc(scattered, 1)
                        pe.wait_ge(hm_ready, g + 1)
                        pe.wait_ge(selT_copied, g + 1)
                        for c in range(2):
                            m = nc.tensor.transpose(HT[:, c, :], hm[:, c * P:(c + 1) * P], ident[:, :])
                        m.then_inc(turned, 1)
                        pe.wait_ge(sel_built, g + 2)
                        gather(1 - u)
                        pe.wait_ge(hT_copied, g + 1)
                        turn_sel(1 - u)
                        pe.wait_ge(w2_landed[u], (r * E + e) * 8 + 16)
                        for k in range(4):
                            for half in range(2):
                                m = nc.tensor.matmul(bank_Y[64 * half:64 * half + 64, :],
                                                     hTs[:, k % 2, (k // 2) * 64:(k // 2) * 64 + 64],
                                                     w2b[:, u, k, half * 512:half * 512 + 512],
                                                     start=(k == 0), stop=(k == 3), skip_group_check=True)
                        m.then_inc(down_done, 1)
            pe.wait_ge(y_copied, rounds * E + 1)
            scatter(1).then_inc(scattered, 1)

        @block.scalar
        def _(act):
            act.wait_ge(exp_asked, 1)
            nc.scalar.activation(small[:, 4, 0:2 * GROUPS], small[:, 3, 0:2 * GROUPS], ACT.Exp).then_inc(exp_done, 1)
            act.wait_ge(exp_asked, 2)
            nc.scalar.activation(small[:, 7, 2:4], small[:, 7, 0:2], ACT.Exp).then_inc(exp_done, 1)
            act.wait_ge(steps_ready, 1)
            act.wait_ge(gathered, 1)
            nc.scalar.copy(xg[:, 0], XG).then_inc(xg_copied, 1)
            rounds = steps(act)
            with act.Fori(0, rounds) as r:
                with act.Fori(0, E, 2) as e:
                    for u in range(2):
                        g = r * E + e + u
                        act.wait_ge(up_done, g + 1)
                        nc.scalar.activation(sil[:, :], H1, ACT.Silu).then_inc(silu_done, 1)
                        act.wait_ge(gathered, g + 2)
                        nc.scalar.copy(xg[:, 1 - u], XG).then_inc(xg_copied, 1)
                        act.wait_ge(down_done, g + 1)
                        nc.scalar.copy(y[:, u, :], bank_Y[:, :]).then_inc(y_copied, 1)

        @block.vector
        def _(dve):
            link = Chain(dve, dve_step)
            lg = mem["lg"]
            dve.wait_ge(logits_done, 1)
            dve.wait_ge(rt_landed, 64)
            for t in range(TILES):
                link(nc.vector.tensor_tensor(lg[:, t, :], bank_H[:, t * 64:t * 64 + 36], rb[:, :], ALU.add))

            def bc(ap, n):
                return ap.unsqueeze(2).to_broadcast([P, TILES, n])

            def v(k, n):
                return small[:, k, 0:TILES * n].rearrange("p (t n) -> p t n", t=TILES)

            def first_max(vals, n, best, onehot, key):
                link(nc.vector.tensor_reduce(best, vals, AX.X, ALU.max))
                link(nc.vector.tensor_tensor(onehot, vals, bc(best, n), ALU.is_equal))
                link(nc.vector.tensor_tensor(onehot, onehot, order[:, 0:n].unsqueeze(1).to_broadcast([P, TILES, n]), ALU.mult))
                link(nc.vector.tensor_reduce(key, onehot, AX.X, ALU.max))
                link(nc.vector.tensor_tensor(onehot, onehot, bc(key, n), ALU.is_equal))

            gl, el = lg[:, :, 0:GROUPS], lg[:, :, GROUPS:]
            gmax, key, m1, m2, pg, w_a, w_b = (small[:, 5, 2 * i:2 * i + 2] for i in range(7))
            ohg, oh1, oh2 = v(0, GROUPS), v(1, E), v(2, E)
            first_max(gl, GROUPS, gmax, ohg, key)
            link(nc.vector.tensor_tensor(v(3, GROUPS), gl, bc(gmax, GROUPS), ALU.subtract))
            dve.sem_inc(exp_asked, 1)
            pen = v(6, E)
            link(nc.vector.tensor_copy(pen.rearrange("p t (g n) -> p t g n", g=GROUPS),
                                       ohg.unsqueeze(3).to_broadcast([P, TILES, GROUPS, PER_GROUP])))
            link(nc.vector.tensor_scalar(pen, pen, 1.0, BIG, ALU.subtract, ALU.mult))
            link(nc.vector.tensor_tensor(el, el, pen, ALU.add))
            first_max(el, E, m1, oh1, key)
            link(nc.vector.scalar_tensor_tensor(el, oh1, -2.0 * BIG, el, ALU.mult, ALU.add))
            first_max(el, E, m2, oh2, key)
            mask = mem["mask"]
            link(nc.vector.tensor_tensor(mask[:, :, :], oh1, oh2, ALU.add))
            dve.sem_inc(mask_ready, 1)
            link(nc.vector.tensor_tensor(small[:, 7, 0:2], m2, m1, ALU.subtract))
            dve.sem_inc(exp_asked, 1)
            dve.wait_ge(exp_done, 1)
            link(nc.vector.tensor_reduce(pg, v(4, GROUPS), AX.X, ALU.add))
            dve.wait_ge(exp_done, 2)
            ex = small[:, 7, 2:4]
            link(nc.vector.tensor_scalar(w_a, ex, 1.0, None, ALU.add))
            link(nc.vector.tensor_tensor(w_a, w_a, pg, ALU.mult))
            link(nc.vector.reciprocal(w_b, w_a))
            link(nc.vector.tensor_tensor(w_a, w_b, ex, ALU.mult))
            link(nc.vector.tensor_tensor(oh1, oh1, bc(w_b, E), ALU.mult))
            link(nc.vector.tensor_tensor(oh2, oh2, bc(w_a, E), ALU.mult))
            for k in range(ROUNDS):
                link(nc.vector.tensor_tensor(comb[:, :, k * E:(k + 1) * E], oh1, oh2, ALU.add))
            link(nc.vector.memset(slots[:, :, ROUNDS * E:], -1000.0))
            link(nc.vector.memset(comb[:, :, ROUNDS * E:], 0.0))
            link(nc.vector.memset(selT[:, 1, :], 0.0))
            link(nc.vector.memset(y[:, 1, :], 0.0))
            dve.wait_ge(pos_done, 1)
            base = v(6, E)
            link(nc.vector.scalar_tensor_tensor(base, bank_T[:, 0:2 * E].rearrange("p (t n) -> p t n", t=2), 1000.0,
                                                mask[:, :, :], ALU.add, ALU.mult))
            for k in range(ROUNDS):
                link(nc.vector.tensor_scalar(slots[:, :, k * E:(k + 1) * E], base, 1000.0 + BLOCK * k, None, ALU.subtract))
            full = small[:, 5, 14:15]
            link(nc.vector.tensor_reduce(full, bank_T[:, 2 * E:3 * E], AX.X, ALU.max))
            rnd = small[:, 5, 15:16]
            link(nc.vector.tensor_scalar(rnd, full, float(BLOCK), 1.0, ALU.is_gt, ALU.add))
            for k in range(2, ROUNDS):
                link(nc.vector.tensor_scalar(small[:, 5, 16:17], full, float(BLOCK * k), None, ALU.is_gt))
                link(nc.vector.tensor_tensor(rnd, rnd, small[:, 5, 16:17], ALU.add))
            link(nc.vector.tensor_copy(nsteps[:, :], rnd))
            dve.sem_inc(steps_ready, 1)

            def build_sel(u, g):
                for t in range(TILES):
                    nc.vector.tensor_scalar(sel[:, u, t, :], iota2[:, 0:BLOCK], slots[:, t, bass.ds(g, 1)], None, ALU.is_equal)
                    m = nc.vector.tensor_scalar(selw[:, u, t, :], iota2[:, :], slots[:, t, bass.ds(g, 1)],
                                                comb[:, t, bass.ds(g, 1)], ALU.is_equal, ALU.mult)
                m.then_inc(sel_built, 1)

            build_sel(0, 0)
            build_sel(1, 1)
            dve.wait_ge(gathered, 1)
            nc.vector.tensor_copy(selT[:, 0, :], bank_T[:, 256:512]).then_inc(selT_copied, 1)
            dve.sem_inc(y_copied, 1)
            rounds = steps(dve)
            with dve.Fori(0, rounds) as r:
                with dve.Fori(0, E, 2) as e:
                    for u in range(2):
                        g = r * E + e + u
                        dve.wait_ge(silu_done, g + 1)
                        nc.vector.tensor_tensor(hm[:, :], sil[:, :], H3, ALU.mult).then_inc(hm_ready, 1)
                        dve.wait_ge(turned, g + 1)
                        nc.vector.tensor_copy(hTs[:, :, :], HT).then_inc(hT_copied, 1)
                        dve.wait_ge(gathered, g + 2)
                        nc.vector.tensor_copy(selT[:, 1 - u, :], bank_T[:, 256:512]).then_inc(selT_copied, 1)
                        build_sel(u, g + 2)
            dve.wait_ge(scattered, rounds * E + 1)
            for t in range(TILES):
                for half in range(2):
                    cols = slice(half * 512, half * 512 + 512)
                    link(nc.vector.tensor_tensor(h[:, t, cols], bank_acc[2 * t + half][:, :], gate2[:, cols], ALU.mult)
                         if gate2 is not None else nc.vector.tensor_copy(h[:, t, cols], bank_acc[2 * t + half][:, :]))
                    link(nc.vector.tensor_tensor(x[:, t, cols], x[:, t, cols], h[:, t, cols], ALU.add))
    stage.close()


def bucket_of(dist):
    import numpy as np
    exact = REL_BUCKETS // 2
    d = np.maximum(dist, 0)
    logd = np.log(np.maximum(d, 1).astype(np.float32) / np.float32(exact)) / np.float32(math.log(REL_MAX_DIST / exact))
    far = np.minimum(exact + (logd.astype(np.float32) * np.float32(REL_BUCKETS - exact)).astype(np.int32), REL_BUCKETS - 1)
    return np.where(d < exact, d, far)


def host_constants():
    import numpy as np
    f = np.float32
    c = {}
    c["ident"] = np.eye(P, dtype=f)
    c["tri"] = np.triu(np.ones((P, P), f), 1)
    c["ones"] = np.ones((P, P), f)
    c["iota2"] = np.tile(np.arange(BLOCK, dtype=f), (P, 2))
    c["order"] = np.tile(np.arange(E, 0, -1, dtype=f), (P, 1))
    c["zeros"] = np.zeros((P, 512), f)
    i = np.arange(P)
    same = (i[:, None] // CHUNK) == (i[None, :] // CHUNK)
    c["upto"] = ((i[:, None] <= i[None, :]) & same).astype(f)
    c["after"] = ((i[:, None] > i[None, :]) & same).astype(f)
    dist = 255 - np.arange(SKEW)
    hot = (bucket_of(dist)[None, :] == np.arange(REL_BUCKETS)[:, None])
    for name, ok in (("hot_window", (dist >= 0) & (dist < A_WINDOW)), ("hot_causal", dist >= 0)):
        c[name] = np.concatenate([hot & ok, ~ok[None]], 0).astype(f)
    j = np.arange(TOK)
    c["causal"] = np.where(P + i[:, None] - j[None, :] >= 0, 0.0, -BIG).astype(f)
    c["levels"] = np.stack([((i[:, None] // (2 * m)) == (i[None, :] // (2 * m))) & (i[:, None] % (2 * m) < m)
                            & (i[None, :] % (2 * m) >= m) for m in LEVELS] + [i[:, None] == i[None, :]], 1
                           ).astype(f).reshape(P, -1)
    half = ROPE_DIM // 2
    inv = (f(ROPE_THETA) ** (-np.arange(half, dtype=f) / f(half))).astype(f)
    ang = np.arange(TOK, dtype=f)[:, None] * inv[None, :]
    rope = np.concatenate([np.cos(ang), np.sin(ang)], 1).astype(f)
    c["rope"] = rope.reshape(TILES, P, ROPE_DIM).transpose(1, 0, 2).reshape(P, -1)
    c["rope_cmp"] = np.zeros((P, ROPE_DIM), f)
    c["rope_cmp"][:N_CMP] = rope[np.arange(N_CMP) * CMP_STRIDE]
    ok = (np.arange(N_CMP) * CMP_STRIDE + CMP_LEN - 1)[None, :] <= j[:, None]
    ok = ok.reshape(TILES, P, N_CMP).transpose(1, 0, 2)
    c["cmp_bias"] = np.where(ok, 0.0, -BIG).astype(f).reshape(P, -1)
    c["cmp_mask"] = ok.astype(f).reshape(P, -1)
    return c


def alloc_consts(nc):
    return {n: nc.alloc_sbuf_tensor(f"const_{n}", list(a.shape), F32) for n, a in host_constants().items()}


class Arena:

    def __init__(self, nc, words):
        self.t, self.words, self.at = nc.alloc_sbuf_tensor("arena", [P, words], F32), words, 0

    def take(self, shape, parts=P):
        n = math.prod(shape)
        assert self.at + n <= self.words, (self.at, n, self.words)
        ap = self.t[0:parts, self.at:self.at + n]
        self.at += n
        names = "abcd"[:len(shape)]
        if len(shape) > 1:
            ap = ap.rearrange(f"p ({' '.join(names)}) -> p {' '.join(names)}", **dict(zip(names, shape)))
        return ap


def col(w):
    return w.rearrange("(p c) -> p c", p=P)


def modulation_stage(nc, tag, c_vec, ada_w, ada_b, mod, consts, arena, banks):
    stage = Stage(nc, tag)
    sem = stage.sem
    mark = arena.at
    ccol, crep = arena.take([DC]), arena.take([DC, P])
    wt = arena.take([2, DC, 512])
    brow = arena.take([2, 512], parts=1)
    N = ada_w.shape[1] // 512
    c_landed, w_landed, silu_done, spread = sem("c"), [sem("w0"), sem("w1")], sem("silu"), sem("spread")
    row_done, copied = sem("row"), sem("copied")
    wv = ada_w.rearrange("(p c) (i u n) -> i u p c n", p=P, n=512, u=2)
    bv = ada_b.rearrange("(i u n) -> i u n", n=512, u=2)
    with nc.Block() as block:
        @block.sync
        def _(sp):
            sp.dma_start(ccol, col(c_vec)).then_inc(c_landed, 16)

            def load(i, u):
                sp.dma_start(wt[:, u], wv[i, u]).then_inc(w_landed[u], 16)
                sp.dma_start(brow[:, u], bv[i, u].unsqueeze(0)).then_inc(w_landed[u], 16)
            for u in range(2):
                load(0, u)
            with sp.Fori(1, N // 2) as i:
                for u in range(2):
                    sp.wait_ge(row_done, i * 2 + (u - 1))
                    load(i, u)

        @block.scalar
        def _(act):
            act.wait_ge(c_landed, 16)
            nc.scalar.activation(ccol, ccol, ACT.Silu).then_inc(silu_done, 1)

        @block.tensor
        def _(pe):
            pe.wait_ge(spread, 1)
            with pe.Fori(0, N // 2) as i:
                for u in range(2):
                    pe.wait_ge(w_landed[u], i * 32 + 32)
                    pe.wait_ge(copied, i * 2 + (u + 1))
                    for k in range(DC):
                        nc.tensor.matmul(banks[u][:, :], crep[:, k, :], wt[:, u, k, :], start=(k == 0), stop=False)
                    nc.tensor.matmul(banks[u][:, :], consts["ones"][0:1, :], brow[:, u, :], start=False,
                                     stop=True).then_inc(row_done, 1)

        @block.vector
        def _(dve):
            dve.wait_ge(silu_done, 1)
            dve.sem_inc(copied, 2)
            nc.vector.tensor_copy(crep, ccol.unsqueeze(2).to_broadcast([P, DC, P])).then_inc(spread, 1)
            with dve.Fori(0, N // 2) as i:
                for u in range(2):
                    dve.wait_ge(row_done, i * 2 + (u + 1))
                    nc.vector.tensor_copy(mod.rearrange("p (i u n) -> p u i n", u=2, n=512)[:, u, bass.ds(i, 1), :],
                                          banks[u][:, :].unsqueeze(1)).then_inc(copied, 1)
    stage.close()
    arena.at = mark


def norm_stage(nc, tag, x, out, w_row, scale, shift, arena):
    stage = Stage(nc, tag)
    sem = stage.sem
    mark = arena.at
    w, sq, ss, rs = arena.take([D]), arena.take([TILES, D]), arena.take([TILES]), arena.take([TILES])
    landed, squared, root_asked, root_done, step, astep = sem("w"), sem("sq"), sem("ask"), sem("root"), sem("dve"), sem("act")
    with nc.Block() as block:
        @block.sync
        def _(sp):
            sp.dma_start(w, w_row.partition_broadcast(P)).then_inc(landed, 16)

        @block.scalar
        def _(act):
            for t in range(TILES):
                nc.scalar.activation(sq[:, t], x[:, t, :], ACT.Square, accum_out=ss[:, t:t + 1]).then_inc(squared, 1)
            act.wait_ge(root_asked, 1)
            nc.scalar.activation(rs, ss, ACT.Sqrt).then_inc(root_done, 1)

        @block.vector
        def _(dve):
            link = Chain(dve, step)
            dve.wait_ge(landed, 16)
            if scale is not None:
                link(nc.vector.scalar_tensor_tensor(w, scale, 1.0, w, ALU.add, ALU.mult))
            dve.wait_ge(squared, TILES)
            link(nc.vector.tensor_scalar(ss, ss, 1.0 / D, EPS, ALU.mult, ALU.add))
            dve.sem_inc(root_asked, 1)
            dve.wait_ge(root_done, 1)
            link(nc.vector.reciprocal(rs, rs))
            for t in range(TILES):
                link(nc.vector.scalar_tensor_tensor(out[:, t, :], x[:, t, :], rs[:, t:t + 1], w, ALU.mult, ALU.mult))
                if shift is not None:
                    link(nc.vector.tensor_tensor(out[:, t, :], out[:, t, :], shift, ALU.add))
    stage.close()
    arena.at = mark


def turn_stage(nc, tag, jobs, ident, banks):
    stage = Stage(nc, tag)
    sem = stage.sem
    pairs = [(src, w, i, min(2, n - i), dst) for src, w, n, dst in jobs for i in range(0, n, 2)]
    turned, copied = sem("turned"), [sem("copied_dve"), sem("copied_act")]
    with nc.Block() as block:
        @block.tensor
        def _(pe):
            for j, (src, w, i, m, dst) in enumerate(pairs):
                if j >= 8:
                    pe.wait_ge(copied[j % 2], (j - 8) // 2 + 1)
                for k in range(m):
                    for t in range(TILES):
                        last = nc.tensor.transpose(banks[j % 8][0:w, k * TOK + t * P:k * TOK + (t + 1) * P],
                                                   src[:, t, (i + k) * w:(i + k + 1) * w], ident[:, :])
                last.then_inc(turned, 1)

        def out(j):
            src, w, i, m, dst = pairs[j]
            return dst[:, i:i + m, :], banks[j % 8][0:w, 0:m * TOK].rearrange("p (m n) -> p m n", m=m)

        @block.vector
        def _(dve):
            for j in range(0, len(pairs), 2):
                dve.wait_ge(turned, j + 1)
                nc.vector.tensor_copy(*out(j)).then_inc(copied[0], 1)

        @block.scalar
        def _(act):
            for j in range(1, len(pairs), 2):
                act.wait_ge(turned, j + 1)
                nc.scalar.copy(*out(j)).then_inc(copied[1], 1)
    stage.close()


def project_stage(nc, tag, inT, kc, w, width, out, arena, banks, gate=None, add=False):
    stage = Stage(nc, tag)
    sem = stage.sem
    mark = arena.at
    wt = arena.take([2, kc, width])
    tmp = arena.take([2, width])
    N = w.shape[1] // width
    landed, row_done, copied, step = [sem("w0"), sem("w1")], sem("row"), [sem("copied0"), sem("copied1")], sem("dve")
    plain = gate is None and not add
    wv = w.rearrange("(c p) (i n) -> i p c n", p=P, n=width)

    def both(eng, first, body):
        if N // 2 > first:
            with eng.Fori(first, N // 2) as i:
                for u in range(2):
                    body(i * 2 + u, i, u)
        if N % 2 and N // 2 >= first:
            body(N - 1, N // 2, 0)

    with nc.Block() as block:
        @block.sync
        def _(sp):
            def load(b, i, u):
                src = w[:, bass.ds(b * width, width)] if not isinstance(b, int) else w[:, b * width:(b + 1) * width]
                sp.dma_start(wt[:, u], src.rearrange("(c p) n -> p c n", p=P)).then_inc(landed[u], 16)

            def later(b, i, u):
                sp.wait_ge(row_done, i * 2 + (u - 1))
                load(b, i, u)
            for u in range(min(2, N)):
                load(u, 0, u)
            both(sp, 1, later)

        @block.tensor
        def _(pe):
            def body(b, i, u):
                pe.wait_ge(landed[u], i * 16 + 16)
                for t in range(TILES):
                    pe.wait_ge(copied[t], i * 2 + (u + 1))
                    for k in range(kc):
                        m = nc.tensor.matmul(banks[2 * u + t][:, 0:width], inT[:, k, t * P:(t + 1) * P], wt[:, u, k, :],
                                             start=(k == 0), stop=(k == kc - 1))
                m.then_inc(row_done, 1)
            both(pe, 0, body)

        def at(ap, t, b):
            return ap[:, t, bass.ds(b * width, width)] if not isinstance(b, int) else ap[:, t, b * width:(b + 1) * width]

        @block.scalar
        def _(act):
            if plain:
                act.sem_inc(copied[1], 2)

                def body(b, i, u):
                    act.wait_ge(row_done, i * 2 + (u + 1))
                    nc.scalar.copy(at(out, 1, b), banks[2 * u + 1][:, 0:width]).then_inc(copied[1], 1)
                both(act, 0, body)

        @block.vector
        def _(dve):
            dve.sem_inc(copied[0], 2)
            if plain:
                def body(b, i, u):
                    dve.wait_ge(row_done, i * 2 + (u + 1))
                    nc.vector.tensor_copy(at(out, 0, b), banks[2 * u][:, 0:width]).then_inc(copied[0], 1)
            else:
                dve.sem_inc(copied[1], 2)

                def body(b, i, u):
                    dve.wait_ge(row_done, i * 2 + (u + 1))
                    for t in range(TILES):
                        o, src = at(out, t, b), banks[2 * u + t][:, 0:width]
                        if gate is not None and not add:
                            nc.vector.tensor_tensor(o, src, at(gate, t, b), ALU.mult).then_inc(copied[t], 1)
                        elif gate is None:
                            nc.vector.tensor_tensor(o, src, o, ALU.add).then_inc(copied[t], 1)
                        else:
                            nc.vector.tensor_tensor(tmp[:, t], src, at(gate, t, b), ALU.mult).then_inc(step, 1)
                            dve.wait_ge(step, i * 4 + (u * 2 + t + 1))
                            nc.vector.tensor_tensor(o, tmp[:, t], o, ALU.add).then_inc(copied[t], 1)
            both(dve, 0, body)
    stage.close()
    arena.at = mark


def head_norm_stage(nc, tag, jobs, arena):
    stage = Stage(nc, tag)
    sem = stage.sem
    mark = arena.at
    most = max(n * w for _, n, w, _ in jobs)
    total = sum(n for _, n, _, _ in jobs) * TILES
    sq, ss, rs = arena.take([TILES, most]), arena.take([total]), arena.take([total])
    ws = [arena.take([w]) for _, _, w, _ in jobs]
    landed, root_asked, root_done, step = sem("w"), sem("ask"), sem("root"), sem("dve")
    with nc.Block() as block:
        @block.sync
        def _(sp):
            for (_, _, _, w_row), w in zip(jobs, ws):
                sp.dma_start(w, w_row.partition_broadcast(P)).then_inc(landed, 16)

        @block.scalar
        def _(act):
            act.wait_ge(root_asked, 1)
            nc.scalar.activation(rs, ss, ACT.Sqrt).then_inc(root_done, 1)

        @block.vector
        def _(dve):
            link = Chain(dve, step)
            at, places = 0, []
            for rows, n, w, _ in jobs:
                for t in range(TILES):
                    r = rows[:, t, :]
                    link(nc.vector.tensor_tensor(sq[:, t, 0:n * w], r, r, ALU.mult))
                    link(nc.vector.tensor_reduce(ss[:, at:at + n], sq[:, t, 0:n * w].rearrange("p (n w) -> p n w", w=w),
                                                 AX.X, ALU.add))
                    link(nc.vector.tensor_scalar(ss[:, at:at + n], ss[:, at:at + n], 1.0 / w, EPS, ALU.mult, ALU.add))
                    places.append(at)
                    at += n
            dve.sem_inc(root_asked, 1)
            dve.wait_ge(root_done, 1)
            link(nc.vector.reciprocal(rs, rs))
            dve.wait_ge(landed, 16 * len(jobs))
            for k, (rows, n, w, _) in enumerate(jobs):
                for t in range(TILES):
                    r = rows[:, t, :].rearrange("p (n w) -> p n w", w=w)
                    a = places[k * TILES + t]
                    link(nc.vector.tensor_tensor(r, r, rs[:, a:a + n].unsqueeze(2).to_broadcast([P, n, w]), ALU.mult))
                    link(nc.vector.tensor_tensor(r, r, ws[k].unsqueeze(1).to_broadcast([P, n, w]), ALU.mult))
    stage.close()
    arena.at = mark


def bias_stage(nc, tag, rel_bias, hot, out, scratch, arena, banks):
    stage = Stage(nc, tag)
    sem = stage.sem
    mark = arena.at
    rb, rep, rows = arena.take([HEADS], parts=REL_BUCKETS + 1), arena.take([HEADS, P], parts=REL_BUCKETS + 1), arena.take([HEADS, SKEW])
    masked, landed, spread, made, copied, stored, back, step = (sem(n) for n in ("masked", "rb", "spread", "made", "copied", "stored", "back", "dve"))
    with nc.Block() as block:
        @block.gpsimd
        def _(pool):
            nc.gpsimd.memset(rb[REL_BUCKETS:REL_BUCKETS + 1, :], -BIG).then_inc(masked, 1)

        @block.sync
        def _(sp):
            sp.dma_start(rb[0:REL_BUCKETS, :], rel_bias).then_inc(landed, 16)
            sp.wait_ge(copied, 1)
            sp.dma_start(scratch.rearrange("h p s -> p h s"), rows).then_inc(stored, 16)
            sp.wait_ge(stored, 16)
            skewed = bass.AP(scratch.tensor, P - 1, [[SKEW - 1, P], [P * SKEW, HEADS], [1, TOK]])
            sp.dma_start(out, skewed).then_inc(back, 16)
            sp.wait_ge(back, 16)

        @block.tensor
        def _(pe):
            pe.wait_ge(spread, 1)
            for h in range(HEADS):
                m = nc.tensor.matmul(banks[h][:, 0:SKEW], rep[:, h, :], hot[:, :], start=True, stop=True)
            m.then_inc(made, 1)

        @block.vector
        def _(dve):
            link = Chain(dve, step)
            dve.wait_ge(landed, 16)
            dve.wait_ge(masked, 1)
            nc.vector.tensor_copy(rep, rb.unsqueeze(2).to_broadcast([REL_BUCKETS + 1, HEADS, P])).then_inc(spread, 1)
            dve.wait_ge(made, 1)
            for h in range(HEADS):
                link(nc.vector.tensor_copy(rows[:, h, :], banks[h][:, 0:SKEW]))
            dve.sem_inc(copied, 1)
    stage.close()
    arena.at = mark


def attend_stage(nc, tag, qT, kT, v, hd, kv_of, scale, bias, out, ident, arena, psum, sinks=None, factor=None,
                 add=False, keys=None, mask=None):
    stage = Stage(nc, tag)
    sem = stage.sem
    mark = arena.at
    nk_of = [keys or (t + 1) * P for t in range(TILES)]
    L, PT = arena.take([HEADS, max(nk_of)]), arena.take([2 * HEADS, P])
    mx, sm, es = arena.take([HEADS]), arena.take([HEADS]), arena.take([HEADS])
    tmp = arena.take([HEADS * hd])
    sem_names = ("scores", "shifted", "exp", "probs", "turned", "pt_dve", "pt_act", "outs", "written", "dve", "act", "sink")
    scores, shifted, exp_done, probs, turned, pt_dve, pt_act, outs, written, step, astep, sink_done = (sem(n) for n in sem_names)
    S = psum[:, 0:2048].rearrange("p (h n) -> p h n", h=HEADS)
    T = psum[:, 2048:4096].rearrange("p (u n) -> p u n", n=P)
    O = psum[:, 0:HEADS * hd]
    with nc.Block() as block:
        @block.tensor
        def _(pe):
            for t, nk in enumerate(nk_of):
                nkt = -(-nk // P)
                if t:
                    pe.wait_ge(written, t)
                for h in range(HEADS):
                    m = nc.tensor.matmul(S[:, h, 0:nk], qT[:, h, t * P:(t + 1) * P], kT[:, kv_of(h), 0:nk], start=True, stop=True)
                m.then_inc(scores, 1)
                pe.wait_ge(probs, t + 1)
                for h in range(HEADS):
                    for kt in range(nkt):
                        w = min(P, nk - kt * P)
                        m = nc.tensor.transpose(T[0:w, h * nkt + kt, :], L[:, h, kt * P:kt * P + w], ident[:, :])
                m.then_inc(turned, 1)
                pe.wait_ge(pt_dve, t + 1)
                pe.wait_ge(pt_act, t + 1)
                for h in range(HEADS):
                    for kt in range(nkt):
                        w = min(P, nk - kt * P)
                        m = nc.tensor.matmul(O[:, h * hd:(h + 1) * hd], PT[0:w, h * nkt + kt, :], v(kt, kv_of(h)),
                                             start=(kt == 0), stop=(kt == nkt - 1))
                m.then_inc(outs, 1)

        @block.scalar
        def _(act):
            for t, nk in enumerate(nk_of):
                n, w = HEADS * -(-nk // P), min(P, nk)
                act.wait_ge(shifted, t + 1)
                nc.scalar.activation(L[:, :, 0:nk], L[:, :, 0:nk], ACT.Exp).then_inc(exp_done, 1)
                if sinks is not None:
                    nc.scalar.activation(es, es, ACT.Exp).then_inc(sink_done, 1)
                act.wait_ge(turned, t + 1)
                nc.scalar.copy(PT[0:w, n // 2:n, :], T[0:w, n // 2:n, :]).then_inc(pt_act, 1)

        @block.vector
        def _(dve):
            link = Chain(dve, step)
            for t, nk in enumerate(nk_of):
                n, w = HEADS * -(-nk // P), min(P, nk)
                Lt = L[:, :, 0:nk]
                dve.wait_ge(scores, t + 1)
                link(nc.vector.scalar_tensor_tensor(Lt, S[:, :, 0:nk], scale, bias(t, nk), ALU.mult, ALU.add))
                link(nc.vector.tensor_reduce(mx, Lt, AX.X, ALU.max))
                if sinks is not None:
                    link(nc.vector.tensor_tensor(mx, mx, sinks, ALU.max))
                    link(nc.vector.tensor_tensor(es, sinks, mx, ALU.subtract))
                link(nc.vector.tensor_tensor(Lt, Lt, mx.unsqueeze(2).to_broadcast([P, HEADS, nk]), ALU.subtract))
                dve.sem_inc(shifted, 1)
                dve.wait_ge(exp_done, t + 1)
                link(nc.vector.tensor_reduce(sm, Lt, AX.X, ALU.add))
                if mask is not None:
                    link(nc.vector.tensor_tensor(Lt, Lt, mask(t), ALU.mult))
                dve.sem_inc(probs, 1)
                if sinks is not None:
                    dve.wait_ge(sink_done, t + 1)
                    link(nc.vector.tensor_tensor(sm, sm, es, ALU.add))
                link(nc.vector.reciprocal(sm, sm))
                if factor is not None:
                    link(nc.vector.tensor_tensor(sm, sm, factor(t), ALU.mult))
                dve.wait_ge(turned, t + 1)
                nc.vector.tensor_copy(PT[0:w, 0:n // 2, :], T[0:w, 0:n // 2, :]).then_inc(pt_dve, 1)
                dve.wait_ge(outs, t + 1)
                o3 = O.rearrange("p (h w) -> p h w", h=HEADS)
                dst = (tmp if add else out[:, t, :]).rearrange("p (h w) -> p h w", h=HEADS)
                link(nc.vector.tensor_tensor(dst, o3, sm.unsqueeze(2).to_broadcast([P, HEADS, hd]), ALU.mult))
                dve.sem_inc(written, 1)
                if add:
                    link(nc.vector.tensor_tensor(out[:, t, :], out[:, t, :], tmp, ALU.add))
    stage.close()
    arena.at = mark


GLA_HEADS, GLA_K, GLA_V, GLA_RANK = 4, 64, 128, 16
HG_HEADS, HG_K, HG_V = 4, 128, 128


def decay_stage(nc, tag, abT, gate_up, gate_bias, g, consts, arena, banks):
    stage = Stage(nc, tag)
    sem = stage.sem
    mark = arena.at
    W = GLA_HEADS * GLA_K
    up, brow = arena.take([W], parts=GLA_RANK), arena.take([W], parts=1)
    z, e = arena.take([TILES, W]), arena.take([TILES, W])
    landed, made, absolute, logged, step, astep = (sem(n) for n in ("w", "z", "abs", "log", "dve", "act"))
    with nc.Block() as block:
        @block.sync
        def _(sp):
            sp.dma_start(up, gate_up).then_inc(landed, 16)
            sp.dma_start(brow, gate_bias.unsqueeze(0)).then_inc(landed, 16)

        @block.tensor
        def _(pe):
            pe.wait_ge(landed, 32)
            for t in range(TILES):
                nc.tensor.matmul(banks[0][:, t * W:(t + 1) * W], abT[:, 0, t * P:(t + 1) * P], up, start=True, stop=False)
                m = nc.tensor.matmul(banks[0][:, t * W:(t + 1) * W], consts["ones"][0:1, :], brow, start=False, stop=True)
            m.then_inc(made, 1)

        @block.scalar
        def _(act):
            link = Chain(act, astep)
            act.wait_ge(absolute, 1)
            link(nc.scalar.activation(e, e, ACT.Exp, scale=-1.0))
            nc.scalar.activation(e, e, ACT.Ln, bias=1.0).then_inc(logged, 1)

        @block.vector
        def _(dve):
            link = Chain(dve, step)
            dve.wait_ge(made, 1)
            link(nc.vector.tensor_copy(z, banks[0][:, 0:TILES * W].rearrange("p (t n) -> p t n", t=TILES)))
            link(nc.vector.scalar_tensor_tensor(e, z, -1.0, z, ALU.mult, ALU.max))
            dve.sem_inc(absolute, 1)
            link(nc.vector.tensor_scalar(z, z, 0.0, None, ALU.min))
            dve.wait_ge(logged, 1)
            link(nc.vector.tensor_tensor(z, z, e, ALU.subtract))
            link(nc.vector.tensor_scalar(g, z, 1.0 / 16.0, None, ALU.mult))
    stage.close()
    arena.at = mark


def gla_stage(nc, tag, g, qT, kT, k, v, out, consts, arena, psum, banks):
    stage = Stage(nc, tag)
    sem = stage.sem
    mark = arena.at
    FC = GLA_HEADS * GLA_K // P
    W = GLA_HEADS * GLA_K
    eb, ei = arena.take([FC, TOK]), arena.take([FC, TOK])
    er = arena.take([TILES, W])
    AT = arena.take([2, 4, P])
    St = arena.take([CHUNKS - 1, FC, GLA_V])
    sums, exps, decayed, attn, masked, upd, states, outs, step = (
        sem(n) for n in ("sums", "exps", "decayed", "attn", "masked", "upd", "states", "outs", "dve"))
    Bs, Rs = banks[0][:, :].rearrange("p (f n) -> p f n", f=FC), banks[1][:, :].rearrange("p (t n) -> p t n", t=TILES)

    def U(c, rows, f):
        at = (c // 2) * FC * GLA_V + f * GLA_V
        return banks[4 + c % 2][rows, at:at + GLA_V]

    with nc.Block() as block:
        @block.tensor
        def _(pe):
            for f in range(FC):
                for t in range(TILES):
                    nc.tensor.matmul(Bs[:, f, t * P:(t + 1) * P], g[:, t, f * P:(f + 1) * P], consts["upto"][:, :], start=True, stop=True)
            for t in range(TILES):
                m = nc.tensor.matmul(Rs[:, t, :], consts["after"][:, :], g[:, t, :], start=True, stop=True)
            m.then_inc(sums, 1)
            pe.wait_ge(decayed, 1)
            for h in range(GLA_HEADS):
                rows = slice(64 * (h % 2), 64 * (h % 2) + 64)
                for t in range(TILES):
                    n = (h // 2) * TILES + t
                    m = nc.tensor.matmul(banks[2 + h % 2][:, n * P:(n + 1) * P], ei[rows, h // 2, t * P:(t + 1) * P],
                                         eb[rows, h // 2, t * P:(t + 1) * P], start=True, stop=True)
            m.then_inc(attn, 1)
            for c in range(CHUNKS - 1):
                rows, t = slice(64 * (c % 2), 64 * (c % 2) + 64), c // 2
                for h in range(GLA_HEADS):
                    m = nc.tensor.matmul(U(c, slice(64 * (h % 2), 64 * (h % 2) + 64), h // 2), er[rows, t, h * GLA_K:(h + 1) * GLA_K],
                                         v[rows, t, h * GLA_V:(h + 1) * GLA_V], start=True, stop=True, skip_group_check=True)
            m.then_inc(upd, 1)
            pe.wait_ge(masked, 1)
            pe.wait_ge(states, 1)
            for h in range(GLA_HEADS):
                rows = slice(64 * (h % 2), 64 * (h % 2) + 64)
                for t in range(TILES):
                    n = (h // 2) * TILES + t
                    o = banks[6 + h % 2][:, n * P:(n + 1) * P]
                    m = nc.tensor.matmul(o, AT[:, h % 2, n, :], v[:, t, h * GLA_V:(h + 1) * GLA_V], start=True, stop=False,
                                         skip_group_check=True)
                    for c in (2 * t, 2 * t + 1):
                        if c:
                            half = slice(64 * (c % 2), 64 * (c % 2) + 64)
                            m = nc.tensor.matmul(o[half, :], eb[rows, h // 2, c * CHUNK:(c + 1) * CHUNK], St[rows, c - 1, h // 2, :],
                                                 start=False, stop=True, skip_group_check=True)
            m.then_inc(outs, 1)

        dec = arena.take([FC, CHUNKS])

        @block.scalar
        def _(act):
            act.wait_ge(sums, 1)
            nc.scalar.activation(eb, Bs, ACT.Exp)
            nc.scalar.activation(ei, Bs, ACT.Exp, scale=-1.0)
            nc.scalar.activation(er, Rs, ACT.Exp).then_inc(exps, 1)

        @block.vector
        def _(dve):
            link = Chain(dve, step)
            dve.wait_ge(exps, 1)
            link(nc.vector.tensor_copy(dec, eb.rearrange("p f (c n) -> p f c n", n=CHUNK)[:, :, :, CHUNK - 1]))
            link(nc.vector.scalar_tensor_tensor(eb, qT, GLA_K ** -0.5, eb, ALU.mult, ALU.mult))
            link(nc.vector.tensor_tensor(ei, kT, ei, ALU.mult))
            link(nc.vector.tensor_tensor(er, k, er, ALU.mult))
            dve.sem_inc(decayed, 1)
            dve.wait_ge(attn, 1)
            for par in range(2):
                link(nc.vector.tensor_tensor(AT[:, par], banks[2 + par][:, :].rearrange("p (n k) -> p n k", n=4),
                                             consts["upto"][:, :].unsqueeze(1).to_broadcast([P, 4, P]), ALU.mult))
            dve.sem_inc(masked, 1)
            dve.wait_ge(upd, 1)
            for c in range(CHUNKS - 1):
                for f in range(FC):
                    if c == 0:
                        link(nc.vector.tensor_copy(St[:, 0, f, :], U(c, slice(0, P), f)))
                    else:
                        link(nc.vector.scalar_tensor_tensor(St[:, c, f, :], St[:, c - 1, f, :], dec[:, f, c:c + 1],
                                                            U(c, slice(0, P), f), ALU.mult, ALU.add))
            dve.sem_inc(states, 1)
            dve.wait_ge(outs, 1)
            o5 = out.rearrange("p t (h q v) -> p q h t v", q=2, v=GLA_V)
            for par in range(2):
                for t in range(TILES):
                    link(nc.vector.tensor_copy(o5[:, par, :, t, :], banks[6 + par][:, :].rearrange("p (h t v) -> p h t v", h=2, t=2)[:, :, t, :]))
    stage.close()
    arena.at = mark


def forget_stage(nc, tag, lb_logits, z, f, k, g, arena):
    stage = Stage(nc, tag)
    sem = stage.sem
    mark = arena.at
    W = HG_HEADS * HG_K
    l, mx = arena.take([2, W]), arena.take([W])
    landed, sig, asked, exped, made, step, astep = (sem(n) for n in ("l", "sig", "asked", "exp", "made", "dve", "act"))
    with nc.Block() as block:
        @block.sync
        def _(sp):
            for i in range(2):
                sp.dma_start(l[:, i], lb_logits[i].partition_broadcast(P)).then_inc(landed, 16)

        @block.scalar
        def _(act):
            nc.scalar.activation(f, z, ACT.Sigmoid).then_inc(sig, 1)
            act.wait_ge(asked, 1)
            nc.scalar.activation(l, l, ACT.Exp).then_inc(exped, 1)
            act.wait_ge(made, 1)
            nc.scalar.activation(g, f, ACT.Ln)

        @block.vector
        def _(dve):
            link = Chain(dve, step)
            dve.wait_ge(landed, 32)
            link(nc.vector.tensor_tensor(mx, l[:, 0], l[:, 1], ALU.max))
            link(nc.vector.tensor_tensor(l, l, mx.unsqueeze(1).to_broadcast([P, 2, W]), ALU.subtract))
            dve.sem_inc(asked, 1)
            dve.wait_ge(exped, 1)
            link(nc.vector.tensor_tensor(mx, l[:, 0], l[:, 1], ALU.add))
            link(nc.vector.reciprocal(mx, mx))
            link(nc.vector.tensor_tensor(l[:, 0], l[:, 0], mx, ALU.mult))
            link(nc.vector.tensor_scalar(l[:, 1], l[:, 0], -1.0, 1.0, ALU.mult, ALU.add))
            dve.wait_ge(sig, 1)
            link(nc.vector.tensor_tensor(f, f, l[:, 1].unsqueeze(1).to_broadcast([P, TILES, W]), ALU.mult))
            link(nc.vector.tensor_tensor(f, f, l[:, 0].unsqueeze(1).to_broadcast([P, TILES, W]), ALU.add))
            dve.sem_inc(made, 1)
            link(nc.vector.tensor_scalar(k, f, -1.0, 1.0, ALU.mult, ALU.add))
    stage.close()
    arena.at = mark


def hgrn_stage(nc, tag, g, qT, kT, k, v, out, consts, arena, banks):
    stage = Stage(nc, tag)
    sem = stage.sem
    mark = arena.at
    H, W = HG_HEADS, HG_HEADS * HG_K
    U = H * TILES
    b, eb, er = arena.take([H, TOK]), arena.take([H, TOK]), arena.take([TILES, W])
    ex, ql, kl = arena.take([H * TOK]), arena.take([H * TOK]), arena.take([H * TOK])
    A, tmp = arena.take([U, P]), arena.take([U, P])
    St, dec = arena.take([CHUNKS - 1, H, HG_V]), arena.take([H, CHUNKS])
    sums, exps, decayed, upd, asked, exped, split, level, added, states, outs, step = (
        sem(n) for n in ("sums", "exps", "decayed", "upd", "asked", "exped", "split", "level", "added", "states", "outs", "dve"))
    flat = lambda ap: ap.rearrange("p h n -> p (h n)")
    with nc.Block() as block:
        @block.tensor
        def _(pe):
            for h in range(H):
                for t in range(TILES):
                    nc.tensor.matmul(banks[h // 2][:, (h % 2) * TOK + t * P:(h % 2) * TOK + (t + 1) * P],
                                     g[:, t, h * P:(h + 1) * P], consts["upto"][:, :], start=True, stop=True)
            for t in range(TILES):
                m = nc.tensor.matmul(banks[2 + t][:, :], consts["after"][:, :], g[:, t, :], start=True, stop=True)
            m.then_inc(sums, 1)
            pe.wait_ge(decayed, 1)
            for c in range(CHUNKS - 1):
                rows = slice(64 * (c % 2), 64 * (c % 2) + 64)
                for h in range(H):
                    m = nc.tensor.matmul(banks[4 + c][:, h * HG_V:(h + 1) * HG_V], er[rows, c // 2, h * P:(h + 1) * P],
                                         v[rows, c // 2, h * HG_V:(h + 1) * HG_V], start=True, stop=True)
            m.then_inc(upd, 1)
            for n in range(len(LEVELS) + 1):
                if n < len(LEVELS):
                    pe.wait_ge(split, n + 1)
                if n:
                    pe.wait_ge(added, n)
                for u in range(U):
                    s = slice(u * P, (u + 1) * P)
                    kk, qq = (kl[:, s], ql[:, s]) if n < len(LEVELS) else (flat(kT)[:, s], flat(qT)[:, s])
                    m = nc.tensor.matmul(banks[u // 4][:, (u % 4) * P:(u % 4 + 1) * P], kk, qq, start=True, stop=True)
                m.then_inc(level, 1)
            pe.wait_ge(states, 1)
            pe.wait_ge(added, len(LEVELS) + 1)
            for t in range(TILES):
                for h in range(H):
                    o = banks[2 + t][:, h * HG_V:(h + 1) * HG_V]
                    m = nc.tensor.matmul(o, A[:, h * TILES + t, :], v[:, t, h * HG_V:(h + 1) * HG_V], start=True, stop=False,
                                         skip_group_check=True)
                    for c in (2 * t, 2 * t + 1):
                        if c:
                            half = slice(64 * (c % 2), 64 * (c % 2) + 64)
                            m = nc.tensor.matmul(o[half, :], eb[:, h, c * CHUNK:(c + 1) * CHUNK], St[:, c - 1, h, :],
                                                 start=False, stop=True, skip_group_check=True)
            m.then_inc(outs, 1)

        @block.scalar
        def _(act):
            act.wait_ge(sums, 1)
            for i in range(2):
                src = banks[i][:, :].rearrange("p (h n) -> p h n", h=2)
                nc.scalar.activation(eb[:, 2 * i:2 * i + 2, :], src, ACT.Exp)
                nc.scalar.copy(b[:, 2 * i:2 * i + 2, :], src)
            for t in range(TILES):
                m = nc.scalar.activation(er[:, t], banks[2 + t][:, :], ACT.Exp)
            m.then_inc(exps, 1)
            for n in range(len(LEVELS)):
                act.wait_ge(asked, n + 1)
                nc.scalar.activation(ex, ex, ACT.Exp).then_inc(exped, 1)

        @block.vector
        def _(dve):
            link = Chain(dve, step)
            link(nc.vector.memset(ql, 0.0))
            link(nc.vector.memset(kl, 0.0))
            dve.wait_ge(exps, 1)
            link(nc.vector.tensor_copy(dec, eb.rearrange("p h (c n) -> p h c n", n=CHUNK)[:, :, :, CHUNK - 1]))
            link(nc.vector.tensor_tensor(eb, eb, qT, ALU.mult))
            link(nc.vector.tensor_tensor(er, er, k, ALU.mult))
            dve.sem_inc(decayed, 1)
            for n, m in enumerate(LEVELS + (0,)):
                if m:
                    def halves(ap, m=m):
                        v4 = ap.rearrange("p (n two m) -> p n two m", two=2, m=m)
                        return v4[:, :, 0, :], v4[:, :, 1, :]
                    b0, b1 = halves(flat(b))
                    e0, e1 = halves(ex)
                    r = b0[:, :, m - 1:m].to_broadcast([P, H * TOK // (2 * m), m])
                    if n:
                        dve.wait_ge(level, n)
                    link(nc.vector.tensor_tensor(e0, r, b0, ALU.subtract))
                    link(nc.vector.tensor_tensor(e1, b1, r, ALU.subtract))
                    dve.sem_inc(asked, 1)
                    dve.wait_ge(exped, n + 1)
                    link(nc.vector.tensor_tensor(halves(kl)[0], halves(flat(kT))[0], e0, ALU.mult))
                    link(nc.vector.tensor_tensor(halves(ql)[1], halves(flat(qT))[1], e1, ALU.mult))
                    dve.sem_inc(split, 1)
                dve.wait_ge(level, n + 1)
                mask = consts["levels"][:, n * P:(n + 1) * P].unsqueeze(1).to_broadcast([P, 4, P])
                for i in range(2):
                    dst = (tmp if n else A)[:, 4 * i:4 * i + 4, :]
                    link(nc.vector.tensor_tensor(dst, banks[i][:, :].rearrange("p (u k) -> p u k", u=4), mask, ALU.mult))
                if n:
                    link(nc.vector.tensor_tensor(A, A, tmp, ALU.add))
                dve.sem_inc(added, 1)
            dve.wait_ge(upd, 1)
            for c in range(CHUNKS - 1):
                u3 = banks[4 + c][:, :].rearrange("p (h v) -> p h v", h=H)
                if c == 0:
                    link(nc.vector.tensor_copy(St[:, 0], u3))
                else:
                    link(nc.vector.tensor_tensor(St[:, c], St[:, c - 1], dec[:, :, c:c + 1].to_broadcast([P, H, HG_V]), ALU.mult))
                    link(nc.vector.tensor_tensor(St[:, c], u3, St[:, c], ALU.add))
            dve.sem_inc(states, 1)
            dve.wait_ge(outs, 1)
            for t in range(TILES):
                link(nc.vector.tensor_copy(out[:, t, :], banks[2 + t][:, :]))
    stage.close()
    arena.at = mark


def gate_stage(nc, tag, jobs):
    stage = Stage(nc, tag)
    done, step = stage.sem("done"), stage.sem("dve")
    with nc.Block() as block:
        @block.scalar
        def _(act):
            for func, src, dst, times in jobs:
                nc.scalar.activation(src if times else dst, src, func).then_inc(done, 1)

        @block.vector
        def _(dve):
            link = Chain(dve, step)
            for n, (func, src, dst, times) in enumerate(jobs):
                if times:
                    dve.wait_ge(done, n + 1)
                    link(nc.vector.tensor_tensor(dst, dst, src, ALU.mult))
    stage.close()


def rope_stage(nc, tag, jobs, arena):
    stage = Stage(nc, tag)
    step = stage.sem("dve")
    mark = arena.at
    half = ROPE_DIM // 2
    with nc.Block() as block:
        @block.vector
        def _(dve):
            link = Chain(dve, step)
            tmp = arena.take([4, HEADS, half])
            for rows, cos, sin in jobs:
                np_, n = rows.shape[0], rows.shape[1]
                cb, sb = (a.unsqueeze(1).to_broadcast([np_, n, half]) for a in (cos, sin))
                t1, t2 = rows[:, :, 0:half], rows[:, :, half:ROPE_DIM]
                a, b, c, d = (tmp[0:np_, i, 0:n, :] for i in range(4))
                nc.vector.tensor_tensor(a, t1, cb, ALU.mult)
                nc.vector.tensor_tensor(b, t2, sb, ALU.mult)
                nc.vector.tensor_tensor(c, t2, cb, ALU.mult)
                link(nc.vector.tensor_tensor(d, t1, sb, ALU.mult))
                nc.vector.tensor_tensor(t1, a, b, ALU.subtract)
                link(nc.vector.tensor_tensor(t2, c, d, ALU.add))
    stage.close()
    arena.at = mark


def compress_stage(nc, tag, inT, pos, w_k, w_v, kcT, vc, consts, arena, banks):
    stage = Stage(nc, tag)
    sem = stage.sem
    mark = arena.at
    hd = 64
    prow, posT = arena.take([hd], parts=CMP_LEN), arena.take([CMP_LEN], parts=hd)
    w = arena.take([2, CMP_LEN, hd], parts=hd)
    blk = arena.take([4, CMP_LEN, N_CMP], parts=hd)
    kc, tmp = arena.take([2, hd], parts=N_CMP), arena.take([4, 2, ROPE_DIM // 2], parts=N_CMP)
    landed, turned, added, made, roped, back, step = (sem(n) for n in ("w", "turned", "added", "made", "roped", "back", "dve"))
    with nc.Block() as block:
        @block.sync
        def _(sp):
            sp.dma_start(prow, pos).then_inc(landed, 16)
            sp.dma_start(w[:, 0], w_k.rearrange("(l d) o -> d l o", d=hd)).then_inc(landed, 16)
            sp.dma_start(w[:, 1], w_v.rearrange("(l d) o -> d l o", d=hd)).then_inc(landed, 16)

        @block.tensor
        def _(pe):
            pe.wait_ge(landed, 48)
            nc.tensor.transpose(banks[0][0:hd, 0:CMP_LEN], prow, consts["ident"][0:CMP_LEN, 0:CMP_LEN]).then_inc(turned, 1)
            pe.wait_ge(added, 1)
            for u in range(4):
                for l in range(CMP_LEN):
                    m = nc.tensor.matmul(banks[1][0:N_CMP, u * hd:(u + 1) * hd], blk[:, u, l, :], w[:, u // 2, l, :],
                                         start=(l == 0), stop=(l == CMP_LEN - 1))
            m.then_inc(made, 1)
            pe.wait_ge(roped, 1)
            for g in range(2):
                m = nc.tensor.transpose(banks[2][0:hd, g * 64:g * 64 + N_CMP], kc[:, g, :], consts["ident"][0:N_CMP, 0:N_CMP])
            m.then_inc(back, 1)

        @block.vector
        def _(dve):
            link = Chain(dve, step)
            dve.wait_ge(turned, 1)
            link(nc.vector.tensor_copy(posT, banks[0][0:hd, 0:CMP_LEN]))
            for u in range(4):
                src = inT[:, u, :]
                windows = bass.AP(src.tensor, src.offset, [src.ap[0], [1, CMP_LEN], [CMP_STRIDE, N_CMP]])
                link(nc.vector.tensor_tensor(blk[:, u], windows, posT.unsqueeze(2).to_broadcast([hd, CMP_LEN, N_CMP]), ALU.add))
            dve.sem_inc(added, 1)
            dve.wait_ge(made, 1)
            link(nc.vector.tensor_copy(kc, banks[1][0:N_CMP, 0:2 * hd].rearrange("p (g d) -> p g d", g=2)))
            link(nc.vector.tensor_copy(vc, banks[1][0:N_CMP, 2 * hd:4 * hd].rearrange("p (g d) -> p g d", g=2)))
            half = ROPE_DIM // 2
            cs = consts["rope_cmp"]
            cb, sb = (cs[0:N_CMP, i * half:(i + 1) * half].unsqueeze(1).to_broadcast([N_CMP, 2, half]) for i in range(2))
            t1, t2 = kc[:, :, 0:half], kc[:, :, half:ROPE_DIM]
            for i, (x_, y_) in enumerate(((t1, cb), (t2, sb), (t2, cb), (t1, sb))):
                link(nc.vector.tensor_tensor(tmp[:, i], x_, y_, ALU.mult))
            link(nc.vector.tensor_tensor(t1, tmp[:, 0], tmp[:, 1], ALU.subtract))
            link(nc.vector.tensor_tensor(t2, tmp[:, 2], tmp[:, 3], ALU.add))
            dve.sem_inc(roped, 1)
            dve.wait_ge(back, 1)
            link(nc.vector.tensor_copy(kcT, banks[2][0:hd, 0:2 * 64].rearrange("p (g n) -> p g n", g=2)[:, :, 0:N_CMP]))
    stage.close()
    arena.at = mark


def copy_stage(nc, tag, pairs):
    stage = Stage(nc, tag)
    landed = stage.sem("landed")
    with nc.Block() as block:
        @block.sync
        def _(sp):
            for dst, src in pairs:
                sp.dma_start(dst, src).then_inc(landed, 16)
            sp.wait_ge(landed, 16 * len(pairs))
    stage.close()


def program(nc, ins, const_dram, out, dump=None):
    psum = nc.alloc_psum_tensor("psum", [P, 4096], F32)
    banks = [psum[:, 512 * i:512 * (i + 1)] for i in range(8)]
    x, h, hT = (nc.alloc_sbuf_tensor(n, s, F32)[:, :, :] for n, s in (("x", [P, TILES, D]), ("h", [P, TILES, D]), ("hT", [P, DC, TOK])))
    consts = alloc_consts(nc)
    ident = consts["ident"]
    scratch = nc.dram_tensor("skew_scratch", (HEADS, P, SKEW), F32).ap()
    arena = Arena(nc, (nc.sbuf_usable_end - nc.sbuf_base) // 4 - 3 * 2048 * 0 - ARENA_SPARE)
    rows = lambda ap: ap.rearrange("(t p) d -> p t d", p=P)
    copy_stage(nc, "start", [(consts[n][0:const_dram[n].shape[0], :], const_dram[n]) for n in consts] + [(x[:, :, :], rows(ins["x"][0]))])

    def moe(tag, gate2, names, layer):
        wg, bg, wr, br, w1, w3, w2 = (ins[n][layer] for n in names)
        mark = arena.at
        mem = alloc_moe(nc, arena)
        moe_stage(nc, tag, x, h, hT, gate2, wg, bg, wr, br, w1, w3, w2, consts, mem, banks)
        arena.at = mark

    def normed(tag, w, scale=None, shift=None):
        norm_stage(nc, tag, x, h, w, scale, shift, arena)
        turn_stage(nc, tag + "_turn", [(h, P, DC, hT)], ident, banks)

    for layer in range(2):
        L = f"l{layer}"
        mod = arena.take([6 * D])
        modulation_stage(nc, L + "_mod", ins["c"][0], ins["ada_w"][layer], ins["ada_b"][layer], mod, consts, arena, banks)
        shift1, scale1, gate1, shift2, scale2, gate2 = (mod[:, i * D:(i + 1) * D] for i in range(6))
        normed(L + "_norm1", ins["norm1_w"][layer], scale1, shift1)
        mark = arena.at
        o = arena.take([TILES, D])
        bias = arena.take([HEADS, TOK])
        if layer == 0:
            N = ins["even_w_in"].shape[2]
            pr = arena.take([TILES, N])
            project_stage(nc, L + "_in", hT, DC, ins["even_w_in"][0], N // 5, pr, arena, banks)
            qa, ka, va, qb, kb, vb, rb, ab = (pr[:, :, a:b] for a, b in (
                (0, 512), (512, 640), (640, 768), (768, 1024), (1024, 1280), (1280, 1792), (1792, 2304), (2304, 2320)))
            head_norm_stage(nc, L + "_qknorm", [(qa, 8, 64, ins["a_q_norm"][0]), (ka, 2, 64, ins["a_k_norm"][0])], arena)
            qT, kT = arena.take([HEADS, TOK], parts=64), arena.take([2, TOK], parts=64)
            qbT, kbT, abT = arena.take([2, TOK]), arena.take([2, TOK]), arena.take([1, TOK], parts=16)
            turn_stage(nc, L + "_turn", [(qa, 64, 8, qT), (ka, 64, 2, kT), (qb, P, 2, qbT), (kb, P, 2, kbT), (ab, 16, 1, abT)],
                       ident, banks)
            bias_stage(nc, L + "_bias", ins["rel_bias"], consts["hot_window"], bias, scratch, arena, banks)
            sinks = arena.take([HEADS])
            copy_stage(nc, L + "_sinks", [(sinks, ins["a_sinks"][0].partition_broadcast(P))])
            attend_stage(nc, L + "_swa", qT, kT, lambda kt, kv: va[:, kt, kv * 64:(kv + 1) * 64], 64, lambda hh: hh // 4, 64 ** -0.5,
                         lambda t, nk: bias[:, :, TOK - nk:], o[:, :, 0:512], ident, arena, psum, sinks=sinks)
            g = arena.take([TILES, 256])
            decay_stage(nc, L + "_decay", abT, ins["b_gate_up"][0], ins["b_gate_bias"][0], g, consts, arena, banks)
            ob = arena.take([TILES, 512])
            gla_stage(nc, L + "_gla", g, qbT, kbT, kb, vb, ob, consts, arena, psum, banks)
            head_norm_stage(nc, L + "_onorm", [(ob, 4, 128, ins["b_out_norm"][0])], arena)
            gate_stage(nc, L + "_ogate", [(ACT.Silu, rb, ob, True)])
            gate_stage(nc, L + "_put", [(ACT.Copy, ob, o[:, :, 512:1024], False)])
            w_out = ins["even_w_out"][0]
        else:
            pr = arena.take([TILES, 3 * D])
            project_stage(nc, L + "_in", hT, DC, ins["odd_w_in"][0], 512, pr, arena, banks)
            q, k, v = (pr[:, :, i * D:(i + 1) * D] for i in range(3))
            head_norm_stage(nc, L + "_qknorm", [(q, 8, 128, ins["c_q_norm"][0]), (k, 8, 128, ins["c_k_norm"][0])], arena)
            qT, kT = arena.take([HEADS, TOK]), arena.take([HEADS, TOK])
            turn_stage(nc, L + "_turn", [(q, P, 8, qT), (k, P, 8, kT)], ident, banks)
            bias_stage(nc, L + "_bias", ins["rel_bias"], consts["hot_causal"], bias, scratch, arena, banks)
            attend_stage(nc, L + "_attn", qT, kT, lambda kt, kv: v[:, kt, kv * P:(kv + 1) * P], P, lambda hh: hh, P ** -0.5,
                         lambda t, nk: bias[:, :, TOK - nk:], o, ident, arena, psum)
            w_out = ins["odd_w_out"][0]
        turn_stage(nc, L + "_oturn", [(o, P, DC, hT)], ident, banks)
        gate_both = bass.AP(gate1.tensor, gate1.offset, [gate1.ap[0], [0, TILES], [1, D]])
        project_stage(nc, L + "_out", hT, DC, w_out, 512, x, arena, banks, gate=gate_both, add=True)
        if dump: dump(L + "_mix", x)
        arena.at = mark
        normed(L + "_norm2", ins["norm2_w"][layer], scale2, shift2)
        moe(L + "_moe", gate2, ("moe_w_group", "moe_b_group", "moe_w_expert", "moe_b_expert", "moe_w1", "moe_w3", "moe_w2"), layer)
        if dump: dump(L + "_moe", x)
        arena.at = 0

    normed("s_norm1", ins["attn_norm_2"][0])
    mark = arena.at
    o = arena.take([TILES, D])
    N = ins["w_in_2"].shape[2]
    pr = arena.take([TILES, N])
    project_stage(nc, "s_in", hT, DC, ins["w_in_2"][0], N // 12, pr, arena, banks)
    kv = pr[:, :, 512:1280].rearrange("p t (s g d) -> p t s g d", s=6, g=2)
    mark2 = arena.at
    half = ROPE_DIM // 2
    rope = consts["rope"][:, :].rearrange("p (t n) -> p t n", t=TILES)
    heads = lambda ap: ap.rearrange("p (n d) -> p n d", d=64)
    jobs = []
    for t in range(TILES):
        cs = (rope[:, t, 0:half], rope[:, t, half:])
        jobs += [(heads(pr[:, t, 0:512]), *cs), (kv[:, t, 2], *cs), (kv[:, t, 4], *cs)]
    rope_stage(nc, "s_rope", jobs, arena)
    qT, cT = arena.take([HEADS, TOK], parts=64), arena.take([4, TOK], parts=64)
    ksT, kwT = arena.take([2, TOK], parts=64), arena.take([2, TOK], parts=64)
    turn_stage(nc, "s_turn", [(pr[:, :, 0:512], 64, 8, qT), (pr[:, :, 512:768], 64, 4, cT), (pr[:, :, 768:896], 64, 2, ksT),
                              (pr[:, :, 1024:1152], 64, 2, kwT)], ident, banks)
    kcT, vc = arena.take([2, N_CMP], parts=64), arena.take([2, 64], parts=N_CMP)
    compress_stage(nc, "s_cmp", cT, ins["cmp_pos_2"][0], ins["w_cmp_k_2"][0], ins["w_cmp_v_2"][0], kcT, vc, consts, arena, banks)
    gates = pr[:, :, 1280:1304].rearrange("p t (h i) -> p i t h", i=3)
    gate_stage(nc, "s_gates", [(ACT.Sigmoid, pr[:, :, 1280:1304], pr[:, :, 1280:1304], False),
                               (ACT.Sigmoid, pr[:, :, 3352:], pr[:, :, 3352:], False)])
    cb = consts["cmp_bias"][:, :].rearrange("p (t n) -> p t n", t=TILES)
    cm = consts["cmp_mask"][:, :].rearrange("p (t n) -> p t n", t=TILES)
    o_nsa = o[:, :, 0:512]
    attend_stage(nc, "s_acmp", qT, kcT, lambda kt, g_: vc[:, g_, :], 64, lambda hh: hh // 4, 64 ** -0.5,
                 lambda t, nk: cb[:, t, :].unsqueeze(1).to_broadcast([P, HEADS, N_CMP]), o_nsa, ident, arena, psum,
                 factor=lambda t: gates[:, 0, t, :], keys=N_CMP,
                 mask=lambda t: cm[:, t, :].unsqueeze(1).to_broadcast([P, HEADS, N_CMP]))
    for i, (tag, kk, s) in enumerate((("s_aslc", ksT, 3), ("s_awin", kwT, 5))):
        attend_stage(nc, tag, qT, kk, lambda kt, g_, s=s: kv[:, kt, s, g_, :], 64, lambda hh: hh // 4, 64 ** -0.5,
                     lambda t, nk: consts["causal"][:, TOK - nk:].unsqueeze(1).to_broadcast([P, HEADS, nk]), o_nsa, ident, arena, psum,
                     factor=lambda t, i=i: gates[:, i + 1, t, :], add=True)
    if dump: dump("s_nsa", o)
    arena.at = mark2
    hq, hf, hi, hg = (pr[:, :, 1304 + i * 512:1304 + (i + 1) * 512] for i in range(4))
    kk, g = arena.take([TILES, 512]), arena.take([TILES, 512])
    forget_stage(nc, "s_forget", ins["hg_lb_logits_2"], hf, hf, kk, g, arena)
    hqT, hkT = arena.take([HG_HEADS, TOK]), arena.take([HG_HEADS, TOK])
    turn_stage(nc, "s_hturn", [(hq, P, 4, hqT), (kk, P, 4, hkT)], ident, banks)
    o_hg = o[:, :, 512:1024]
    hgrn_stage(nc, "s_hgrn", g, hqT, hkT, kk, hi, o_hg, consts, arena, banks)
    head_norm_stage(nc, "s_hnorm", [(o_hg, 4, 128, ins["hg_norm_2"][0])], arena)
    gate_stage(nc, "s_hgate", [(ACT.Silu, hg, o_hg, True)])
    arena.at = mark2
    turn_stage(nc, "s_oturn", [(o, P, DC, hT)], ident, banks)
    mixed = arena.take([TILES, D])
    project_stage(nc, "s_brn", hT[:, 0:4, :], 4, ins["w_br_nsa_2"][0], 512, mixed, arena, banks, gate=pr[:, :, 3352:3352 + D])
    project_stage(nc, "s_brh", hT[:, 4:8, :], 4, ins["w_br_hg_2"][0], 512, mixed, arena, banks, gate=pr[:, :, 3352 + D:], add=True)
    turn_stage(nc, "s_mturn", [(mixed, P, DC, hT)], ident, banks)
    project_stage(nc, "s_out", hT, DC, ins["w_out_2"][0], 512, x, arena, banks, add=True)
    if dump: dump("s_mix", x)
    arena.at = mark
    normed("s_norm2", ins["ffn_norm_2"][0])
    moe("s_moe", None, ("w_grp_2", "b_grp_2", "w_rtr_2", "b_rtr_2", "w_gate_2", "w_up_2", "w_down_2"), 0)
    norm_stage(nc, "final", x, h, ins["final_norm_2"], None, None, arena)
    copy_stage(nc, "end", [(rows(out[0]), h[:, :, :])])


ARENA_SPARE = 64


def alloc_moe(nc, arena):
    def sb(name, shape, dt=F32):
        ap = arena.take(shape[1:])
        return ap if dt == F32 else ap.bitcast(dt)
    W = ROUNDS * E + 4
    return dict(
        rt=sb("rt", [P, DC, 36]), rb=sb("rb", [P, 36]), lg=sb("lg", [P, TILES, 36]), small=sb("small", [P, 8, 64]),
        mask=sb("mask", [P, TILES, E]), slots=sb("slots", [P, TILES, W]), comb=sb("comb", [P, TILES, W]),
        nsteps=sb("nsteps", [P, 1], I32), sel=sb("sel", [P, 2, TILES, BLOCK]), selw=sb("selw", [P, 2, TILES, P]),
        selT=sb("selT", [P, 2, TOK]), xg=sb("xg", [P, 2, DC, BLOCK]), hm=sb("hm", [P, 256]), sil=sb("sil", [P, 256]),
        hTs=sb("hTs", [P, 2, P]), y=sb("y", [P, 2, 512]),
        w1b=sb("w1b", [P, 2, DC, FF]), w3b=sb("w3b", [P, 2, DC, FF]), w2b=sb("w2b", [P, 2, FF // P, D]))


def kernel(**inputs):
    import numpy as _np
    import concourse.bacc as _bacc
    from concourse import mybir as _mybir
    from concourse.bass_utils import run_bass_kernel_spmd as _run

    nc = _bacc.Bacc("TRN2", target_bir_lowering=False, num_devices=1)
    arrays, ins, consts = {}, {}, {}
    for name, a in inputs.items():
        a = _np.ascontiguousarray(a)
        arrays[f"in_{name}_dram"] = a
        ins[name] = nc.dram_tensor(f"in_{name}_dram", a.shape, _mybir.dt.from_np(a.dtype), kind="ExternalInput").ap()
    for name, a in host_constants().items():
        arrays[f"const_{name}_dram"] = a
        consts[name] = nc.dram_tensor(f"const_{name}_dram", a.shape, _mybir.dt.from_np(a.dtype), kind="ExternalInput").ap()
    out = nc.dram_tensor("out_dram", inputs["x"].shape, F32, kind="ExternalOutput").ap()
    program(nc, ins, consts, out)
    r = _run(nc, [arrays], core_ids=[0])
    return _np.asarray(r.results[0]["out_dram"])
```

```python
import math

import concourse.bass as bass
from concourse import mybir

F32 = mybir.dt.float32
I32 = mybir.dt.int32
ALU = mybir.AluOpType
ACT = mybir.ActivationFunctionType
AX = mybir.AxisListType

P = 128
TOK = 256
TILES = TOK // P
D = 1024
DC = D // P
E = 32
FF = 512
GROUPS = 4
PER_GROUP = 8
BLOCK = 64
ROUNDS = TOK // BLOCK
BIG = 1.0e30
EPS = 1e-6
CHUNK = 64
CHUNKS = TOK // CHUNK
REL_BUCKETS = 32
REL_MAX_DIST = 128
A_WINDOW = 128
SKEW = 384
LEVELS = (32, 16, 8, 4, 2, 1)
ROPE_DIM = 16
ROPE_THETA = 500000.0
CMP_LEN, CMP_STRIDE = 32, 16
N_CMP = (TOK - CMP_LEN) // CMP_STRIDE + 1
HEADS = 8


class Stage:

    def __init__(self, nc, name):
        self.nc, self.name, self.sems = nc, name, []

    def sem(self, name):
        self.sems.append(self.nc.alloc_semaphore(name=f"{self.name}_{name}"))
        return self.sems[-1]

    def close(self):
        self.nc.clear_and_free_semaphores(self.sems)
        self.nc.all_engine_barrier()


class Chain:

    def __init__(self, eng, sem):
        self.eng, self.sem, self.n = eng, sem, 0

    def __call__(self, ins):
        self.n += 1
        ins.then_inc(self.sem, 1)
        self.eng.wait_ge(self.sem, self.n)


class Experts:

    SLOTS = 3
    LOADS = tuple(len(range(slot, E, 3)) for slot in range(3))

    def __init__(self, stage, mem, extra, w_grp, b_grp, w_rtr, b_rtr, w1, w3, w2):
        self.mem = mem
        self.router = ((mem["rt"][:, :, 0:GROUPS], w_grp.rearrange("(c p) n -> p c n", p=P)),
                       (mem["rt"][:, :, GROUPS:], w_rtr.rearrange("(c p) n -> p c n", p=P)),
                       (mem["rb"][:, 0:GROUPS], b_grp.partition_broadcast(P)),
                       (mem["rb"][:, GROUPS:], b_rtr.partition_broadcast(P)))
        self.slots = [(mem["w1b"][:, u], mem["w3b"][:, u], mem["w2b"][:, u]) for u in range(2)] + [extra]
        self.rt_landed = stage.sem("router_landed")
        self.w1_landed, self.w3_landed, self.w2_landed = ([stage.sem(f"{w}_landed{u}") for u in range(3)]
                                                          for w in ("w1", "w3", "w2"))
        pairs = lambda w: w.rearrange("(j two) (c p) n -> two j p c n", two=2, p=P)
        self.w1, self.w3, self.w2 = pairs(w1), pairs(w3), pairs(w2)

    def load_up(self, sp, slot, u, pair):
        sp.dma_start(self.slots[slot][0], self.w1[u, pair]).then_inc(self.w1_landed[slot], 16)
        sp.dma_start(self.slots[slot][1], self.w3[u, pair]).then_inc(self.w3_landed[slot], 16)

    def load_down(self, sp, slot, u, pair):
        sp.dma_start(self.slots[slot][2], self.w2[u, pair]).then_inc(self.w2_landed[slot], 16)

    def prefetch(self, sp):
        for dst, src in self.router:
            sp.dma_start(dst, src).then_inc(self.rt_landed, 16)
        for u in range(2):
            self.load_up(sp, u, u, 0)
            self.load_down(sp, u, u, 0)


def moe_stage(nc, stage, experts, x, h, hT, gate2, consts, mem, ps, loads):
    sem = stage.sem
    rt, rb = mem["rt"], mem["rb"]
    ident, tri, ones, iota, order = (consts[k] for k in ("ident", "tri", "ones", "iota", "order"))
    small = mem["small"]
    slots, comb, nsteps = mem["slots"], mem["comb"], mem["nsteps"]
    sel, selw, selT, xg, hm, hTs, y = (mem[k] for k in ("sel", "selw", "selT", "xg", "hm", "hTs", "y"))
    sil = mem["sil"]
    bank_acc, bank_H, bank_T, bank_G, bank_Y = ps[0:4], ps[4], ps[5], ps[6], ps[7]
    rt_landed, w1_landed, w3_landed, w2_landed = experts.rt_landed, experts.w1_landed, experts.w3_landed, experts.w2_landed

    logits_done, mask_ready, pos_done, steps_ready = sem("logits"), sem("mask"), sem("pos"), sem("steps")
    exp_done, exp_asked = sem("exp_done"), sem("exp_asked")
    sel_built, selw_built, gathered, xg_copied = sem("sel_built"), sem("selw_built"), sem("gathered"), sem("xg_copied")
    sel_turned, selT_copied = sem("sel_turned"), sem("selT_copied")
    up_done, silu_done, hm_ready, turned, hT_copied = sem("up"), sem("silu"), sem("hm"), sem("turned"), sem("hT_copied")
    down_done, y_copied, scattered, dve_step = sem("down"), [sem("y_act"), sem("y_dve")], sem("scattered"), sem("dve_step")

    HALF = FF // 2
    H1, H3 = bank_H[:, 0:HALF], bank_H[:, HALF:FF]
    HT = bank_T[:, 0:256].rearrange("p (c n) -> p c n", c=2)
    ST = bank_T[:, 256:512].rearrange("p (t n) -> p t n", t=2)
    XG = bank_G[:, :].rearrange("p (c n) -> p c n", c=DC // 2)
    XG_first = bank_Y[:, :].rearrange("p (c n) -> p c n", c=DC // 2)
    PAIRS = E // 2

    def steps(eng):
        return eng.value_load(nsteps[0:1, 0:1], min_val=1, max_val=ROUNDS)

    with nc.Block() as block:
        @block.sync
        def _(sp):
            experts.load_down(sp, 2, 0, 1)
            loads(sp)
            sp.wait_ge(steps_ready, 1)
            rounds = steps(sp)
            with sp.Fori(0, rounds) as r:
                def refill(k, off):
                    slot, u, pair, done = off % 3, off % 2, k * 3 + off // 2, r * E + k * 6 + (off - 2)
                    sp.wait_ge(up_done, done)
                    experts.load_up(sp, slot, u, pair)
                    sp.wait_ge(down_done, done)
                    experts.load_down(sp, slot, u, pair)

                for off in range(3, 6):
                    refill(0, off)
                with sp.Fori(1, E // 6) as k:
                    for off in range(6):
                        refill(k, off)
                for off in range(E % 6):
                    refill(E // 6, off)
                with sp.If(rounds > r + 1):
                    sp.wait_ge(down_done, r * E + E)
                    for slot, u, pair in ((0, 0, 0), (1, 1, 0), (2, 0, 1)):
                        experts.load_up(sp, slot, u, pair)
                        experts.load_down(sp, slot, u, pair)

        @block.tensor
        def _(pe):
            pe.wait_ge(rt_landed, 64)
            for t in range(TILES):
                for c in range(DC):
                    m = nc.tensor.matmul(bank_H[:, t * 64:t * 64 + 36], hT[:, c, t * P:(t + 1) * P], rt[:, c, :],
                                         start=(c == 0), stop=(c == DC - 1))
            m.then_inc(logits_done, 1)
            pe.wait_ge(mask_ready, 1)
            M = mem["mask"]
            nc.tensor.matmul(bank_T[:, 0:E], tri[:, :], M[:, 0, :], start=True, stop=True)
            nc.tensor.matmul(bank_T[:, E:2 * E], ones[:, :], M[:, 0, :], start=True, stop=False)
            nc.tensor.matmul(bank_T[:, E:2 * E], tri[:, :], M[:, 1, :], start=False, stop=True)
            nc.tensor.matmul(bank_T[:, 2 * E:3 * E], ones[:, :], M[:, 0, :], start=True, stop=False)
            nc.tensor.matmul(bank_T[:, 2 * E:3 * E], ones[:, :], M[:, 1, :], start=False, stop=True).then_inc(pos_done, 1)
            for b in range(4):
                m = nc.tensor.matmul(bank_acc[b][:, :], consts["after"][0:1, :], consts["levels"][0:1, 0:512], start=True, stop=True)

            def gather(part, XG=XG):
                for c in range(DC // 2):
                    cc = part * DC // 2 + c
                    for t in range(TILES):
                        m = nc.tensor.matmul(XG[:, c, :], h[:, t, cc * P:(cc + 1) * P], sel[:, t, :],
                                             start=(t == 0), stop=(t == 1))
                m.then_inc(gathered, 1)

            def scatter(t):
                for half in range(2):
                    m = nc.tensor.matmul(bank_acc[2 * t + half][:, :], selT[:, t, :], y[:, half, :], start=False, stop=False,
                                         skip_group_check=True)
                return m

            def up(u, slot, nth):
                for w, out, landed in ((experts.slots[slot][0], H1, w1_landed), (experts.slots[slot][1], H3, w3_landed)):
                    pe.wait_ge(landed[slot], nth * 16)
                    for c in range(DC):
                        for half in range(2):
                            m = nc.tensor.matmul(out[64 * half:64 * half + 64, :], xg[:, c, BLOCK * u:BLOCK * (u + 1)],
                                                 w[:, c, half * HALF:(half + 1) * HALF],
                                                 start=(c == 0), stop=(c == DC - 1), skip_group_check=True)
                m.then_inc(up_done, 1)

            def turn():
                for c in range(2):
                    m = nc.tensor.transpose(HT[:, c, :], hm[:, c * P:(c + 1) * P], ident[:, :])
                m.then_inc(turned, 1)

            def down(slot, nth):
                pe.wait_ge(w2_landed[slot], nth * 16)
                for k in range(4):
                    for half in range(2):
                        m = nc.tensor.matmul(bank_Y[64 * half:64 * half + 64, :],
                                             hTs[:, k % 2, (k // 2) * 64:(k // 2) * 64 + 64],
                                             experts.slots[slot][2][:, k, half * 512:half * 512 + 512],
                                             start=(k == 0), stop=(k == 3), skip_group_check=True)
                m.then_inc(down_done, 1)

            def pair(q, first, second):
                pe.wait_ge(xg_copied, q * 2 + 2)
                up(0, *first)
                for c in y_copied:
                    pe.wait_ge(c, q * 2 + 1)
                pe.wait_ge(selT_copied, q + 1)
                scatter(0)
                pe.wait_ge(hm_ready, q * 2 + 1)
                turn()
                scatter(1).then_inc(scattered, 1)
                pe.wait_ge(hT_copied, q * 2 + 1)
                down(*first)
                pe.wait_ge(selw_built, q + 1)
                for t in range(TILES):
                    m = nc.tensor.transpose(ST[:, t, :], selw[:, t, :], ident[:, :])
                m.then_inc(sel_turned, 1)
                up(1, *second)
                pe.wait_ge(sel_built, q + 2)
                gather(0)
                pe.wait_ge(hm_ready, q * 2 + 2)
                pe.wait_ge(selT_copied, q + 2)
                turn()
                pe.wait_ge(xg_copied, q * 2 + 3)
                gather(1)
                pe.wait_ge(hT_copied, q * 2 + 2)
                for c in y_copied:
                    pe.wait_ge(c, q * 2 + 2)
                down(*second)

            pe.wait_ge(sel_built, 1)
            gather(0)
            gather(1, XG_first)
            pe.wait_ge(steps_ready, 1)
            rounds = steps(pe)
            with pe.Fori(0, rounds) as r:
                def turn_of(k, off):
                    return off % 3, r * experts.LOADS[off % 3] + k * 2 + (off // 3 + 1)

                with pe.Fori(0, E // 6) as k:
                    for a in range(3):
                        pair(r * PAIRS + k * 3 + a, turn_of(k, 2 * a), turn_of(k, 2 * a + 1))
                for a in range(E % 6 // 2):
                    pair(r * PAIRS + (E // 6 * 3 + a), turn_of(E // 6, 2 * a), turn_of(E // 6, 2 * a + 1))
            for c in y_copied:
                pe.wait_ge(c, rounds * E + 1)
            pe.wait_ge(selT_copied, rounds * PAIRS + 1)
            for t in range(TILES):
                scatter(t).then_inc(scattered, 1)

        def copy_y(eng_copy, u, half):
            return eng_copy(y[BLOCK * u:BLOCK * (u + 1), half, :], bank_Y[64 * half:64 * half + 64, :])

        @block.scalar
        def _(act):
            act.wait_ge(exp_asked, 1)
            nc.scalar.activation(small[:, 4, 0:2 * GROUPS], small[:, 3, 0:2 * GROUPS], ACT.Exp).then_inc(exp_done, 1)
            act.wait_ge(exp_asked, 2)
            nc.scalar.activation(small[:, 7, 2:4], small[:, 7, 0:2], ACT.Exp).then_inc(exp_done, 1)
            act.sem_inc(y_copied[0], 1)
            for part in range(2):
                act.wait_ge(gathered, part + 1)
                nc.scalar.copy(xg[:, 4 * part:4 * part + 4, :], (XG, XG_first)[part]).then_inc(xg_copied, 1)
            act.wait_ge(steps_ready, 1)
            rounds = steps(act)
            with act.Fori(0, rounds) as r:
                with act.Fori(0, PAIRS) as i:
                    q = r * PAIRS + i
                    for u in range(2):
                        act.wait_ge(up_done, q * 2 + (u + 1))
                        nc.scalar.activation(sil, H1, ACT.Silu).then_inc(silu_done, 1)
                        if u == 1:
                            for part in range(2):
                                act.wait_ge(gathered, q * 2 + (part + 3))
                                nc.scalar.copy(xg[:, 4 * part:4 * part + 4, :], XG).then_inc(xg_copied, 1)
                        act.wait_ge(down_done, q * 2 + (u + 1))
                        copy_y(nc.scalar.copy, u, 0).then_inc(y_copied[0], 1)

        @block.vector
        def _(dve):
            link = Chain(dve, dve_step)
            nc.vector.memset(selT, 0.0)
            nc.vector.memset(slots[:, :, ROUNDS * E:], -1000.0)
            nc.vector.memset(comb[:, :, ROUNDS * E:], 0.0)
            link(nc.vector.memset(y, 0.0))
            dve.sem_inc(y_copied[1], 1)
            dve.sem_inc(selT_copied, 1)
            lg = mem["lg"]
            dve.wait_ge(logits_done, 1)
            dve.wait_ge(rt_landed, 64)
            for t in range(TILES):
                link(nc.vector.tensor_tensor(lg[:, t, :], bank_H[:, t * 64:t * 64 + 36], rb[:, :], ALU.add))

            def bc(ap, n):
                return ap.unsqueeze(2).to_broadcast([P, TILES, n])

            def v(k, n):
                return small[:, k, 0:TILES * n].rearrange("p (t n) -> p t n", t=TILES)

            def first_max(vals, n, best, onehot, key):
                link(nc.vector.tensor_reduce(best, vals, AX.X, ALU.max))
                link(nc.vector.tensor_tensor(onehot, vals, bc(best, n), ALU.is_equal))
                link(nc.vector.tensor_tensor(onehot, onehot, order[:, 0:n].unsqueeze(1).to_broadcast([P, TILES, n]), ALU.mult))
                link(nc.vector.tensor_reduce(key, onehot, AX.X, ALU.max))
                link(nc.vector.tensor_tensor(onehot, onehot, bc(key, n), ALU.is_equal))

            gl, el = lg[:, :, 0:GROUPS], lg[:, :, GROUPS:]
            gmax, key, m1, m2, pg, w_a, w_b = (small[:, 5, 2 * i:2 * i + 2] for i in range(7))
            ohg, oh1, oh2 = v(0, GROUPS), v(1, E), v(2, E)
            first_max(gl, GROUPS, gmax, ohg, key)
            link(nc.vector.tensor_tensor(v(3, GROUPS), gl, bc(gmax, GROUPS), ALU.subtract))
            dve.sem_inc(exp_asked, 1)
            pen = v(6, E)
            link(nc.vector.tensor_copy(pen.rearrange("p t (g n) -> p t g n", g=GROUPS),
                                       ohg.unsqueeze(3).to_broadcast([P, TILES, GROUPS, PER_GROUP])))
            link(nc.vector.tensor_scalar(pen, pen, 1.0, BIG, ALU.subtract, ALU.mult))
            link(nc.vector.tensor_tensor(el, el, pen, ALU.add))
            first_max(el, E, m1, oh1, key)
            link(nc.vector.scalar_tensor_tensor(el, oh1, -2.0 * BIG, el, ALU.mult, ALU.add))
            first_max(el, E, m2, oh2, key)
            mask = mem["mask"]
            link(nc.vector.tensor_tensor(mask, oh1, oh2, ALU.add))
            dve.sem_inc(mask_ready, 1)
            link(nc.vector.tensor_tensor(small[:, 7, 0:2], m2, m1, ALU.subtract))
            dve.sem_inc(exp_asked, 1)

            def build(dst, pair, weighted):
                for t in range(TILES):
                    for u in range(2):
                        g = pair * 2 + u
                        place = slots[:, t, bass.ds(g, 1)]
                        m = nc.vector.tensor_scalar(dst[:, t, BLOCK * u:BLOCK * (u + 1)], iota[:, 0:BLOCK], place,
                                                    comb[:, t, bass.ds(g, 1)] if weighted else None, ALU.is_equal,
                                                    ALU.mult if weighted else ALU.bypass)
                return m

            dve.wait_ge(pos_done, 1)
            base = v(6, E)
            link(nc.vector.scalar_tensor_tensor(base, bank_T[:, 0:2 * E].rearrange("p (t n) -> p t n", t=2), 1000.0,
                                                mask, ALU.add, ALU.mult))
            link(nc.vector.tensor_scalar(slots[:, :, 0:E], base, 1000.0, None, ALU.subtract))
            build(sel, 0, False).then_inc(sel_built, 1)
            for k in range(1, ROUNDS):
                link(nc.vector.tensor_scalar(slots[:, :, k * E:(k + 1) * E], base, 1000.0 + BLOCK * k, None, ALU.subtract))
            full, rnd, more = (small[:, 5, c:c + 1] for c in (14, 15, 16))
            link(nc.vector.tensor_reduce(full, bank_T[:, 2 * E:3 * E], AX.X, ALU.max))
            link(nc.vector.tensor_scalar(rnd, full, float(BLOCK), 1.0, ALU.is_gt, ALU.add))
            for k in range(2, ROUNDS):
                link(nc.vector.tensor_scalar(more, full, float(BLOCK * k), None, ALU.is_gt))
                link(nc.vector.tensor_tensor(rnd, rnd, more, ALU.add))
            link(nc.vector.tensor_copy(nsteps[:, :], rnd))
            dve.sem_inc(steps_ready, 1)
            dve.wait_ge(exp_done, 1)
            link(nc.vector.tensor_reduce(pg, v(4, GROUPS), AX.X, ALU.add))
            dve.wait_ge(exp_done, 2)
            ex = small[:, 7, 2:4]
            link(nc.vector.tensor_scalar(w_a, ex, 1.0, None, ALU.add))
            link(nc.vector.tensor_tensor(w_a, w_a, pg, ALU.mult))
            link(nc.vector.reciprocal(w_b, w_a))
            link(nc.vector.tensor_tensor(w_a, w_b, ex, ALU.mult))
            link(nc.vector.tensor_tensor(oh1, oh1, bc(w_b, E), ALU.mult))
            link(nc.vector.tensor_tensor(oh2, oh2, bc(w_a, E), ALU.mult))
            for k in range(ROUNDS):
                link(nc.vector.tensor_tensor(comb[:, :, k * E:(k + 1) * E], oh1, oh2, ALU.add))
            build(selw, 0, True).then_inc(selw_built, 1)
            dve.wait_ge(gathered, 2)
            build(sel, 1, False).then_inc(sel_built, 1)
            rounds = steps(dve)
            with dve.Fori(0, rounds) as r:
                with dve.Fori(0, PAIRS) as i:
                    q = r * PAIRS + i
                    for u in range(2):
                        dve.wait_ge(silu_done, q * 2 + (u + 1))
                        nc.vector.tensor_tensor(hm, sil, H3, ALU.mult).then_inc(hm_ready, 1)
                        dve.wait_ge(turned, q * 2 + (u + 1))
                        nc.vector.tensor_copy(hTs, HT).then_inc(hT_copied, 1)
                        if u == 1:
                            dve.wait_ge(gathered, q * 2 + 4)
                            build(sel, q + 2, False).then_inc(sel_built, 1)
                        dve.wait_ge(down_done, q * 2 + (u + 1))
                        copy_y(nc.vector.tensor_copy, u, 1).then_inc(y_copied[1], 1)
                        if u == 0:
                            dve.wait_ge(sel_turned, q + 1)
                            nc.vector.tensor_copy(selT, ST).then_inc(selT_copied, 1)
                            build(selw, q + 1, True).then_inc(selw_built, 1)
            for t in range(TILES):
                dve.wait_ge(scattered, rounds * PAIRS + (t + 1))
                for half in range(2):
                    cols = slice(half * 512, half * 512 + 512)
                    moved = bank_acc[2 * t + half][:, :]
                    if gate2 is not None:
                        link(nc.vector.tensor_tensor(h[:, t, cols], moved, gate2[:, cols], ALU.mult))
                        moved = h[:, t, cols]
                    link(nc.vector.tensor_tensor(x[:, t, cols], moved, x[:, t, cols], ALU.add))
    stage.close()


def bucket_of(dist):
    import numpy as np
    exact = REL_BUCKETS // 2
    d = np.maximum(dist, 0)
    logd = np.log(np.maximum(d, 1).astype(np.float32) / np.float32(exact)) / np.float32(math.log(REL_MAX_DIST / exact))
    far = np.minimum(exact + (logd.astype(np.float32) * np.float32(REL_BUCKETS - exact)).astype(np.int32), REL_BUCKETS - 1)
    return np.where(d < exact, d, far)


def host_constants():
    import numpy as np
    f = np.float32
    c = {}
    c["ident"] = np.eye(P, dtype=f)
    c["tri"] = np.triu(np.ones((P, P), f), 1)
    c["ones"] = np.ones((P, P), f)
    c["iota"] = np.tile(np.arange(BLOCK, dtype=f), (P, 1))
    c["order"] = np.tile(np.arange(E, 0, -1, dtype=f), (P, 1))
    i = np.arange(P)
    same = (i[:, None] // CHUNK) == (i[None, :] // CHUNK)
    c["upto"] = ((i[:, None] <= i[None, :]) & same).astype(f)
    c["after"] = ((i[:, None] > i[None, :]) & same).astype(f)
    dist = 255 - np.arange(SKEW)
    hot = (bucket_of(dist)[None, :] == np.arange(REL_BUCKETS)[:, None])
    for name, ok in (("hot_window", (dist >= 0) & (dist < A_WINDOW)), ("hot_causal", dist >= 0)):
        c[name] = np.concatenate([hot & ok, ~ok[None]], 0).astype(f)
    j = np.arange(TOK)
    c["causal"] = np.where(P + i[:, None] - j[None, :] >= 0, 0.0, -BIG).astype(f)
    c["levels"] = np.stack([((i[:, None] // (2 * m)) == (i[None, :] // (2 * m))) & (i[:, None] % (2 * m) < m)
                            & (i[None, :] % (2 * m) >= m) for m in LEVELS] + [i[:, None] == i[None, :]], 1
                           ).astype(f).reshape(P, -1)
    half = ROPE_DIM // 2
    inv = (f(ROPE_THETA) ** (-np.arange(half, dtype=f) / f(half))).astype(f)
    ang = np.arange(TOK, dtype=f)[:, None] * inv[None, :]
    rope = np.concatenate([np.cos(ang), np.sin(ang)], 1).astype(f)
    c["rope"] = rope.reshape(TILES, P, ROPE_DIM).transpose(1, 0, 2).reshape(P, -1)
    c["rope_cmp"] = np.zeros((P, ROPE_DIM), f)
    c["rope_cmp"][:N_CMP] = rope[np.arange(N_CMP) * CMP_STRIDE]
    ok = (np.arange(N_CMP) * CMP_STRIDE + CMP_LEN - 1)[None, :] <= j[:, None]
    ok = ok.reshape(TILES, P, N_CMP).transpose(1, 0, 2)
    c["cmp_bias"] = np.where(ok, 0.0, -BIG).astype(f).reshape(P, -1)
    c["cmp_mask"] = ok.astype(f).reshape(P, -1)
    return c


def alloc_consts(nc):
    return {n: nc.alloc_sbuf_tensor(f"const_{n}", list(a.shape), F32) for n, a in host_constants().items() if "hot" not in n}


class Arena:

    def __init__(self, nc, words):
        self.t, self.words, self.at = nc.alloc_sbuf_tensor("arena", [P, words], F32), words, 0
        self.top = words

    def reserve(self, shape):
        self.top -= math.prod(shape)
        assert self.at <= self.top, (self.at, self.top)
        return self.view(shape, self.top, P)

    def take(self, shape, parts=P):
        self.at += math.prod(shape)
        assert self.at <= self.top, (self.at, self.top)
        return self.view(shape, self.at - math.prod(shape), parts)

    def view(self, shape, at, parts):
        ap = self.t[0:parts, at:at + math.prod(shape)]
        names = "abcd"[:len(shape)]
        if len(shape) > 1:
            ap = ap.rearrange(f"p ({' '.join(names)}) -> p {' '.join(names)}", **dict(zip(names, shape)))
        return ap


def col(w):
    return w.rearrange("(p c) -> p c", p=P)


MB = 512


class Modulation:

    STEPS = DC + 1
    LANDED = 32

    def __init__(self, nc, ccol, ada_w, ada_b, mod):
        self.nc, self.ccol, self.mod = nc, ccol, mod
        self.wv, self.b = ada_w.rearrange("(p c) n -> p c n", p=P), ada_b.unsqueeze(0)

    @staticmethod
    def slots(arena, n):
        return arena.take([n, DC, MB]), arena.take([n, MB], parts=1)

    def load(self, sp, slots, u, col, landed):
        cols = bass.ds(col, MB)
        sp.dma_start(slots[0][:, u], self.wv[:, :, cols]).then_inc(landed, 16)
        sp.dma_start(slots[1][:, u], self.b[:, cols]).then_inc(landed, 16)

    def accumulate(self, eng, slots, u, out, step, done):
        nc, wt = self.nc, slots[0][:, u]
        for k in range(DC):
            if k == 0:
                m = nc.vector.tensor_scalar(out, wt[:, 0, :], self.ccol[:, 0:1], None, ALU.mult)
            else:
                eng.wait_ge(step, done + k)
                m = nc.vector.scalar_tensor_tensor(out, wt[:, k, :], self.ccol[:, k:k + 1], out, ALU.mult, ALU.add)
            m.then_inc(step, 1)
        eng.wait_ge(step, done + DC)
        nc.vector.tensor_tensor(out[0:1, :], out[0:1, :], slots[1][:, u], ALU.add).then_inc(step, 1)

    def finisher(self, stage, blocks, banks, consts, to=None):
        return Finish(self, stage, blocks, banks, consts, to if to is not None else self.mod)


class Finish:

    def __init__(self, m, stage, blocks, banks, consts, to):
        self.m, self.blocks, self.banks, self.consts, self.to = m, blocks, banks, consts, to
        self.summed, self.copied = stage.sem("mod_summed"), stage.sem("mod_copied")

    def tensor(self, pe, added=None):
        nc = self.m.nc
        for n, j in enumerate(self.blocks):
            bank = self.banks[n % len(self.banks)]
            if added is not None:
                pe.wait_ge(added, Modulation.STEPS * (n + 1))
            if n >= len(self.banks):
                pe.wait_ge(self.copied, n - len(self.banks) + 1)
            nc.tensor.matmul(bank, self.consts["ones"][:, :], self.m.mod[:, j * MB:(j + 1) * MB], start=True,
                             stop=True).then_inc(self.summed, 1)

    def scalar(self, act):
        for n, j in enumerate(self.blocks):
            act.wait_ge(self.summed, n + 1)
            self.m.nc.scalar.copy(self.to[:, j * MB:(j + 1) * MB], self.banks[n % len(self.banks)]).then_inc(self.copied, 1)


class NormWeight:

    def __init__(self, stage, tile, sums):
        self.tile, self.sums, self.landed, self.n = tile, sums, stage.sem("norm_w"), 0

    def fetch(self, sp, w_row):
        self.n += 1
        sp.dma_start(self.tile, w_row.partition_broadcast(P)).then_inc(self.landed, 16)

    def wait(self, eng):
        eng.wait_ge(self.landed, 16 * self.n)


def start_stage(nc, c_vec, ccol, m, blocks, early, late, hot_dram, rel_bias, skewed, norm_w, first_norm, arena, banks, consts):
    stage = Stage(nc, "start")
    mark = arena.at
    SLOTS = 3
    slots = m.slots(arena, SLOTS)
    hot, rows = arena.take([2, SKEW], parts=REL_BUCKETS + 1), arena.take([2, SKEW], parts=HEADS)
    rb = arena.take([HEADS], parts=REL_BUCKETS + 1)
    landed, step, c_landed, c_ready = [stage.sem(f"w{u}") for u in range(SLOTS)], stage.sem("dve"), stage.sem("c"), stage.sem("silu")
    early_landed, late_landed, masked, made, copied = (stage.sem(n) for n in ("early", "late", "masked", "made", "copied"))
    fin = m.finisher(stage, blocks, banks[0:6], consts)
    with nc.Block() as block:
        @block.gpsimd
        def _(pool):
            nc.gpsimd.memset(rb[REL_BUCKETS:REL_BUCKETS + 1, :], -BIG).then_inc(masked, 1)

        @block.sync
        def _(sp):
            sp.dma_start(ccol, col(c_vec)).then_inc(c_landed, 16)
            for n, j in enumerate(blocks):
                if n >= SLOTS:
                    sp.wait_ge(step, m.STEPS * (n - SLOTS + 1))
                m.load(sp, slots, n % SLOTS, j * MB, landed[n % SLOTS])
                if n == 0:
                    for dst, src in early:
                        sp.dma_start(dst, src).then_inc(early_landed, 16)
                    sp.dma_start(rb[0:REL_BUCKETS, :], rel_bias).then_inc(early_landed, 16)
                    for i in range(2):
                        sp.dma_start(hot[:, i], hot_dram[i]).then_inc(early_landed, 16)
            for dst, src in late:
                sp.dma_start(dst, src).then_inc(late_landed, 16)
            norm_w.fetch(sp, first_norm)
            sp.wait_ge(copied, 1)
            skewed.store(sp, rows)
            sp.wait_ge(late_landed, 16 * len(late))
            skewed.wait_stored(sp)

        @block.tensor
        def _(pe):
            pe.wait_ge(early_landed, 16 * (len(early) + 3))
            pe.wait_ge(masked, 1)
            for i in range(2):
                r = nc.tensor.matmul(banks[6 + i][0:HEADS, 0:SKEW], rb, hot[:, i], start=True, stop=True)
            r.then_inc(made, 1)
            fin.tensor(pe, step)

        @block.vector
        def _(dve):
            dve.wait_ge(c_ready, 1)
            for n, j in enumerate(blocks):
                dve.wait_ge(landed[n % SLOTS], m.LANDED * (n // SLOTS + 1))
                m.accumulate(dve, slots, n % SLOTS, m.mod[:, j * MB:(j + 1) * MB], step, m.STEPS * n)

        @block.scalar
        def _(act):
            act.wait_ge(c_landed, 16)
            nc.scalar.activation(ccol, ccol, ACT.Silu).then_inc(c_ready, 1)
            act.wait_ge(made, 1)
            nc.scalar.copy(rows[:, 0], banks[6][0:HEADS, 0:SKEW])
            nc.scalar.copy(rows[:, 1], banks[7][0:HEADS, 0:SKEW]).then_inc(copied, 1)
            fin.scalar(act)
    stage.close()
    arena.at = mark


class SkewedBias:

    def __init__(self, stage, scratch):
        self.scratch, self.stored, self.landed = scratch, stage.sem("skew_stored"), stage.sem("bias_landed")

    def store(self, sp, rows):
        for i in range(2):
            sp.dma_start(self.scratch[i], rows[:, i].unsqueeze(1).to_broadcast([HEADS, P, SKEW])).then_inc(self.stored, 16)

    def wait_stored(self, sp):
        sp.wait_ge(self.stored, 32)

    def load(self, sp, i, out):
        src = bass.AP(self.scratch.tensor, i * HEADS * P * SKEW + P - 1, [[SKEW - 1, P], [P * SKEW, HEADS], [1, TOK]])
        sp.dma_start(out, src).then_inc(self.landed, 16)

    def wait(self, eng, i):
        eng.wait_ge(self.landed, 16 * (i + 1))


def norm_stage(nc, tag, x, out, norm_w, scale, shift, outT=None, ident=None, banks=None, store=None,
               loads=None):
    stage = Stage(nc, tag)
    sem = stage.sem
    w, ss, rs = norm_w.tile, norm_w.sums[:, 0], norm_w.sums[:, 1]
    squared, root_asked, root_done, step, ready, turned = (sem(n) for n in ("sq", "ask", "root", "dve", "ready", "turned"))
    kept = sem("kept")
    HC = DC // 2
    with nc.Block() as block:
        @block.scalar
        def _(act):
            for t in range(TILES):
                nc.scalar.activation(out[:, t, :], x[:, t, :], ACT.Square, accum_out=ss[:, t:t + 1]).then_inc(squared, 1)
            act.wait_ge(root_asked, 1)
            nc.scalar.activation(rs, ss, ACT.Sqrt).then_inc(root_done, 1)
            if outT is not None:
                for n in range(2 * TILES):
                    t, half = n // 2, n % 2
                    if n != 2 * TILES - 2:
                        act.wait_ge(turned, n + 1)
                        nc.scalar.copy(outT[:, HC * half:HC * half + HC, t * P:(t + 1) * P], banks[n].rearrange("p (c n) -> p c n", c=HC))

        @block.vector
        def _(dve):
            link = Chain(dve, step)
            norm_w.wait(dve)
            if scale is not None:
                link(nc.vector.scalar_tensor_tensor(w, scale, 1.0, w, ALU.add, ALU.mult))
            dve.wait_ge(squared, TILES)
            link(nc.vector.tensor_scalar(ss, ss, 1.0 / D, EPS, ALU.mult, ALU.add))
            dve.sem_inc(root_asked, 1)
            dve.wait_ge(root_done, 1)
            link(nc.vector.reciprocal(rs, rs))
            for t in range(TILES):
                for half in range(2):
                    cols = slice(half * D // 2, (half + 1) * D // 2)
                    link(nc.vector.scalar_tensor_tensor(out[:, t, cols], x[:, t, cols], rs[:, t:t + 1], w[:, cols], ALU.mult, ALU.mult))
                    if shift is not None:
                        link(nc.vector.tensor_tensor(out[:, t, cols], out[:, t, cols], shift[:, cols], ALU.add))
                    dve.sem_inc(ready, 1)
            if outT is not None:
                n = 2 * TILES - 2
                dve.wait_ge(turned, n + 1)
                nc.vector.tensor_copy(outT[:, 0:HC, (TILES - 1) * P:], banks[n].rearrange("p (c n) -> p c n", c=HC))

        if outT is not None:
            @block.tensor
            def _(pe):
                for n in range(2 * TILES):
                    t, half = n // 2, n % 2
                    pe.wait_ge(ready, n + 1)
                    for c in range(HC):
                        m = nc.tensor.transpose(banks[n][:, c * P:(c + 1) * P], out[:, t, (half * HC + c) * P:(half * HC + c + 1) * P],
                                                ident[:, :])
                    m.then_inc(turned, 1)

        @block.sync
        def _(sp):
            if loads is not None:
                loads(sp)
            if store is not None:
                for t in range(TILES):
                    sp.wait_ge(ready, 2 * (t + 1))
                    sp.dma_start(store[:, t, :], out[:, t, :]).then_inc(kept, 16)
                sp.wait_ge(kept, 16 * TILES)
    stage.close()


def turn_stage(nc, tag, jobs, ident, banks):
    stage = Stage(nc, tag)
    sem = stage.sem
    pairs = [(src, w, i, min(2, n - i), dst) for src, w, n, dst in jobs for i in range(0, n, 2)]
    turned, copied = sem("turned"), [sem("copied_dve"), sem("copied_act")]
    with nc.Block() as block:
        @block.tensor
        def _(pe):
            for j, (src, w, i, m, dst) in enumerate(pairs):
                if j >= 8:
                    pe.wait_ge(copied[j % 2], (j - 8) // 2 + 1)
                for k in range(m):
                    for t in range(TILES):
                        last = nc.tensor.transpose(banks[j % 8][0:w, k * TOK + t * P:k * TOK + (t + 1) * P],
                                                   src[:, t, (i + k) * w:(i + k + 1) * w], ident[:, :])
                last.then_inc(turned, 1)

        def out(j):
            src, w, i, m, dst = pairs[j]
            return dst[:, i:i + m, :], banks[j % 8][0:w, 0:m * TOK].rearrange("p (m n) -> p m n", m=m)

        @block.vector
        def _(dve):
            for j in range(0, len(pairs), 2):
                dve.wait_ge(turned, j + 1)
                nc.vector.tensor_copy(*out(j)).then_inc(copied[0], 1)

        @block.scalar
        def _(act):
            for j in range(1, len(pairs), 2):
                act.wait_ge(turned, j + 1)
                nc.scalar.copy(*out(j)).then_inc(copied[1], 1)
    stage.close()


def project_stage(nc, tag, inT, kc, w, width, out, arena, banks, gate=None, add=False, ahead=None, tmp=None, side=None):
    stage = Stage(nc, tag)
    sem = stage.sem
    mark = arena.at
    wt = arena.take([2, kc, width])
    if gate is not None and add and tmp is None:
        tmp = arena.take([2, width])
    N = w.shape[1] // width
    landed, row_done, copied, step = [sem("w0"), sem("w1")], sem("row"), [sem("copied0"), sem("copied1")], sem("dve")
    plain = gate is None and not add
    if side:
        modulation, side_col = side
        side_slots = modulation.slots(arena, 2)
        side_landed, side_step = [sem("side0"), sem("side1")], sem("side_step")
        STEPS, LANDED = modulation.STEPS, modulation.LANDED
    wv = w.rearrange("(c p) (i n) -> i p c n", p=P, n=width)

    def both(eng, first, body):
        if N // 2 > first:
            with eng.Fori(first, N // 2) as i:
                for u in range(2):
                    body(i * 2 + u, i, u)
        if N % 2 and N // 2 >= first:
            body(N - 1, N // 2, 0)

    with nc.Block() as block:
        @block.sync
        def _(sp):
            def load(b, i, u):
                src = w[:, bass.ds(b * width, width)] if not isinstance(b, int) else w[:, b * width:(b + 1) * width]
                sp.dma_start(wt[:, u], src.rearrange("(c p) n -> p c n", p=P)).then_inc(landed[u], 16)
                if side:
                    if not (isinstance(b, int) and b < 2):
                        sp.wait_ge(side_step, i * (2 * STEPS) + STEPS * (u - 1))
                    modulation.load(sp, side_slots, u, b * MB + side_col, side_landed[u])

            def later(b, i, u):
                sp.wait_ge(row_done, i * 2 + (u - 1))
                load(b, i, u)
            for u in range(min(2, N)):
                load(u, 0, u)
            both(sp, 1, later)
            if ahead:
                ahead(sp)

        @block.tensor
        def _(pe):
            def body(b, i, u):
                pe.wait_ge(landed[u], i * 16 + 16)
                for t in range(TILES):
                    pe.wait_ge(copied[t], i * 2 + (u + 1))
                    for k in range(kc):
                        m = nc.tensor.matmul(banks[2 * u + t][:, 0:width], inT[:, k, t * P:(t + 1) * P], wt[:, u, k, :],
                                             start=(k == 0), stop=(k == kc - 1))
                m.then_inc(row_done, 1)
            both(pe, 0, body)

        def at(ap, t, b):
            return ap[:, t, bass.ds(b * width, width)] if not isinstance(b, int) else ap[:, t, b * width:(b + 1) * width]

        @block.scalar
        def _(act):
            if plain:
                act.sem_inc(copied[1], 2)

                def body(b, i, u):
                    act.wait_ge(row_done, i * 2 + (u + 1))
                    nc.scalar.copy(at(out, 1, b), banks[2 * u + 1][:, 0:width]).then_inc(copied[1], 1)
                both(act, 0, body)

        @block.vector
        def _(dve):
            dve.sem_inc(copied[0], 2)
            if plain:
                def body(b, i, u):
                    dve.wait_ge(row_done, i * 2 + (u + 1))
                    nc.vector.tensor_copy(at(out, 0, b), banks[2 * u][:, 0:width]).then_inc(copied[0], 1)
                    if side:
                        dve.wait_ge(side_landed[u], i * LANDED + LANDED)
                        modulation.accumulate(dve, side_slots, u, modulation.mod[:, bass.ds(b * MB + side_col, MB)], side_step,
                                              i * (2 * STEPS) + STEPS * u)
            else:
                dve.sem_inc(copied[1], 2)

                def body(b, i, u):
                    dve.wait_ge(row_done, i * 2 + (u + 1))
                    for t in range(TILES):
                        o, src = at(out, t, b), banks[2 * u + t][:, 0:width]
                        if gate is not None and not add:
                            nc.vector.tensor_tensor(o, src, at(gate, t, b), ALU.mult).then_inc(copied[t], 1)
                        elif gate is None:
                            nc.vector.tensor_tensor(o, src, o, ALU.add).then_inc(copied[t], 1)
                        else:
                            nc.vector.tensor_tensor(tmp[:, t], src, at(gate, t, b), ALU.mult).then_inc(step, 1)
                            dve.wait_ge(step, i * 4 + (u * 2 + t + 1))
                            nc.vector.tensor_tensor(o, tmp[:, t], o, ALU.add).then_inc(copied[t], 1)
            both(dve, 0, body)
    stage.close()
    arena.at = mark


def head_norm_stage(nc, tag, jobs, arena, finish=None, loads=None):
    stage = Stage(nc, tag)
    sem = stage.sem
    mark = arena.at
    most = max(n * w for _, n, w, _ in jobs)
    total = sum(n for _, n, _, _ in jobs) * TILES
    sq, ss, rs = arena.take([TILES, most]), arena.take([total]), arena.take([total])
    ws = [arena.take([w]) for _, _, w, _ in jobs]
    landed, root_asked, root_done, step = sem("w"), sem("ask"), sem("root"), sem("dve")
    fin = finish and finish(stage)
    with nc.Block() as block:
        @block.sync
        def _(sp):
            for (_, _, _, w_row), w in zip(jobs, ws):
                sp.dma_start(w, w_row.partition_broadcast(P)).then_inc(landed, 16)
            if loads:
                loads(sp)

        @block.tensor
        def _(pe):
            if fin:
                fin.tensor(pe)

        @block.scalar
        def _(act):
            act.wait_ge(root_asked, 1)
            nc.scalar.activation(rs, ss, ACT.Sqrt).then_inc(root_done, 1)
            if fin:
                fin.scalar(act)

        @block.vector
        def _(dve):
            link = Chain(dve, step)
            at, places = 0, []
            for rows, n, w, _ in jobs:
                for t in range(TILES):
                    r = rows[:, t, :]
                    link(nc.vector.tensor_tensor(sq[:, t, 0:n * w], r, r, ALU.mult))
                    link(nc.vector.tensor_reduce(ss[:, at:at + n], sq[:, t, 0:n * w].rearrange("p (n w) -> p n w", w=w),
                                                 AX.X, ALU.add))
                    link(nc.vector.tensor_scalar(ss[:, at:at + n], ss[:, at:at + n], 1.0 / w, EPS, ALU.mult, ALU.add))
                    places.append(at)
                    at += n
            dve.sem_inc(root_asked, 1)
            dve.wait_ge(root_done, 1)
            link(nc.vector.reciprocal(rs, rs))
            dve.wait_ge(landed, 16 * len(jobs))
            for k, (rows, n, w, _) in enumerate(jobs):
                for t in range(TILES):
                    r = rows[:, t, :].rearrange("p (n w) -> p n w", w=w)
                    a = places[k * TILES + t]
                    link(nc.vector.tensor_tensor(r, r, rs[:, a:a + n].unsqueeze(2).to_broadcast([P, n, w]), ALU.mult))
                    link(nc.vector.tensor_tensor(r, r, ws[k].unsqueeze(1).to_broadcast([P, n, w]), ALU.mult))
    stage.close()
    arena.at = mark


def attend_stage(nc, tag, jobs, ident, arena, psum, side=None, bias_wait=None):
    stage = Stage(nc, tag)
    sem = stage.sem
    mark = arena.at
    G = HEADS // 2
    units = [(job, t, slice(G * g, G * g + G), job.get("keys") or (t + 1) * P)
             for job in jobs for t in range(TILES) for g in range(2)]
    most = max(nk for *_, nk in units)
    L, PT = arena.take([2, G, most]), arena.take([2, 2 * G, P])
    mx, sm, es, tmp = arena.take([3, G]), arena.take([3, G]), arena.take([3, G]), arena.take([G * max(j["hd"] for j in jobs)])
    names = ("scores", "scaled", "maxed", "probs", "turned", "pt", "outs", "written", "dve", "act")
    scores, scaled, maxed, probs, turned, pt_copied, outs, written, step, astep = (sem(n) for n in names)

    if side:
        modulation, blocks = side
        side_slots = modulation.slots(arena, 2)
        side_landed, side_step = [sem("side0"), sem("side1")], sem("side_step")

    def S(n, nk):
        return psum[:, 1024 * (n % 2):1024 * (n % 2 + 1)].rearrange("p (h n) -> p h n", h=G)[:, :, 0:nk]

    T = psum[:, 2048:3072].rearrange("p (u n) -> p u n", n=P)

    def O(n, hd):
        return psum[:, 3072 + 512 * (n % 2):3072 + 512 * (n % 2) + G * hd]

    with nc.Block() as block:
        @block.tensor
        def _(pe):
            for n in range(len(units) + 2):
                if n < len(units):
                    job, t, hs, nk = units[n]
                    if n >= 2:
                        pe.wait_ge(scaled, n - 1)
                    for i, h in enumerate(range(hs.start, hs.stop)):
                        m = nc.tensor.matmul(S(n, nk)[:, i, :], job["qT"][:, h, t * P:(t + 1) * P],
                                             job["kT"][:, job["kv_of"](h), 0:nk], start=True, stop=True)
                    m.then_inc(scores, 1)
                if 0 <= n - 1 < len(units):
                    job, t, hs, nk = units[n - 1]
                    nkt, w = -(-nk // P), min(P, nk)
                    pe.wait_ge(probs, n)
                    if n >= 2:
                        pe.wait_ge(pt_copied, n - 1)
                    for i in range(G):
                        for kt in range(nkt):
                            m = nc.tensor.transpose(T[0:w, i * nkt + kt, :], L[:, (n - 1) % 2, i, kt * P:kt * P + w], ident[:, :])
                    m.then_inc(turned, 1)
                if n >= 2:
                    job, t, hs, nk = units[n - 2]
                    hd, nkt, w = job["hd"], -(-nk // P), min(P, nk)
                    pe.wait_ge(pt_copied, n - 1)
                    if n >= 4:
                        pe.wait_ge(written, n - 3)
                    for i, h in enumerate(range(hs.start, hs.stop)):
                        for kt in range(nkt):
                            m = nc.tensor.matmul(O(n - 2, hd)[:, i * hd:(i + 1) * hd], PT[0:w, (n - 2) % 2, i * nkt + kt, :],
                                                 job["v"](kt, job["kv_of"](h)), start=(kt == 0), stop=(kt == nkt - 1))
                    m.then_inc(outs, 1)

        @block.scalar
        def _(act):
            for n in range(len(units) + 1):
                if n < len(units):
                    job, t, hs, nk = units[n]
                    act.wait_ge(maxed, n + 1)
                    for i in range(G):
                        m = nc.scalar.activation(L[:, n % 2, i, 0:nk], L[:, n % 2, i, 0:nk], ACT.Exp, bias=mx[:, n % 3, i:i + 1],
                                                 accum_out=sm[:, n % 3, i:i + 1])
                    if job.get("sinks") is not None:
                        m = nc.scalar.activation(es[:, n % 3], es[:, n % 3], ACT.Exp)
                    m.then_inc(probs, 1)
                if n:
                    job, t, hs, nk = units[n - 1]
                    k, w = G * -(-nk // P), min(P, nk)
                    act.wait_ge(turned, n)
                    if n >= 3:
                        act.wait_ge(outs, n - 2)
                    nc.scalar.copy(PT[0:w, (n - 1) % 2, 0:k, :], T[0:w, 0:k, :]).then_inc(pt_copied, 1)

        @block.vector
        def _(dve):
            link = Chain(dve, step)
            if bias_wait:
                bias_wait(dve)
            for n in range(len(units) + 2):
                if n < len(units):
                    job, t, hs, nk = units[n]
                    u = n % 2
                    dve.wait_ge(scores, n + 1)
                    if n >= 2:
                        dve.wait_ge(turned, n - 1)
                    nc.vector.scalar_tensor_tensor(L[:, u, :, 0:nk], S(n, nk), job["scale"], job["bias"](t, hs, nk),
                                                   ALU.mult, ALU.add).then_inc(scaled, 1)
                    dve.wait_ge(scaled, n + 1)
                    if job.get("sinks") is None:
                        nc.vector.tensor_reduce(mx[:, n % 3], L[:, u, :, 0:nk], AX.X, ALU.max, negate=True).then_inc(maxed, 1)
                    else:
                        link(nc.vector.tensor_reduce(mx[:, n % 3], L[:, u, :, 0:nk], AX.X, ALU.max))
                        link(nc.vector.tensor_tensor(mx[:, n % 3], mx[:, n % 3], job["sinks"][:, hs], ALU.max))
                        link(nc.vector.tensor_tensor(es[:, n % 3], job["sinks"][:, hs], mx[:, n % 3], ALU.subtract))
                        nc.vector.tensor_scalar(mx[:, n % 3], mx[:, n % 3], -1.0, None, ALU.mult).then_inc(maxed, 1)
                if n >= 2:
                    job, t, hs, nk = units[n - 2]
                    u, hd = n % 2, job["hd"]
                    dve.wait_ge(probs, n - 1)
                    dve.wait_ge(outs, n - 1)
                    if job.get("sinks") is not None:
                        link(nc.vector.tensor_tensor(sm[:, (n - 2) % 3], sm[:, (n - 2) % 3], es[:, (n - 2) % 3], ALU.add))
                    link(nc.vector.reciprocal(sm[:, (n - 2) % 3], sm[:, (n - 2) % 3]))
                    for f in job.get("factors", ()):
                        link(nc.vector.tensor_tensor(sm[:, (n - 2) % 3], sm[:, (n - 2) % 3], f(t, hs), ALU.mult))
                    out = job["out"][:, t, hs.start * hd:hs.stop * hd].rearrange("p (h w) -> p h w", h=G)
                    dst = tmp[:, 0:G * hd].rearrange("p (h w) -> p h w", h=G) if job.get("add") else out
                    nc.vector.tensor_tensor(dst, O(n - 2, hd).rearrange("p (h w) -> p h w", h=G),
                                            sm[:, (n - 2) % 3].unsqueeze(2).to_broadcast([P, G, hd]), ALU.mult).then_inc(written, 1)
                    dve.wait_ge(written, n - 1)
                    if job.get("add"):
                        link(nc.vector.tensor_tensor(out, out, dst, ALU.add))
                if side and n < len(blocks):
                    dve.wait_ge(side_landed[n % 2], modulation.LANDED * (n // 2 + 1))
                    modulation.accumulate(dve, side_slots, n % 2, modulation.mod[:, blocks[n] * MB:(blocks[n] + 1) * MB], side_step,
                                          modulation.STEPS * n)

        if side:
            @block.sync
            def _(sp):
                for n, j in enumerate(blocks):
                    if n >= 2:
                        sp.wait_ge(side_step, modulation.STEPS * (n - 1))
                    modulation.load(sp, side_slots, n % 2, j * MB, side_landed[n % 2])
    stage.close()
    arena.at = mark


GLA_HEADS, GLA_K, GLA_V, GLA_RANK = 4, 64, 128, 16
HG_HEADS, HG_K, HG_V = 4, 128, 128


def decay_stage(nc, tag, abT, gate_up, gate_bias, g, consts, arena, banks):
    stage = Stage(nc, tag)
    sem = stage.sem
    mark = arena.at
    W = GLA_HEADS * GLA_K
    up, brow = arena.take([W], parts=GLA_RANK), arena.take([W], parts=1)
    z, e = arena.take([TILES, W]), arena.take([TILES, W])
    landed, made, absolute, logged, step, astep = (sem(n) for n in ("w", "z", "abs", "log", "dve", "act"))
    with nc.Block() as block:
        @block.sync
        def _(sp):
            sp.dma_start(up, gate_up).then_inc(landed, 16)
            sp.dma_start(brow, gate_bias.unsqueeze(0)).then_inc(landed, 16)

        @block.tensor
        def _(pe):
            pe.wait_ge(landed, 32)
            for t in range(TILES):
                nc.tensor.matmul(banks[0][:, t * W:(t + 1) * W], abT[:, 0, t * P:(t + 1) * P], up, start=True, stop=False)
                m = nc.tensor.matmul(banks[0][:, t * W:(t + 1) * W], consts["ones"][0:1, :], brow, start=False, stop=True)
            m.then_inc(made, 1)

        @block.scalar
        def _(act):
            link = Chain(act, astep)
            act.wait_ge(absolute, 1)
            link(nc.scalar.activation(e, e, ACT.Exp, scale=-1.0))
            nc.scalar.activation(e, e, ACT.Ln, bias=1.0).then_inc(logged, 1)

        @block.vector
        def _(dve):
            link = Chain(dve, step)
            dve.wait_ge(made, 1)
            link(nc.vector.tensor_copy(z, banks[0][:, 0:TILES * W].rearrange("p (t n) -> p t n", t=TILES)))
            link(nc.vector.scalar_tensor_tensor(e, z, -1.0, z, ALU.mult, ALU.max))
            dve.sem_inc(absolute, 1)
            link(nc.vector.tensor_scalar(z, z, 0.0, None, ALU.min))
            dve.wait_ge(logged, 1)
            link(nc.vector.tensor_tensor(z, z, e, ALU.subtract))
            link(nc.vector.tensor_scalar(g, z, 1.0 / 16.0, None, ALU.mult))
    stage.close()
    arena.at = mark


def gla_stage(nc, tag, g, qT, kT, k, v, out, consts, arena, psum, banks):
    stage = Stage(nc, tag)
    sem = stage.sem
    mark = arena.at
    FC = GLA_HEADS * GLA_K // P
    W = GLA_HEADS * GLA_K
    eb, ei = arena.take([FC, TOK]), arena.take([FC, TOK])
    er = arena.take([TILES, W])
    AT = arena.take([2, 4, P])
    St = arena.take([CHUNKS - 1, FC, GLA_V])
    sums, exps, decayed, attn, masked, upd, states, outs, step = (
        sem(n) for n in ("sums", "exps", "decayed", "attn", "masked", "upd", "states", "outs", "dve"))
    Bs, Rs = banks[0][:, :].rearrange("p (f n) -> p f n", f=FC), banks[1][:, :].rearrange("p (t n) -> p t n", t=TILES)

    def U(c, rows, f):
        at = (c // 2) * FC * GLA_V + f * GLA_V
        return banks[4 + c % 2][rows, at:at + GLA_V]

    with nc.Block() as block:
        @block.tensor
        def _(pe):
            for f in range(FC):
                for t in range(TILES):
                    nc.tensor.matmul(Bs[:, f, t * P:(t + 1) * P], g[:, t, f * P:(f + 1) * P], consts["upto"][:, :], start=True, stop=True)
            for t in range(TILES):
                m = nc.tensor.matmul(Rs[:, t, :], consts["after"][:, :], g[:, t, :], start=True, stop=True)
            m.then_inc(sums, 1)
            pe.wait_ge(decayed, 1)
            for h in range(GLA_HEADS):
                rows = slice(64 * (h % 2), 64 * (h % 2) + 64)
                for t in range(TILES):
                    n = (h // 2) * TILES + t
                    m = nc.tensor.matmul(banks[2 + h % 2][:, n * P:(n + 1) * P], ei[rows, h // 2, t * P:(t + 1) * P],
                                         eb[rows, h // 2, t * P:(t + 1) * P], start=True, stop=True)
            m.then_inc(attn, 1)
            for c in range(CHUNKS - 1):
                rows, t = slice(64 * (c % 2), 64 * (c % 2) + 64), c // 2
                for h in range(GLA_HEADS):
                    m = nc.tensor.matmul(U(c, slice(64 * (h % 2), 64 * (h % 2) + 64), h // 2), er[rows, t, h * GLA_K:(h + 1) * GLA_K],
                                         v[rows, t, h * GLA_V:(h + 1) * GLA_V], start=True, stop=True, skip_group_check=True)
            m.then_inc(upd, 1)
            pe.wait_ge(masked, 1)
            pe.wait_ge(states, 1)
            for h in range(GLA_HEADS):
                rows = slice(64 * (h % 2), 64 * (h % 2) + 64)
                for t in range(TILES):
                    n = (h // 2) * TILES + t
                    o = banks[6 + h % 2][:, n * P:(n + 1) * P]
                    m = nc.tensor.matmul(o, AT[:, h % 2, n, :], v[:, t, h * GLA_V:(h + 1) * GLA_V], start=True, stop=False,
                                         skip_group_check=True)
                    for c in (2 * t, 2 * t + 1):
                        if c:
                            half = slice(64 * (c % 2), 64 * (c % 2) + 64)
                            m = nc.tensor.matmul(o[half, :], eb[rows, h // 2, c * CHUNK:(c + 1) * CHUNK], St[rows, c - 1, h // 2, :],
                                                 start=False, stop=True, skip_group_check=True)
            m.then_inc(outs, 1)

        dec = arena.take([FC, CHUNKS])

        @block.scalar
        def _(act):
            act.wait_ge(sums, 1)
            nc.scalar.activation(eb, Bs, ACT.Exp)
            nc.scalar.activation(ei, Bs, ACT.Exp, scale=-1.0)
            nc.scalar.activation(er, Rs, ACT.Exp).then_inc(exps, 1)

        @block.vector
        def _(dve):
            link = Chain(dve, step)
            dve.wait_ge(exps, 1)
            link(nc.vector.tensor_copy(dec, eb.rearrange("p f (c n) -> p f c n", n=CHUNK)[:, :, :, CHUNK - 1]))
            link(nc.vector.scalar_tensor_tensor(eb, qT, GLA_K ** -0.5, eb, ALU.mult, ALU.mult))
            link(nc.vector.tensor_tensor(ei, kT, ei, ALU.mult))
            link(nc.vector.tensor_tensor(er, k, er, ALU.mult))
            dve.sem_inc(decayed, 1)
            dve.wait_ge(attn, 1)
            for par in range(2):
                link(nc.vector.tensor_tensor(AT[:, par], banks[2 + par][:, :].rearrange("p (n k) -> p n k", n=4),
                                             consts["upto"][:, :].unsqueeze(1).to_broadcast([P, 4, P]), ALU.mult))
            dve.sem_inc(masked, 1)
            dve.wait_ge(upd, 1)
            for c in range(CHUNKS - 1):
                for f in range(FC):
                    if c == 0:
                        link(nc.vector.tensor_copy(St[:, 0, f, :], U(c, slice(0, P), f)))
                    else:
                        link(nc.vector.scalar_tensor_tensor(St[:, c, f, :], St[:, c - 1, f, :], dec[:, f, c:c + 1],
                                                            U(c, slice(0, P), f), ALU.mult, ALU.add))
            dve.sem_inc(states, 1)
            dve.wait_ge(outs, 1)
            o5 = out.rearrange("p t (h q v) -> p q h t v", q=2, v=GLA_V)
            for par in range(2):
                for t in range(TILES):
                    link(nc.vector.tensor_copy(o5[:, par, :, t, :], banks[6 + par][:, :].rearrange("p (h t v) -> p h t v", h=2, t=2)[:, :, t, :]))
    stage.close()
    arena.at = mark


def forget_stage(nc, tag, lb_logits, z, f, k, g, arena):
    stage = Stage(nc, tag)
    sem = stage.sem
    mark = arena.at
    W = HG_HEADS * HG_K
    l, mx = arena.take([2, W]), arena.take([W])
    landed, sig, asked, exped, made, step, astep = (sem(n) for n in ("l", "sig", "asked", "exp", "made", "dve", "act"))
    with nc.Block() as block:
        @block.sync
        def _(sp):
            for i in range(2):
                sp.dma_start(l[:, i], lb_logits[i].partition_broadcast(P)).then_inc(landed, 16)

        @block.scalar
        def _(act):
            nc.scalar.activation(f, z, ACT.Sigmoid).then_inc(sig, 1)
            act.wait_ge(asked, 1)
            nc.scalar.activation(l, l, ACT.Exp).then_inc(exped, 1)
            act.wait_ge(made, 1)
            nc.scalar.activation(g, f, ACT.Ln)

        @block.vector
        def _(dve):
            link = Chain(dve, step)
            dve.wait_ge(landed, 32)
            link(nc.vector.tensor_tensor(mx, l[:, 0], l[:, 1], ALU.max))
            link(nc.vector.tensor_tensor(l, l, mx.unsqueeze(1).to_broadcast([P, 2, W]), ALU.subtract))
            dve.sem_inc(asked, 1)
            dve.wait_ge(exped, 1)
            link(nc.vector.tensor_tensor(mx, l[:, 0], l[:, 1], ALU.add))
            link(nc.vector.reciprocal(mx, mx))
            link(nc.vector.tensor_tensor(l[:, 0], l[:, 0], mx, ALU.mult))
            link(nc.vector.tensor_scalar(l[:, 1], l[:, 0], -1.0, 1.0, ALU.mult, ALU.add))
            dve.wait_ge(sig, 1)
            link(nc.vector.tensor_tensor(f, f, l[:, 1].unsqueeze(1).to_broadcast([P, TILES, W]), ALU.mult))
            link(nc.vector.tensor_tensor(f, f, l[:, 0].unsqueeze(1).to_broadcast([P, TILES, W]), ALU.add))
            dve.sem_inc(made, 1)
            link(nc.vector.tensor_scalar(k, f, -1.0, 1.0, ALU.mult, ALU.add))
    stage.close()
    arena.at = mark


def hgrn_stage(nc, tag, g, qT, kT, k, v, out, consts, arena, banks):
    stage = Stage(nc, tag)
    sem = stage.sem
    mark = arena.at
    H, W = HG_HEADS, HG_HEADS * HG_K
    U = H * TILES
    b, eb, er = arena.take([H, TOK]), arena.take([H, TOK]), arena.take([TILES, W])
    ex, ql, kl = arena.take([H * TOK]), arena.take([H * TOK]), arena.take([H * TOK])
    A, tmp = arena.take([U, P]), arena.take([U, P])
    St, dec = arena.take([CHUNKS - 1, H, HG_V]), arena.take([H, CHUNKS])
    sums, exps, decayed, upd, asked, exped, split, level, added, states, outs, step = (
        sem(n) for n in ("sums", "exps", "decayed", "upd", "asked", "exped", "split", "level", "added", "states", "outs", "dve"))
    flat = lambda ap: ap.rearrange("p h n -> p (h n)")
    with nc.Block() as block:
        @block.tensor
        def _(pe):
            for h in range(H):
                for t in range(TILES):
                    nc.tensor.matmul(banks[h // 2][:, (h % 2) * TOK + t * P:(h % 2) * TOK + (t + 1) * P],
                                     g[:, t, h * P:(h + 1) * P], consts["upto"][:, :], start=True, stop=True)
            for t in range(TILES):
                m = nc.tensor.matmul(banks[2 + t][:, :], consts["after"][:, :], g[:, t, :], start=True, stop=True)
            m.then_inc(sums, 1)
            pe.wait_ge(decayed, 1)
            for c in range(CHUNKS - 1):
                rows = slice(64 * (c % 2), 64 * (c % 2) + 64)
                for h in range(H):
                    m = nc.tensor.matmul(banks[4 + c][:, h * HG_V:(h + 1) * HG_V], er[rows, c // 2, h * P:(h + 1) * P],
                                         v[rows, c // 2, h * HG_V:(h + 1) * HG_V], start=True, stop=True)
            m.then_inc(upd, 1)
            for n in range(len(LEVELS) + 1):
                if n < len(LEVELS):
                    pe.wait_ge(split, n + 1)
                if n:
                    pe.wait_ge(added, n)
                for u in range(U):
                    s = slice(u * P, (u + 1) * P)
                    kk, qq = (kl[:, s], ql[:, s]) if n < len(LEVELS) else (flat(kT)[:, s], flat(qT)[:, s])
                    m = nc.tensor.matmul(banks[u // 4][:, (u % 4) * P:(u % 4 + 1) * P], kk, qq, start=True, stop=True)
                m.then_inc(level, 1)
            pe.wait_ge(states, 1)
            pe.wait_ge(added, len(LEVELS) + 1)
            for t in range(TILES):
                for h in range(H):
                    o = banks[2 + t][:, h * HG_V:(h + 1) * HG_V]
                    m = nc.tensor.matmul(o, A[:, h * TILES + t, :], v[:, t, h * HG_V:(h + 1) * HG_V], start=True, stop=False,
                                         skip_group_check=True)
                    for c in (2 * t, 2 * t + 1):
                        if c:
                            half = slice(64 * (c % 2), 64 * (c % 2) + 64)
                            m = nc.tensor.matmul(o[half, :], eb[:, h, c * CHUNK:(c + 1) * CHUNK], St[:, c - 1, h, :],
                                                 start=False, stop=True, skip_group_check=True)
            m.then_inc(outs, 1)

        @block.scalar
        def _(act):
            act.wait_ge(sums, 1)
            for i in range(2):
                src = banks[i][:, :].rearrange("p (h n) -> p h n", h=2)
                nc.scalar.activation(eb[:, 2 * i:2 * i + 2, :], src, ACT.Exp)
                nc.scalar.copy(b[:, 2 * i:2 * i + 2, :], src)
            for t in range(TILES):
                m = nc.scalar.activation(er[:, t], banks[2 + t][:, :], ACT.Exp)
            m.then_inc(exps, 1)
            for n in range(len(LEVELS)):
                act.wait_ge(asked, n + 1)
                nc.scalar.activation(ex, ex, ACT.Exp).then_inc(exped, 1)

        @block.vector
        def _(dve):
            link = Chain(dve, step)
            link(nc.vector.memset(ql, 0.0))
            link(nc.vector.memset(kl, 0.0))
            dve.wait_ge(exps, 1)
            link(nc.vector.tensor_copy(dec, eb.rearrange("p h (c n) -> p h c n", n=CHUNK)[:, :, :, CHUNK - 1]))
            link(nc.vector.tensor_tensor(eb, eb, qT, ALU.mult))
            link(nc.vector.tensor_tensor(er, er, k, ALU.mult))
            dve.sem_inc(decayed, 1)
            for n, m in enumerate(LEVELS + (0,)):
                if m:
                    def halves(ap, m=m):
                        v4 = ap.rearrange("p (n two m) -> p n two m", two=2, m=m)
                        return v4[:, :, 0, :], v4[:, :, 1, :]
                    b0, b1 = halves(flat(b))
                    e0, e1 = halves(ex)
                    r = b0[:, :, m - 1:m].to_broadcast([P, H * TOK // (2 * m), m])
                    if n:
                        dve.wait_ge(level, n)
                    link(nc.vector.tensor_tensor(e0, r, b0, ALU.subtract))
                    link(nc.vector.tensor_tensor(e1, b1, r, ALU.subtract))
                    dve.sem_inc(asked, 1)
                    dve.wait_ge(exped, n + 1)
                    link(nc.vector.tensor_tensor(halves(kl)[0], halves(flat(kT))[0], e0, ALU.mult))
                    link(nc.vector.tensor_tensor(halves(ql)[1], halves(flat(qT))[1], e1, ALU.mult))
                    dve.sem_inc(split, 1)
                dve.wait_ge(level, n + 1)
                mask = consts["levels"][:, n * P:(n + 1) * P].unsqueeze(1).to_broadcast([P, 4, P])
                for i in range(2):
                    dst = (tmp if n else A)[:, 4 * i:4 * i + 4, :]
                    link(nc.vector.tensor_tensor(dst, banks[i][:, :].rearrange("p (u k) -> p u k", u=4), mask, ALU.mult))
                if n:
                    link(nc.vector.tensor_tensor(A, A, tmp, ALU.add))
                dve.sem_inc(added, 1)
            dve.wait_ge(upd, 1)
            for c in range(CHUNKS - 1):
                u3 = banks[4 + c][:, :].rearrange("p (h v) -> p h v", h=H)
                if c == 0:
                    link(nc.vector.tensor_copy(St[:, 0], u3))
                else:
                    link(nc.vector.tensor_tensor(St[:, c], St[:, c - 1], dec[:, :, c:c + 1].to_broadcast([P, H, HG_V]), ALU.mult))
                    link(nc.vector.tensor_tensor(St[:, c], u3, St[:, c], ALU.add))
            dve.sem_inc(states, 1)
            dve.wait_ge(outs, 1)
            for t in range(TILES):
                link(nc.vector.tensor_copy(out[:, t, :], banks[2 + t][:, :]))
    stage.close()
    arena.at = mark


def gate_stage(nc, tag, jobs):
    stage = Stage(nc, tag)
    done, step = stage.sem("done"), stage.sem("dve")
    with nc.Block() as block:
        @block.scalar
        def _(act):
            for func, src, dst, times in jobs:
                nc.scalar.activation(src if times else dst, src, func).then_inc(done, 1)

        @block.vector
        def _(dve):
            link = Chain(dve, step)
            for n, (func, src, dst, times) in enumerate(jobs):
                if times:
                    dve.wait_ge(done, n + 1)
                    link(nc.vector.tensor_tensor(dst, dst, src, ALU.mult))
    stage.close()


def rope_stage(nc, tag, jobs, arena):
    stage = Stage(nc, tag)
    step = stage.sem("dve")
    mark = arena.at
    half = ROPE_DIM // 2
    with nc.Block() as block:
        @block.vector
        def _(dve):
            link = Chain(dve, step)
            tmp = arena.take([4, HEADS, half])
            for rows, cos, sin in jobs:
                np_, n = rows.shape[0], rows.shape[1]
                cb, sb = (a.unsqueeze(1).to_broadcast([np_, n, half]) for a in (cos, sin))
                t1, t2 = rows[:, :, 0:half], rows[:, :, half:ROPE_DIM]
                a, b, c, d = (tmp[0:np_, i, 0:n, :] for i in range(4))
                nc.vector.tensor_tensor(a, t1, cb, ALU.mult)
                nc.vector.tensor_tensor(b, t2, sb, ALU.mult)
                nc.vector.tensor_tensor(c, t2, cb, ALU.mult)
                link(nc.vector.tensor_tensor(d, t1, sb, ALU.mult))
                nc.vector.tensor_tensor(t1, a, b, ALU.subtract)
                link(nc.vector.tensor_tensor(t2, c, d, ALU.add))
    stage.close()
    arena.at = mark


def compress_stage(nc, tag, inT, pos, w_k, w_v, kcT, vc, consts, arena, banks):
    stage = Stage(nc, tag)
    sem = stage.sem
    mark = arena.at
    hd = 64
    prow, posT = arena.take([hd], parts=CMP_LEN), arena.take([CMP_LEN], parts=hd)
    w = arena.take([2, CMP_LEN, hd], parts=hd)
    blk = arena.take([4, CMP_LEN, N_CMP], parts=hd)
    kc, tmp = arena.take([2, hd], parts=N_CMP), arena.take([4, 2, ROPE_DIM // 2], parts=N_CMP)
    landed, turned, added, made, roped, back, step = (sem(n) for n in ("w", "turned", "added", "made", "roped", "back", "dve"))
    with nc.Block() as block:
        @block.sync
        def _(sp):
            sp.dma_start(prow, pos).then_inc(landed, 16)
            sp.dma_start(w[:, 0], w_k.rearrange("(l d) o -> d l o", d=hd)).then_inc(landed, 16)
            sp.dma_start(w[:, 1], w_v.rearrange("(l d) o -> d l o", d=hd)).then_inc(landed, 16)

        @block.tensor
        def _(pe):
            pe.wait_ge(landed, 48)
            nc.tensor.transpose(banks[0][0:hd, 0:CMP_LEN], prow, consts["ident"][0:CMP_LEN, 0:CMP_LEN]).then_inc(turned, 1)
            pe.wait_ge(added, 1)
            for l in range(CMP_LEN):
                for u in range(4):
                    m = nc.tensor.matmul(banks[1][32 * u:32 * u + N_CMP, 0:hd], blk[:, u, l, :], w[:, u // 2, l, :],
                                         start=(l == 0), stop=(l == CMP_LEN - 1), skip_group_check=True)
            m.then_inc(made, 1)
            pe.wait_ge(roped, 1)
            for g in range(2):
                m = nc.tensor.transpose(banks[2][0:hd, g * 64:g * 64 + N_CMP], kc[:, g, :], consts["ident"][0:N_CMP, 0:N_CMP])
            m.then_inc(back, 1)

        @block.vector
        def _(dve):
            link = Chain(dve, step)
            dve.wait_ge(turned, 1)
            link(nc.vector.tensor_copy(posT, banks[0][0:hd, 0:CMP_LEN]))
            for u in range(4):
                src = inT[:, u, :]
                windows = bass.AP(src.tensor, src.offset, [src.ap[0], [1, CMP_LEN], [CMP_STRIDE, N_CMP]])
                link(nc.vector.tensor_tensor(blk[:, u], windows, posT.unsqueeze(2).to_broadcast([hd, CMP_LEN, N_CMP]), ALU.add))
            dve.sem_inc(added, 1)
            dve.wait_ge(made, 1)
            for u in range(4):
                link(nc.vector.tensor_copy((kc, vc)[u // 2][:, u % 2, :], banks[1][32 * u:32 * u + N_CMP, 0:hd]))
            half = ROPE_DIM // 2
            cs = consts["rope_cmp"]
            cb, sb = (cs[0:N_CMP, i * half:(i + 1) * half].unsqueeze(1).to_broadcast([N_CMP, 2, half]) for i in range(2))
            t1, t2 = kc[:, :, 0:half], kc[:, :, half:ROPE_DIM]
            for i, (x_, y_) in enumerate(((t1, cb), (t2, sb), (t2, cb), (t1, sb))):
                link(nc.vector.tensor_tensor(tmp[:, i], x_, y_, ALU.mult))
            link(nc.vector.tensor_tensor(t1, tmp[:, 0], tmp[:, 1], ALU.subtract))
            link(nc.vector.tensor_tensor(t2, tmp[:, 2], tmp[:, 3], ALU.add))
            dve.sem_inc(roped, 1)
            dve.wait_ge(back, 1)
            link(nc.vector.tensor_copy(kcT, banks[2][0:hd, 0:2 * 64].rearrange("p (g n) -> p g n", g=2)[:, :, 0:N_CMP]))
    stage.close()
    arena.at = mark


def copy_stage(nc, tag, pairs):
    stage = Stage(nc, tag)
    landed = stage.sem("landed")
    with nc.Block() as block:
        @block.sync
        def _(sp):
            for dst, src in pairs:
                sp.dma_start(dst, src).then_inc(landed, 16)
            sp.wait_ge(landed, 16 * len(pairs))
    stage.close()


def program(nc, ins, const_dram, out, dump=None):
    psum = nc.alloc_psum_tensor("psum", [P, 4096], F32)
    banks = [psum[:, 512 * i:512 * (i + 1)] for i in range(8)]
    x, h, hT = (nc.alloc_sbuf_tensor(n, s, F32)[:, :, :] for n, s in (("x", [P, TILES, D]), ("h", [P, TILES, D]), ("hT", [P, DC, TOK])))
    consts = alloc_consts(nc)
    ident = consts["ident"]
    scratch = nc.dram_tensor("skew_scratch", (2, HEADS, P, SKEW), F32).ap()
    mod_scratch = nc.dram_tensor("mod_scratch", (6 * MB,), F32).ap()
    ccol = nc.alloc_sbuf_tensor("ccol", [P, DC], F32)[:, :]
    norm_tile = nc.alloc_sbuf_tensor("norm_w", [P, D], F32)[:, :]
    norm_sums = nc.alloc_sbuf_tensor("norm_sums", [P, 2, TILES], F32)[:, :, :]
    arena = Arena(nc, (nc.sbuf_usable_end - nc.sbuf_base) // 4 - ARENA_SPARE)
    rows = lambda ap: ap.rearrange("(t p) d -> p t d", p=P)
    whole = Stage(nc, "whole")
    norm_w, skewed = NormWeight(whole, norm_tile, norm_sums), SkewedBias(whole, scratch)

    def experts_of(tag, names, layer):
        stage, mem = Stage(nc, tag), alloc_moe(arena)
        return stage, mem, Experts(stage, mem, extra_slot(arena), *(ins[n][layer] for n in names))

    def moe(plan, gate2, next_norm):
        stage, mem, experts = plan
        moe_stage(nc, stage, experts, x, h, hT, gate2, consts, mem, banks, lambda sp: norm_w.fetch(sp, next_norm))
        arena.top = arena.words

    def normed(tag, scale=None, shift=None, plan=None):
        norm_stage(nc, tag, x, h, norm_w, scale, shift, hT, ident, banks,
                   loads=plan and (lambda sp: plan[2].load_up(sp, 2, 0, 1)))

    def ahead_of(plan, w_row):
        def loads(sp):
            norm_w.fetch(sp, w_row)
            plan[2].prefetch(sp)
        return loads

    later = 6
    for layer in range(2):
        L = f"l{layer}"
        mod = arena.take([6 * D])
        modulation = Modulation(nc, ccol, ins["ada_w"][layer], ins["ada_b"][layer], mod)
        if layer == 0:
            load = lambda n: (consts[n][0:const_dram[n].shape[0], :], const_dram[n])
            start_stage(nc, ins["c"][0], ccol, modulation, [0, 1, 2, 3], [load("ones")],
                        [(x[:, :, :], rows(ins["x"][0]))] + [load(n) for n in consts if n != "ones"],
                        (const_dram["hot_window"], const_dram["hot_causal"]), ins["rel_bias"], skewed, norm_w,
                        ins["norm1_w"][0], arena, banks, consts)
        else:
            copy_stage(nc, L + "_mod", [(mod[:, 0:later * MB], mod_scratch.partition_broadcast(P))])
        shift1, scale1, gate1, shift2, scale2, gate2 = (mod[:, i * D:(i + 1) * D] for i in range(6))
        normed(L + "_norm1", scale1, shift1)
        mark = arena.at
        o = arena.take([TILES, D])
        bias = arena.take([HEADS, TOK])
        if layer == 0:
            N = ins["even_w_in"].shape[2]
            pr = arena.take([TILES, N])
            project_stage(nc, L + "_in", hT, DC, ins["even_w_in"][0], N // 8, pr, arena, banks,
                          side=(modulation, 4 * MB))
            qa, ka, va, qb, kb, vb, rb, ab = (pr[:, :, a:b] for a, b in (
                (0, 512), (512, 640), (640, 768), (768, 1024), (1024, 1280), (1280, 1792), (1792, 2304), (2304, 2320)))
            head_norm_stage(nc, L + "_qknorm", [(qa, 8, 64, ins["a_q_norm"][0]), (ka, 2, 64, ins["a_k_norm"][0])], arena,
                            finish=lambda st: modulation.finisher(st, list(range(4, 12)), banks, consts),
                            loads=lambda sp: skewed.load(sp, 0, bias))
            qT, kT = arena.take([HEADS, TOK], parts=64), arena.take([2, TOK], parts=64)
            qbT, kbT, abT = arena.take([2, TOK]), arena.take([2, TOK]), arena.take([1, TOK], parts=16)
            turn_stage(nc, L + "_turn", [(qa, 64, 8, qT), (ka, 64, 2, kT), (qb, P, 2, qbT), (kb, P, 2, kbT), (ab, 16, 1, abT)],
                       ident, banks)
            sinks = arena.take([HEADS])
            raw = arena.take([later * MB])
            following = Modulation(nc, ccol, ins["ada_w"][1], ins["ada_b"][1], raw)
            copy_stage(nc, L + "_sinks", [(sinks, ins["a_sinks"][0].partition_broadcast(P))])
            attend_stage(nc, L + "_swa", [dict(
                qT=qT, kT=kT, v=lambda kt, kv: va[:, kt, kv * 64:(kv + 1) * 64], hd=64, kv_of=lambda hh: hh // 4, scale=64 ** -0.5,
                bias=lambda t, hs, nk: bias[:, hs, TOK - nk:], out=o[:, :, 0:512], sinks=sinks)], ident, arena, psum,
                side=(following, list(range(later))), bias_wait=lambda eng: skewed.wait(eng, 0))
            g = arena.take([TILES, 256])
            decay_stage(nc, L + "_decay", abT, ins["b_gate_up"][0], ins["b_gate_bias"][0], g, consts, arena, banks)
            ob = arena.take([TILES, 512])
            gla_stage(nc, L + "_gla", g, qbT, kbT, kb, vb, ob, consts, arena, psum, banks)
            head_norm_stage(nc, L + "_onorm", [(ob, 4, 128, ins["b_out_norm"][0])], arena,
                            finish=lambda st: following.finisher(st, list(range(later)), banks, consts))
            copy_stage(nc, L + "_keep", [(mod_scratch.unsqueeze(0), raw[0:1, :])])
            gate_stage(nc, L + "_ogate", [(ACT.Silu, rb, ob, True)])
            gate_stage(nc, L + "_put", [(ACT.Copy, ob, o[:, :, 512:1024], False)])
            w_out = ins["even_w_out"][0]
        else:
            pr = arena.take([TILES, 3 * D])
            project_stage(nc, L + "_in", hT, DC, ins["odd_w_in"][0], 512, pr, arena, banks,
                          side=(modulation, later * MB))
            q, k, v = (pr[:, :, i * D:(i + 1) * D] for i in range(3))
            head_norm_stage(nc, L + "_qknorm", [(q, 8, 128, ins["c_q_norm"][0]), (k, 8, 128, ins["c_k_norm"][0])], arena,
                            finish=lambda st: modulation.finisher(st, list(range(later, 12)), banks, consts),
                            loads=lambda sp: skewed.load(sp, 1, bias))
            qT, kT = arena.take([HEADS, TOK]), arena.take([HEADS, TOK])
            turn_stage(nc, L + "_turn", [(q, P, 8, qT), (k, P, 8, kT)], ident, banks)
            attend_stage(nc, L + "_attn", [dict(
                qT=qT, kT=kT, v=lambda kt, kv: v[:, kt, kv * P:(kv + 1) * P], hd=P, kv_of=lambda hh: hh, scale=P ** -0.5,
                bias=lambda t, hs, nk: bias[:, hs, TOK - nk:], out=o)], ident, arena, psum,
                bias_wait=lambda eng: skewed.wait(eng, 1))
            w_out = ins["odd_w_out"][0]
        turn_stage(nc, L + "_oturn", [(o, P, DC, hT)], ident, banks)
        arena.at = mark
        plan = experts_of(L + "_moe", ("moe_w_group", "moe_b_group", "moe_w_expert", "moe_b_expert", "moe_w1", "moe_w3", "moe_w2"), layer)
        gate_both = bass.AP(gate1.tensor, gate1.offset, [gate1.ap[0], [0, TILES], [1, D]])
        project_stage(nc, L + "_out", hT, DC, w_out, 512, x, arena, banks, gate=gate_both, add=True,
                      ahead=ahead_of(plan, ins["norm2_w"][layer]), tmp=h[:, :, 0:512])
        if dump: dump(L + "_mix", x)
        arena.at = mark
        normed(L + "_norm2", scale2, shift2, plan)
        moe(plan, gate2, ins["attn_norm_2"][0] if layer else ins["norm1_w"][1])
        if dump: dump(L + "_moe", x)
        arena.at = 0

    normed("s_norm1")
    mark = arena.at
    o = arena.take([TILES, D])
    N = ins["w_in_2"].shape[2]
    pr = arena.take([TILES, N])
    project_stage(nc, "s_in", hT, DC, ins["w_in_2"][0], N // 12, pr, arena, banks)
    kv = pr[:, :, 512:1280].rearrange("p t (s g d) -> p t s g d", s=6, g=2)
    mark2 = arena.at
    half = ROPE_DIM // 2
    rope = consts["rope"][:, :].rearrange("p (t n) -> p t n", t=TILES)
    heads = lambda ap: ap.rearrange("p (n d) -> p n d", d=64)
    jobs = []
    for t in range(TILES):
        cs = (rope[:, t, 0:half], rope[:, t, half:])
        jobs += [(heads(pr[:, t, 0:512]), *cs), (kv[:, t, 2], *cs), (kv[:, t, 4], *cs)]
    rope_stage(nc, "s_rope", jobs, arena)
    qT, cT = arena.take([HEADS, TOK], parts=64), arena.take([4, TOK], parts=64)
    ksT, kwT = arena.take([2, TOK], parts=64), arena.take([2, TOK], parts=64)
    turn_stage(nc, "s_turn", [(pr[:, :, 0:512], 64, 8, qT), (pr[:, :, 512:768], 64, 4, cT), (pr[:, :, 768:896], 64, 2, ksT),
                              (pr[:, :, 1024:1152], 64, 2, kwT)], ident, banks)
    kcT, vc = arena.take([2, N_CMP], parts=64), arena.take([2, 64], parts=N_CMP)
    compress_stage(nc, "s_cmp", cT, ins["cmp_pos_2"][0], ins["w_cmp_k_2"][0], ins["w_cmp_v_2"][0], kcT, vc, consts, arena, banks)
    gates = pr[:, :, 1280:1304].rearrange("p t (h i) -> p i t h", i=3)
    gate_stage(nc, "s_gates", [(ACT.Sigmoid, pr[:, :, 1280:1304], pr[:, :, 1280:1304], False),
                               (ACT.Sigmoid, pr[:, :, 3352:], pr[:, :, 3352:], False)])
    cb = consts["cmp_bias"][:, :].rearrange("p (t n) -> p t n", t=TILES)
    cm = consts["cmp_mask"][:, :].rearrange("p (t n) -> p t n", t=TILES)
    o_nsa = o[:, :, 0:512]
    nsa = dict(qT=qT, hd=64, kv_of=lambda hh: hh // 4, scale=64 ** -0.5, out=o_nsa)
    some = cm[:, :, 0:1]
    attentions = [dict(nsa, kT=kcT, v=lambda kt, g_: vc[:, g_, :], keys=N_CMP,
                       bias=lambda t, hs, nk: cb[:, t, :].unsqueeze(1).to_broadcast([P, HEADS // 2, N_CMP]),
                       factors=[lambda t, hs: gates[:, 0, t, hs], lambda t, hs: some[:, t, :].to_broadcast([P, HEADS // 2])])]
    for i, (kk, s) in enumerate(((ksT, 3), (kwT, 5))):
        attentions.append(dict(nsa, kT=kk, v=lambda kt, g_, s=s: kv[:, kt, s, g_, :], add=True,
                               bias=lambda t, hs, nk: consts["causal"][:, TOK - nk:].unsqueeze(1).to_broadcast([P, HEADS // 2, nk]),
                               factors=[lambda t, hs, i=i: gates[:, i + 1, t, hs]]))
    attend_stage(nc, "s_attn", attentions, ident, arena, psum)
    if dump: dump("s_nsa", o)
    arena.at = mark2
    hq, hf, hi, hg = (pr[:, :, 1304 + i * 512:1304 + (i + 1) * 512] for i in range(4))
    kk, g = arena.take([TILES, 512]), arena.take([TILES, 512])
    forget_stage(nc, "s_forget", ins["hg_lb_logits_2"], hf, hf, kk, g, arena)
    hqT, hkT = arena.take([HG_HEADS, TOK]), arena.take([HG_HEADS, TOK])
    turn_stage(nc, "s_hturn", [(hq, P, 4, hqT), (kk, P, 4, hkT)], ident, banks)
    o_hg = o[:, :, 512:1024]
    hgrn_stage(nc, "s_hgrn", g, hqT, hkT, kk, hi, o_hg, consts, arena, banks)
    head_norm_stage(nc, "s_hnorm", [(o_hg, 4, 128, ins["hg_norm_2"][0])], arena)
    gate_stage(nc, "s_hgate", [(ACT.Silu, hg, o_hg, True)])
    arena.at = mark2
    turn_stage(nc, "s_oturn", [(o, P, DC, hT)], ident, banks)
    mixed = arena.take([TILES, D])
    project_stage(nc, "s_brn", hT[:, 0:4, :], 4, ins["w_br_nsa_2"][0], 512, mixed, arena, banks, gate=pr[:, :, 3352:3352 + D])
    project_stage(nc, "s_brh", hT[:, 4:8, :], 4, ins["w_br_hg_2"][0], 512, mixed, arena, banks, gate=pr[:, :, 3352 + D:], add=True)
    turn_stage(nc, "s_mturn", [(mixed, P, DC, hT)], ident, banks)
    arena.at = mark
    plan = experts_of("s_moe", ("w_grp_2", "b_grp_2", "w_rtr_2", "b_rtr_2", "w_gate_2", "w_up_2", "w_down_2"), 0)
    project_stage(nc, "s_out", hT, DC, ins["w_out_2"][0], 512, x, arena, banks, add=True,
                  ahead=ahead_of(plan, ins["ffn_norm_2"][0]))
    if dump: dump("s_mix", x)
    arena.at = mark
    normed("s_norm2", plan=plan)
    moe(plan, None, ins["final_norm_2"])
    norm_stage(nc, "final", x, h, norm_w, None, None, store=rows(out[0]))
    whole.close()


ARENA_SPARE = 32


def extra_slot(arena):
    size = DC * FF
    assert 6 * D + 2 * size <= arena.top and (FF // P) * D <= 5 * D
    return arena.view([DC, FF], 6 * D, P), arena.view([DC, FF], 6 * D + size, P), arena.view([FF // P, D], 0, P)


def alloc_moe(arena):
    W = ROUNDS * E + 4
    shapes = dict(
        w1b=[2, DC, FF], w3b=[2, DC, FF], w2b=[2, FF // P, D], rt=[DC, 36], rb=[36], lg=[TILES, 36], small=[8, 64],
        mask=[TILES, E], slots=[TILES, W], comb=[TILES, W], nsteps=[1], sel=[TILES, P], selw=[TILES, P], selT=[TILES, P],
        xg=[DC, P], hm=[256], sil=[256], hTs=[2, P], y=[2, 512])
    mem = {n: arena.reserve(shape) for n, shape in shapes.items()}
    mem["nsteps"] = mem["nsteps"].bitcast(I32)
    return mem


def kernel(**inputs):
    import numpy as _np
    import concourse.bacc as _bacc
    from concourse import mybir as _mybir
    from concourse.bass_utils import run_bass_kernel_spmd as _run

    nc = _bacc.Bacc("TRN2", target_bir_lowering=False, num_devices=1)
    arrays, ins, consts = {}, {}, {}
    for name, a in inputs.items():
        a = _np.ascontiguousarray(a)
        arrays[f"in_{name}_dram"] = a
        ins[name] = nc.dram_tensor(f"in_{name}_dram", a.shape, _mybir.dt.from_np(a.dtype), kind="ExternalInput").ap()
    for name, a in host_constants().items():
        arrays[f"const_{name}_dram"] = a
        consts[name] = nc.dram_tensor(f"const_{name}_dram", a.shape, _mybir.dt.from_np(a.dtype), kind="ExternalInput").ap()
    out = nc.dram_tensor("out_dram", inputs["x"].shape, F32, kind="ExternalOutput").ap()
    program(nc, ins, consts, out)
    r = _run(nc, [arrays], core_ids=[0])
    return _np.asarray(r.results[0]["out_dram"])
```

```python
import math

import concourse.bass as bass
from concourse import mybir

F32 = mybir.dt.float32
I32 = mybir.dt.int32
ALU = mybir.AluOpType
ACT = mybir.ActivationFunctionType
AX = mybir.AxisListType

P = 128
TOK = 256
TILES = TOK // P
D = 1024
DC = D // P
E = 32
FF = 512
GROUPS = 4
PER_GROUP = 8
BLOCK = 64
ROUNDS = TOK // BLOCK
BIG = 1.0e30
EPS = 1e-6
CHUNK = 64
CHUNKS = TOK // CHUNK
REL_BUCKETS = 32
REL_MAX_DIST = 128
A_WINDOW = 128
SKEW = 384
LEVELS = (32, 16, 8, 4, 2, 1)
ROPE_DIM = 16
ROPE_THETA = 500000.0
CMP_LEN, CMP_STRIDE = 32, 16
N_CMP = (TOK - CMP_LEN) // CMP_STRIDE + 1
HEADS = 8


class Stage:

    def __init__(self, nc, name):
        self.nc, self.name, self.sems = nc, name, []

    def sem(self, name):
        self.sems.append(self.nc.alloc_semaphore(name=f"{self.name}_{name}"))
        return self.sems[-1]

    def close(self):
        self.nc.clear_and_free_semaphores(self.sems)
        self.nc.all_engine_barrier()


class Chain:

    def __init__(self, eng, sem):
        self.eng, self.sem, self.n = eng, sem, 0

    def __call__(self, ins):
        self.n += 1
        ins.then_inc(self.sem, 1)
        self.eng.wait_ge(self.sem, self.n)


class Experts:

    SLOTS = 3
    LOADS = tuple(len(range(slot, E, 3)) for slot in range(3))

    def __init__(self, stage, mem, extra, w_grp, b_grp, w_rtr, b_rtr, w1, w3, w2):
        self.mem = mem
        self.router = ((mem["rt"][:, :, 0:GROUPS], w_grp.rearrange("(c p) n -> p c n", p=P)),
                       (mem["rt"][:, :, GROUPS:], w_rtr.rearrange("(c p) n -> p c n", p=P)),
                       (mem["rb"][:, 0:GROUPS], b_grp.partition_broadcast(P)),
                       (mem["rb"][:, GROUPS:], b_rtr.partition_broadcast(P)))
        self.slots = [(mem["w1b"][:, u], mem["w3b"][:, u], mem["w2b"][:, u]) for u in range(2)] + [extra]
        self.rt_landed = stage.sem("router_landed")
        self.w1_landed, self.w3_landed, self.w2_landed = ([stage.sem(f"{w}_landed{u}") for u in range(3)]
                                                          for w in ("w1", "w3", "w2"))
        pairs = lambda w: w.rearrange("(j two) (c p) n -> two j p c n", two=2, p=P)
        self.w1, self.w3, self.w2 = pairs(w1), pairs(w3), pairs(w2)

    def load_w1(self, sp, slot, u, pair):
        sp.dma_start(self.slots[slot][0], self.w1[u, pair]).then_inc(self.w1_landed[slot], 16)

    def load_w3(self, sp, slot, u, pair):
        sp.dma_start(self.slots[slot][1], self.w3[u, pair]).then_inc(self.w3_landed[slot], 16)

    def load_up(self, sp, slot, u, pair):
        self.load_w1(sp, slot, u, pair)
        self.load_w3(sp, slot, u, pair)

    def load_down(self, sp, slot, u, pair):
        sp.dma_start(self.slots[slot][2], self.w2[u, pair]).then_inc(self.w2_landed[slot], 16)

    def prefetch(self, sp):
        for dst, src in self.router:
            sp.dma_start(dst, src).then_inc(self.rt_landed, 16)
        for u in range(2):
            self.load_up(sp, u, u, 0)
            self.load_down(sp, u, u, 0)


def moe_stage(nc, stage, experts, x, h, hT, gate2, consts, mem, ps, loads, after=None):
    sem = stage.sem
    rt, rb = mem["rt"], mem["rb"]
    ident, tri, ones, iota, order = (consts[k] for k in ("ident", "tri", "ones", "iota", "order"))
    small = mem["small"]
    slots, comb, nsteps = mem["slots"], mem["comb"], mem["nsteps"]
    sel, selw, selT, xg, hm, hTs, y = (mem[k] for k in ("sel", "selw", "selT", "xg", "hm", "hTs", "y"))
    sil = mem["sil"]
    bank_acc, bank_H, bank_T, bank_G, bank_Y = ps[0:4], ps[4], ps[5], ps[6], ps[7]
    rt_landed, w1_landed, w3_landed, w2_landed = experts.rt_landed, experts.w1_landed, experts.w3_landed, experts.w2_landed

    logits_done, mask_ready, pos_done, steps_ready = sem("logits"), sem("mask"), sem("pos"), sem("steps")
    exp_done, exp_asked = sem("exp_done"), sem("exp_asked")
    sel_built, selw_built, gathered, xg_copied = sem("sel_built"), sem("selw_built"), sem("gathered"), sem("xg_copied")
    sel_turned, selT_copied = sem("sel_turned"), sem("selT_copied")
    up_done, silu_done, hm_ready, turned, hT_copied = sem("up"), sem("silu"), sem("hm"), sem("turned"), sem("hT_copied")
    down_done, y_copied, scattered, dve_step = sem("down"), [sem("y_act"), sem("y_dve")], sem("scattered"), sem("dve_step")

    shares_done, shares_copied = sem("shares"), sem("shares_copied")
    NR = GROUPS + E
    shares = xg[:, 0:TOK // P, :].rearrange("p c n -> p (c n)")

    w1_used = sem("w1_used")
    HALF = FF // 2
    H1, H3 = bank_H[:, 0:HALF], bank_H[:, HALF:FF]
    HT = bank_T[:, 0:256].rearrange("p (c n) -> p c n", c=2)
    ST = bank_T[:, 256:512].rearrange("p (t n) -> p t n", t=2)
    XG = bank_G[:, :].rearrange("p (c n) -> p c n", c=DC // 2)
    XG_first = bank_Y[:, :].rearrange("p (c n) -> p c n", c=DC // 2)
    PAIRS = E // 2

    def steps(eng):
        return eng.value_load(nsteps[0:1, 0:1], min_val=1, max_val=ROUNDS)

    with nc.Block() as block:
        @block.sync
        def _(sp):
            experts.load_down(sp, 2, 0, 1)
            loads(sp)
            sp.wait_ge(steps_ready, 1)
            rounds = steps(sp)
            with sp.Fori(0, rounds) as r:
                def refill(k, off):
                    slot, u, pair, done = off % 3, off % 2, k * 3 + off // 2, r * E + k * 6 + (off - 2)
                    sp.wait_ge(w1_used, done)
                    experts.load_w1(sp, slot, u, pair)
                    sp.wait_ge(up_done, done)
                    experts.load_w3(sp, slot, u, pair)
                    sp.wait_ge(down_done, done)
                    experts.load_down(sp, slot, u, pair)

                for off in range(3, 6):
                    refill(0, off)
                with sp.Fori(1, E // 6) as k:
                    for off in range(6):
                        refill(k, off)
                for off in range(E % 6):
                    refill(E // 6, off)
                with sp.If(rounds > r + 1):
                    sp.wait_ge(down_done, r * E + E)
                    for slot, u, pair in ((0, 0, 0), (1, 1, 0), (2, 0, 1)):
                        experts.load_up(sp, slot, u, pair)
                        experts.load_down(sp, slot, u, pair)
            if after:
                sp.wait_ge(down_done, rounds * E)
                after(sp)

        @block.tensor
        def _(pe):
            pe.wait_ge(rt_landed, 64)
            for c in range(DC):
                m = nc.tensor.matmul(bank_G[64 * (c % 2):64 * (c % 2) + NR, 0:TOK], rt[:, c, :], hT[:, c, :],
                                     start=(c < 2), stop=(c >= DC - 2), skip_group_check=True)
            m.then_inc(shares_done, 1)
            pe.wait_ge(shares_copied, 1)
            for t in range(TILES):
                for g in range(2):
                    rows = slice(64 * g, 64 * g + NR)
                    m = nc.tensor.matmul((bank_H, bank_Y)[g][:, t * 64:t * 64 + NR], shares[rows, t * P:(t + 1) * P],
                                         ident[rows, rows], start=True, stop=True)
            m.then_inc(logits_done, 1)
            for b in range(4):
                m = nc.tensor.matmul(bank_acc[b][:, :], consts["after"][0:1, :], consts["levels"][0:1, 0:512], start=True, stop=True)
            pe.wait_ge(mask_ready, 1)
            M = mem["mask"]
            nc.tensor.matmul(bank_T[:, 0:E], tri[:, :], M[:, 0, :], start=True, stop=True)
            nc.tensor.matmul(bank_T[:, E:2 * E], ones[:, :], M[:, 0, :], start=True, stop=False)
            nc.tensor.matmul(bank_T[:, E:2 * E], tri[:, :], M[:, 1, :], start=False, stop=True)
            nc.tensor.matmul(bank_T[:, 2 * E:3 * E], ones[:, :], M[:, 0, :], start=True, stop=False)
            nc.tensor.matmul(bank_T[:, 2 * E:3 * E], ones[:, :], M[:, 1, :], start=False, stop=True).then_inc(pos_done, 1)
            def gather(part, XG=XG):
                for c in range(DC // 2):
                    cc = part * DC // 2 + c
                    for t in range(TILES):
                        m = nc.tensor.matmul(XG[:, c, :], h[:, t, cc * P:(cc + 1) * P], sel[:, t, :],
                                             start=(t == 0), stop=(t == 1))
                m.then_inc(gathered, 1)

            def scatter(t):
                for half in range(2):
                    m = nc.tensor.matmul(bank_acc[2 * t + half][:, :], selT[:, t, :], y[:, half, :], start=False, stop=False,
                                         skip_group_check=True)
                return m

            def up(u, slot, nth):
                for w, out, landed in ((experts.slots[slot][0], H1, w1_landed), (experts.slots[slot][1], H3, w3_landed)):
                    pe.wait_ge(landed[slot], nth * 16)
                    for c in range(DC):
                        for half in range(2):
                            m = nc.tensor.matmul(out[64 * half:64 * half + 64, :], xg[:, c, BLOCK * u:BLOCK * (u + 1)],
                                                 w[:, c, half * HALF:(half + 1) * HALF],
                                                 start=(c == 0), stop=(c == DC - 1), skip_group_check=True)
                    m.then_inc(w1_used if out is H1 else up_done, 1)

            def turn():
                for c in range(2):
                    m = nc.tensor.transpose(HT[:, c, :], hm[:, c * P:(c + 1) * P], ident[:, :])
                m.then_inc(turned, 1)

            def down(slot, nth):
                pe.wait_ge(w2_landed[slot], nth * 16)
                for k in range(4):
                    for half in range(2):
                        m = nc.tensor.matmul(bank_Y[64 * half:64 * half + 64, :],
                                             hTs[:, k % 2, (k // 2) * 64:(k // 2) * 64 + 64],
                                             experts.slots[slot][2][:, k, half * 512:half * 512 + 512],
                                             start=(k == 0), stop=(k == 3), skip_group_check=True)
                m.then_inc(down_done, 1)

            def pair(q, first, second):
                pe.wait_ge(xg_copied, q * 2 + 2)
                up(0, *first)
                for c in y_copied:
                    pe.wait_ge(c, q * 2 + 1)
                pe.wait_ge(selT_copied, q + 1)
                scatter(0)
                pe.wait_ge(hm_ready, q * 2 + 1)
                turn()
                scatter(1).then_inc(scattered, 1)
                pe.wait_ge(hT_copied, q * 2 + 1)
                down(*first)
                pe.wait_ge(selw_built, q + 1)
                for t in range(TILES):
                    m = nc.tensor.transpose(ST[:, t, :], selw[:, t, :], ident[:, :])
                m.then_inc(sel_turned, 1)
                up(1, *second)
                pe.wait_ge(sel_built, q + 2)
                gather(0)
                pe.wait_ge(hm_ready, q * 2 + 2)
                pe.wait_ge(selT_copied, q + 2)
                turn()
                pe.wait_ge(xg_copied, q * 2 + 3)
                gather(1)
                pe.wait_ge(hT_copied, q * 2 + 2)
                for c in y_copied:
                    pe.wait_ge(c, q * 2 + 2)
                down(*second)

            pe.wait_ge(sel_built, 1)
            gather(0)
            gather(1, XG_first)
            pe.wait_ge(steps_ready, 1)
            rounds = steps(pe)
            with pe.Fori(0, rounds) as r:
                def turn_of(k, off):
                    return off % 3, r * experts.LOADS[off % 3] + k * 2 + (off // 3 + 1)

                with pe.Fori(0, E // 6) as k:
                    for a in range(3):
                        pair(r * PAIRS + k * 3 + a, turn_of(k, 2 * a), turn_of(k, 2 * a + 1))
                for a in range(E % 6 // 2):
                    pair(r * PAIRS + (E // 6 * 3 + a), turn_of(E // 6, 2 * a), turn_of(E // 6, 2 * a + 1))
            for c in y_copied:
                pe.wait_ge(c, rounds * E + 1)
            pe.wait_ge(selT_copied, rounds * PAIRS + 1)
            for t in range(TILES):
                scatter(t).then_inc(scattered, 1)

        def copy_y(eng_copy, u, half):
            return eng_copy(y[BLOCK * u:BLOCK * (u + 1), half, :], bank_Y[64 * half:64 * half + 64, :])

        @block.scalar
        def _(act):
            act.wait_ge(shares_done, 1)
            nc.scalar.copy(shares[0:NR, :], bank_G[0:NR, 0:TOK])
            nc.scalar.copy(shares[64:64 + NR, :], bank_G[64:64 + NR, 0:TOK]).then_inc(shares_copied, 1)
            act.wait_ge(exp_asked, 1)
            nc.scalar.activation(small[:, 4, 0:2 * GROUPS], small[:, 3, 0:2 * GROUPS], ACT.Exp).then_inc(exp_done, 1)
            act.wait_ge(exp_asked, 2)
            nc.scalar.activation(small[:, 7, 2:4], small[:, 7, 0:2], ACT.Exp).then_inc(exp_done, 1)
            act.sem_inc(y_copied[0], 1)
            for part in range(2):
                act.wait_ge(gathered, part + 1)
                nc.scalar.copy(xg[:, 4 * part:4 * part + 4, :], (XG, XG_first)[part]).then_inc(xg_copied, 1)
            act.wait_ge(steps_ready, 1)
            rounds = steps(act)
            with act.Fori(0, rounds) as r:
                with act.Fori(0, PAIRS) as i:
                    q = r * PAIRS + i
                    for u in range(2):
                        act.wait_ge(up_done, q * 2 + (u + 1))
                        nc.scalar.activation(sil, H1, ACT.Silu).then_inc(silu_done, 1)
                        if u == 1:
                            for part in range(2):
                                act.wait_ge(gathered, q * 2 + (part + 3))
                                nc.scalar.copy(xg[:, 4 * part:4 * part + 4, :], XG).then_inc(xg_copied, 1)
                        act.wait_ge(down_done, q * 2 + (u + 1))
                        copy_y(nc.scalar.copy, u, 0).then_inc(y_copied[0], 1)

        @block.vector
        def _(dve):
            link = Chain(dve, dve_step)
            nc.vector.memset(selT, 0.0)
            nc.vector.memset(slots[:, :, ROUNDS * E:], -1000.0)
            nc.vector.memset(comb[:, :, ROUNDS * E:], 0.0)
            link(nc.vector.memset(y, 0.0))
            dve.sem_inc(y_copied[1], 1)
            dve.sem_inc(selT_copied, 1)
            lg = mem["lg"]
            dve.wait_ge(logits_done, 1)
            dve.wait_ge(rt_landed, 64)
            both = [bank[:, 0:2 * 64].rearrange("p (t n) -> p t n", t=TILES)[:, :, 0:NR] for bank in (bank_H, bank_Y)]
            link(nc.vector.tensor_tensor(lg, both[0], rb.unsqueeze(1).to_broadcast([P, TILES, NR]), ALU.add))
            link(nc.vector.tensor_tensor(lg, both[1], lg, ALU.add))

            def bc(ap, n):
                return ap.unsqueeze(2).to_broadcast([P, TILES, n])

            def v(k, n):
                return small[:, k, 0:TILES * n].rearrange("p (t n) -> p t n", t=TILES)

            def first_max(vals, n, best, onehot, key):
                link(nc.vector.tensor_reduce(best, vals, AX.X, ALU.max))
                link(nc.vector.tensor_tensor(onehot, vals, bc(best, n), ALU.is_equal))
                link(nc.vector.tensor_tensor(onehot, onehot, order[:, 0:n].unsqueeze(1).to_broadcast([P, TILES, n]), ALU.mult))
                link(nc.vector.tensor_reduce(key, onehot, AX.X, ALU.max))
                link(nc.vector.tensor_tensor(onehot, onehot, bc(key, n), ALU.is_equal))

            gl, el = lg[:, :, 0:GROUPS], lg[:, :, GROUPS:]
            gmax, key, m1, m2, pg, w_a, w_b = (small[:, 5, 2 * i:2 * i + 2] for i in range(7))
            ohg, oh1, oh2 = v(0, GROUPS), v(1, E), v(2, E)
            first_max(gl, GROUPS, gmax, ohg, key)
            link(nc.vector.tensor_tensor(v(3, GROUPS), gl, bc(gmax, GROUPS), ALU.subtract))
            dve.sem_inc(exp_asked, 1)
            pen = v(6, E)
            link(nc.vector.tensor_copy(pen.rearrange("p t (g n) -> p t g n", g=GROUPS),
                                       ohg.unsqueeze(3).to_broadcast([P, TILES, GROUPS, PER_GROUP])))
            link(nc.vector.tensor_scalar(pen, pen, 1.0, BIG, ALU.subtract, ALU.mult))
            link(nc.vector.tensor_tensor(el, el, pen, ALU.add))
            first_max(el, E, m1, oh1, key)
            link(nc.vector.scalar_tensor_tensor(el, oh1, -2.0 * BIG, el, ALU.mult, ALU.add))
            first_max(el, E, m2, oh2, key)
            mask = mem["mask"]
            link(nc.vector.tensor_tensor(mask, oh1, oh2, ALU.add))
            dve.sem_inc(mask_ready, 1)
            link(nc.vector.tensor_tensor(small[:, 7, 0:2], m2, m1, ALU.subtract))
            dve.sem_inc(exp_asked, 1)

            def build(dst, pair, weighted):
                for t in range(TILES):
                    for u in range(2):
                        g = pair * 2 + u
                        place = slots[:, t, bass.ds(g, 1)]
                        m = nc.vector.tensor_scalar(dst[:, t, BLOCK * u:BLOCK * (u + 1)], iota[:, 0:BLOCK], place,
                                                    comb[:, t, bass.ds(g, 1)] if weighted else None, ALU.is_equal,
                                                    ALU.mult if weighted else ALU.bypass)
                return m

            dve.wait_ge(pos_done, 1)
            base = v(6, E)
            link(nc.vector.scalar_tensor_tensor(base, bank_T[:, 0:2 * E].rearrange("p (t n) -> p t n", t=2), 1000.0,
                                                mask, ALU.add, ALU.mult))
            link(nc.vector.tensor_scalar(slots[:, :, 0:E], base, 1000.0, None, ALU.subtract))
            build(sel, 0, False).then_inc(sel_built, 1)
            for k in range(1, ROUNDS):
                link(nc.vector.tensor_scalar(slots[:, :, k * E:(k + 1) * E], base, 1000.0 + BLOCK * k, None, ALU.subtract))
            full, rnd, more = (small[:, 5, c:c + 1] for c in (14, 15, 16))
            link(nc.vector.tensor_reduce(full, bank_T[:, 2 * E:3 * E], AX.X, ALU.max))
            link(nc.vector.tensor_scalar(rnd, full, float(BLOCK), 1.0, ALU.is_gt, ALU.add))
            for k in range(2, ROUNDS):
                link(nc.vector.tensor_scalar(more, full, float(BLOCK * k), None, ALU.is_gt))
                link(nc.vector.tensor_tensor(rnd, rnd, more, ALU.add))
            link(nc.vector.tensor_copy(nsteps[:, :], rnd))
            dve.sem_inc(steps_ready, 1)
            dve.wait_ge(exp_done, 1)
            link(nc.vector.tensor_reduce(pg, v(4, GROUPS), AX.X, ALU.add))
            dve.wait_ge(exp_done, 2)
            ex = small[:, 7, 2:4]
            link(nc.vector.tensor_scalar(w_a, ex, 1.0, None, ALU.add))
            link(nc.vector.tensor_tensor(w_a, w_a, pg, ALU.mult))
            link(nc.vector.reciprocal(w_b, w_a))
            link(nc.vector.tensor_tensor(w_a, w_b, ex, ALU.mult))
            link(nc.vector.tensor_tensor(oh1, oh1, bc(w_b, E), ALU.mult))
            link(nc.vector.tensor_tensor(oh2, oh2, bc(w_a, E), ALU.mult))
            for k in range(ROUNDS):
                link(nc.vector.tensor_tensor(comb[:, :, k * E:(k + 1) * E], oh1, oh2, ALU.add))
            build(selw, 0, True).then_inc(selw_built, 1)
            dve.wait_ge(gathered, 2)
            build(sel, 1, False).then_inc(sel_built, 1)
            rounds = steps(dve)
            with dve.Fori(0, rounds) as r:
                with dve.Fori(0, PAIRS) as i:
                    q = r * PAIRS + i
                    for u in range(2):
                        dve.wait_ge(silu_done, q * 2 + (u + 1))
                        nc.vector.tensor_tensor(hm, sil, H3, ALU.mult).then_inc(hm_ready, 1)
                        dve.wait_ge(turned, q * 2 + (u + 1))
                        nc.vector.tensor_copy(hTs, HT).then_inc(hT_copied, 1)
                        if u == 1:
                            dve.wait_ge(gathered, q * 2 + 4)
                            build(sel, q + 2, False).then_inc(sel_built, 1)
                        dve.wait_ge(down_done, q * 2 + (u + 1))
                        copy_y(nc.vector.tensor_copy, u, 1).then_inc(y_copied[1], 1)
                        if u == 0:
                            dve.wait_ge(sel_turned, q + 1)
                            nc.vector.tensor_copy(selT, ST).then_inc(selT_copied, 1)
                            build(selw, q + 1, True).then_inc(selw_built, 1)
            for t in range(TILES):
                dve.wait_ge(scattered, rounds * PAIRS + (t + 1))
                for half in range(2):
                    cols = slice(half * 512, half * 512 + 512)
                    moved = bank_acc[2 * t + half][:, :]
                    if gate2 is not None:
                        link(nc.vector.tensor_tensor(h[:, t, cols], moved, gate2[:, cols], ALU.mult))
                        moved = h[:, t, cols]
                    link(nc.vector.tensor_tensor(x[:, t, cols], moved, x[:, t, cols], ALU.add))
    stage.close()


def bucket_of(dist):
    import numpy as np
    exact = REL_BUCKETS // 2
    d = np.maximum(dist, 0)
    logd = np.log(np.maximum(d, 1).astype(np.float32) / np.float32(exact)) / np.float32(math.log(REL_MAX_DIST / exact))
    far = np.minimum(exact + (logd.astype(np.float32) * np.float32(REL_BUCKETS - exact)).astype(np.int32), REL_BUCKETS - 1)
    return np.where(d < exact, d, far)


def host_constants():
    import numpy as np
    f = np.float32
    c = {}
    c["ident"] = np.eye(P, dtype=f)
    c["tri"] = np.triu(np.ones((P, P), f), 1)
    c["ones"] = np.ones((P, P), f)
    c["iota"] = np.tile(np.arange(BLOCK, dtype=f), (P, 1))
    c["order"] = np.tile(np.arange(E, 0, -1, dtype=f), (P, 1))
    i = np.arange(P)
    same = (i[:, None] // CHUNK) == (i[None, :] // CHUNK)
    c["upto"] = ((i[:, None] <= i[None, :]) & same).astype(f)
    c["after"] = ((i[:, None] > i[None, :]) & same).astype(f)
    dist = 255 - np.arange(SKEW)
    hot = (bucket_of(dist)[None, :] == np.arange(REL_BUCKETS)[:, None])
    for name, ok in (("hot_window", (dist >= 0) & (dist < A_WINDOW)), ("hot_causal", dist >= 0)):
        c[name] = np.concatenate([hot & ok, ~ok[None]], 0).astype(f)
    j = np.arange(TOK)
    c["causal"] = np.where(P + i[:, None] - j[None, :] >= 0, 0.0, -BIG).astype(f)
    c["levels"] = np.stack([((i[:, None] // (2 * m)) == (i[None, :] // (2 * m))) & (i[:, None] % (2 * m) < m)
                            & (i[None, :] % (2 * m) >= m) for m in LEVELS] + [i[:, None] == i[None, :]], 1
                           ).astype(f).reshape(P, -1)
    half = ROPE_DIM // 2
    inv = (f(ROPE_THETA) ** (-np.arange(half, dtype=f) / f(half))).astype(f)
    ang = np.arange(TOK, dtype=f)[:, None] * inv[None, :]
    rope = np.concatenate([np.cos(ang), np.sin(ang)], 1).astype(f)
    c["rope"] = rope.reshape(TILES, P, ROPE_DIM).transpose(1, 0, 2).reshape(P, -1)
    c["rope_cmp"] = np.zeros((P, ROPE_DIM), f)
    c["rope_cmp"][:N_CMP] = rope[np.arange(N_CMP) * CMP_STRIDE]
    ok = (np.arange(N_CMP) * CMP_STRIDE + CMP_LEN - 1)[None, :] <= j[:, None]
    ok = ok.reshape(TILES, P, N_CMP).transpose(1, 0, 2)
    c["cmp_bias"] = np.where(ok, 0.0, -BIG).astype(f).reshape(P, -1)
    c["cmp_mask"] = ok.astype(f).reshape(P, -1)
    return c


def alloc_consts(nc):
    return {n: nc.alloc_sbuf_tensor(f"const_{n}", list(a.shape), F32) for n, a in host_constants().items() if "hot" not in n}


class Arena:

    def __init__(self, nc, words):
        self.t, self.words, self.at = nc.alloc_sbuf_tensor("arena", [P, words], F32), words, 0
        self.top = words

    def reserve(self, shape):
        self.top -= math.prod(shape)
        assert self.at <= self.top, (self.at, self.top)
        return self.view(shape, self.top, P)

    def take(self, shape, parts=P):
        self.at += math.prod(shape)
        assert self.at <= self.top, (self.at, self.top)
        return self.view(shape, self.at - math.prod(shape), parts)

    def view(self, shape, at, parts):
        ap = self.t[0:parts, at:at + math.prod(shape)]
        names = "abcd"[:len(shape)]
        if len(shape) > 1:
            ap = ap.rearrange(f"p ({' '.join(names)}) -> p {' '.join(names)}", **dict(zip(names, shape)))
        return ap


def col(w):
    return w.rearrange("(p c) -> p c", p=P)


MB = 512


class Modulation:

    STEPS = DC + 1
    LANDED = 32

    def __init__(self, nc, ccol, ada_w, ada_b, mod):
        self.nc, self.ccol, self.mod = nc, ccol, mod
        self.wv, self.b = ada_w.rearrange("(p c) n -> p c n", p=P), ada_b.unsqueeze(0)

    @staticmethod
    def slots(arena, n):
        return arena.take([n, DC, MB]), arena.take([n, MB], parts=1)

    def load(self, sp, slots, u, col, landed):
        cols = bass.ds(col, MB)
        sp.dma_start(slots[0][:, u], self.wv[:, :, cols]).then_inc(landed, 16)
        sp.dma_start(slots[1][:, u], self.b[:, cols]).then_inc(landed, 16)

    def accumulate(self, eng, slots, u, out, step, done):
        nc, wt = self.nc, slots[0][:, u]
        for k in range(DC):
            if k == 0:
                m = nc.vector.tensor_scalar(out, wt[:, 0, :], self.ccol[:, 0:1], None, ALU.mult)
            else:
                eng.wait_ge(step, done + k)
                m = nc.vector.scalar_tensor_tensor(out, wt[:, k, :], self.ccol[:, k:k + 1], out, ALU.mult, ALU.add)
            m.then_inc(step, 1)
        eng.wait_ge(step, done + DC)
        nc.vector.tensor_tensor(out[0:1, :], out[0:1, :], slots[1][:, u], ALU.add).then_inc(step, 1)

    def finisher(self, stage, blocks, banks, consts, to=None):
        return Finish(self, stage, blocks, banks, consts, to if to is not None else self.mod)


class Finish:

    def __init__(self, m, stage, blocks, banks, consts, to):
        self.m, self.blocks, self.banks, self.consts, self.to = m, blocks, banks, consts, to
        self.summed, self.copied = stage.sem("mod_summed"), stage.sem("mod_copied")

    def tensor(self, pe, added=None):
        nc = self.m.nc
        for n, j in enumerate(self.blocks):
            bank = self.banks[n % len(self.banks)]
            if added is not None:
                pe.wait_ge(added, Modulation.STEPS * (n + 1))
            if n >= len(self.banks):
                pe.wait_ge(self.copied, n - len(self.banks) + 1)
            nc.tensor.matmul(bank, self.consts["ones"][:, :], self.m.mod[:, j * MB:(j + 1) * MB], start=True,
                             stop=True).then_inc(self.summed, 1)

    def scalar(self, act):
        for n, j in enumerate(self.blocks):
            act.wait_ge(self.summed, n + 1)
            self.m.nc.scalar.copy(self.to[:, j * MB:(j + 1) * MB], self.banks[n % len(self.banks)]).then_inc(self.copied, 1)


class NormWeight:

    def __init__(self, stage, tile, sums):
        self.tile, self.sums, self.landed, self.n = tile, sums, stage.sem("norm_w"), 0

    def fetch(self, sp, w_row):
        self.n += 1
        sp.dma_start(self.tile, w_row.partition_broadcast(P)).then_inc(self.landed, 16)

    def wait(self, eng):
        eng.wait_ge(self.landed, 16 * self.n)


def start_stage(nc, c_vec, ccol, m, blocks, early, late, hot_dram, rel_bias, skewed, norm_w, first_norm, arena, banks, consts):
    stage = Stage(nc, "start")
    mark = arena.at
    SLOTS = 3
    slots = m.slots(arena, SLOTS)
    hot, rows = arena.take([2, SKEW], parts=REL_BUCKETS + 1), arena.take([2, SKEW], parts=HEADS)
    rb = arena.take([HEADS], parts=REL_BUCKETS + 1)
    landed, step, c_landed, c_ready = [stage.sem(f"w{u}") for u in range(SLOTS)], stage.sem("dve"), stage.sem("c"), stage.sem("silu")
    early_landed, late_landed, masked, made, copied = (stage.sem(n) for n in ("early", "late", "masked", "made", "copied"))
    fin = m.finisher(stage, blocks, banks[0:6], consts)
    with nc.Block() as block:
        @block.gpsimd
        def _(pool):
            nc.gpsimd.memset(rb[REL_BUCKETS:REL_BUCKETS + 1, :], -BIG).then_inc(masked, 1)

        @block.sync
        def _(sp):
            sp.dma_start(ccol, col(c_vec)).then_inc(c_landed, 16)
            for n, j in enumerate(blocks):
                if n >= SLOTS:
                    sp.wait_ge(step, m.STEPS * (n - SLOTS + 1))
                m.load(sp, slots, n % SLOTS, j * MB, landed[n % SLOTS])
                if n == 0:
                    for dst, src in early:
                        sp.dma_start(dst, src).then_inc(early_landed, 16)
                    sp.dma_start(rb[0:REL_BUCKETS, :], rel_bias).then_inc(early_landed, 16)
                    for i in range(2):
                        sp.dma_start(hot[:, i], hot_dram[i]).then_inc(early_landed, 16)
            for dst, src in late:
                sp.dma_start(dst, src).then_inc(late_landed, 16)
            norm_w.fetch(sp, first_norm)
            sp.wait_ge(copied, 1)
            skewed.store(sp, rows)
            sp.wait_ge(late_landed, 16 * len(late))
            skewed.wait_stored(sp)

        @block.tensor
        def _(pe):
            pe.wait_ge(early_landed, 16 * (len(early) + 3))
            pe.wait_ge(masked, 1)
            for i in range(2):
                r = nc.tensor.matmul(banks[6 + i][0:HEADS, 0:SKEW], rb, hot[:, i], start=True, stop=True)
            r.then_inc(made, 1)
            fin.tensor(pe, step)

        @block.vector
        def _(dve):
            dve.wait_ge(c_ready, 1)
            for n, j in enumerate(blocks):
                dve.wait_ge(landed[n % SLOTS], m.LANDED * (n // SLOTS + 1))
                m.accumulate(dve, slots, n % SLOTS, m.mod[:, j * MB:(j + 1) * MB], step, m.STEPS * n)

        @block.scalar
        def _(act):
            act.wait_ge(c_landed, 16)
            nc.scalar.activation(ccol, ccol, ACT.Silu).then_inc(c_ready, 1)
            act.wait_ge(made, 1)
            nc.scalar.copy(rows[:, 0], banks[6][0:HEADS, 0:SKEW])
            nc.scalar.copy(rows[:, 1], banks[7][0:HEADS, 0:SKEW]).then_inc(copied, 1)
            fin.scalar(act)
    stage.close()
    arena.at = mark


class SkewedBias:

    def __init__(self, stage, scratch):
        self.scratch, self.stored, self.landed = scratch, stage.sem("skew_stored"), stage.sem("bias_landed")

    def store(self, sp, rows):
        for i in range(2):
            sp.dma_start(self.scratch[i], rows[:, i].unsqueeze(1).to_broadcast([HEADS, P, SKEW])).then_inc(self.stored, 16)

    def wait_stored(self, sp):
        sp.wait_ge(self.stored, 32)

    def load(self, sp, i, out):
        src = bass.AP(self.scratch.tensor, i * HEADS * P * SKEW + P - 1, [[SKEW - 1, P], [P * SKEW, HEADS], [1, TOK]])
        sp.dma_start(out, src).then_inc(self.landed, 16)

    def wait(self, eng, i):
        eng.wait_ge(self.landed, 16 * (i + 1))


def norm_stage(nc, tag, x, out, norm_w, scale, shift, outT=None, ident=None, banks=None, store=None,
               loads=None, ready_too=None):
    stage = Stage(nc, tag)
    sem = stage.sem
    w, ss, rs = norm_w.tile, norm_w.sums[:, 0], norm_w.sums[:, 1]
    squared, root_asked, root_done, step, ready, turned = (sem(n) for n in ("sq", "ask", "root", "dve", "ready", "turned"))
    kept = sem("kept")
    HC = DC // 2
    with nc.Block() as block:
        @block.scalar
        def _(act):
            for t in range(TILES):
                nc.scalar.activation(out[:, t, :], x[:, t, :], ACT.Square, accum_out=ss[:, t:t + 1]).then_inc(squared, 1)
            act.wait_ge(root_asked, 1)
            nc.scalar.activation(rs, ss, ACT.Sqrt).then_inc(root_done, 1)
            if outT is not None:
                for n in range(2 * TILES):
                    t, half = n // 2, n % 2
                    if n != 2 * TILES - 2:
                        act.wait_ge(turned, n + 1)
                        nc.scalar.copy(outT[:, HC * half:HC * half + HC, t * P:(t + 1) * P], banks[n].rearrange("p (c n) -> p c n", c=HC))

        @block.vector
        def _(dve):
            link = Chain(dve, step)
            norm_w.wait(dve)
            if ready_too:
                dve.wait_ge(*ready_too)
            if scale is not None:
                link(nc.vector.scalar_tensor_tensor(w, scale, 1.0, w, ALU.add, ALU.mult))
            dve.wait_ge(squared, TILES)
            link(nc.vector.tensor_scalar(ss, ss, 1.0 / D, EPS, ALU.mult, ALU.add))
            dve.sem_inc(root_asked, 1)
            dve.wait_ge(root_done, 1)
            link(nc.vector.reciprocal(rs, rs))
            for t in range(TILES):
                for half in range(2):
                    cols = slice(half * D // 2, (half + 1) * D // 2)
                    link(nc.vector.scalar_tensor_tensor(out[:, t, cols], x[:, t, cols], rs[:, t:t + 1], w[:, cols], ALU.mult, ALU.mult))
                    if shift is not None:
                        link(nc.vector.tensor_tensor(out[:, t, cols], out[:, t, cols], shift[:, cols], ALU.add))
                    dve.sem_inc(ready, 1)
            if outT is not None:
                n = 2 * TILES - 2
                dve.wait_ge(turned, n + 1)
                nc.vector.tensor_copy(outT[:, 0:HC, (TILES - 1) * P:], banks[n].rearrange("p (c n) -> p c n", c=HC))

        if outT is not None:
            @block.tensor
            def _(pe):
                for n in range(2 * TILES):
                    t, half = n // 2, n % 2
                    pe.wait_ge(ready, n + 1)
                    for c in range(HC):
                        m = nc.tensor.transpose(banks[n][:, c * P:(c + 1) * P], out[:, t, (half * HC + c) * P:(half * HC + c + 1) * P],
                                                ident[:, :])
                    m.then_inc(turned, 1)

        @block.sync
        def _(sp):
            if loads is not None:
                loads(sp)
            if store is not None:
                for t in range(TILES):
                    sp.wait_ge(ready, 2 * (t + 1))
                    sp.dma_start(store[:, t, :], out[:, t, :]).then_inc(kept, 16)
                sp.wait_ge(kept, 16 * TILES)
    stage.close()


def turn_stage(nc, tag, jobs, ident, banks):
    stage = Stage(nc, tag)
    sem = stage.sem
    pairs = [(src, w, i, min(2, n - i), dst) for src, w, n, dst in jobs for i in range(0, n, 2)]
    turned, copied = sem("turned"), [sem("copied_dve"), sem("copied_act")]
    with nc.Block() as block:
        @block.tensor
        def _(pe):
            for j, (src, w, i, m, dst) in enumerate(pairs):
                if j >= 8:
                    pe.wait_ge(copied[j % 2], (j - 8) // 2 + 1)
                for k in range(m):
                    for t in range(TILES):
                        last = nc.tensor.transpose(banks[j % 8][0:w, k * TOK + t * P:k * TOK + (t + 1) * P],
                                                   src[:, t, (i + k) * w:(i + k + 1) * w], ident[:, :])
                last.then_inc(turned, 1)

        def out(j):
            src, w, i, m, dst = pairs[j]
            return dst[:, i:i + m, :], banks[j % 8][0:w, 0:m * TOK].rearrange("p (m n) -> p m n", m=m)

        @block.vector
        def _(dve):
            for j in range(0, len(pairs), 2):
                dve.wait_ge(turned, j + 1)
                nc.vector.tensor_copy(*out(j)).then_inc(copied[0], 1)

        @block.scalar
        def _(act):
            for j in range(1, len(pairs), 2):
                act.wait_ge(turned, j + 1)
                nc.scalar.copy(*out(j)).then_inc(copied[1], 1)
    stage.close()


class Columns:

    def __init__(self, nc, tag, w, kc, width, arena, at=None):
        self.stage, self.w, self.kc, self.width = Stage(nc, tag), w, kc, width
        self.N = w.shape[1] // width
        self.wt = arena.take([2, kc, width]) if at is None else arena.view([2, kc, width], at, P)
        self.landed = [self.stage.sem("w0"), self.stage.sem("w1")]

    def load(self, sp, b, u):
        src = self.w[:, bass.ds(b * self.width, self.width)]
        sp.dma_start(self.wt[:, u], src.rearrange("(c p) n -> p c n", p=P)).then_inc(self.landed[u], 16)

    def fetch(self, sp):
        for u in range(min(2, self.N)):
            self.load(sp, u, u)


def project_stage(nc, columns, inT, out, arena, banks, gate=None, add=False, ahead=None, tmp=None, side=None, first=None):
    stage = columns.stage
    sem = stage.sem
    mark = arena.at
    wt, width, kc, N = columns.wt, columns.width, columns.kc, columns.N
    landed, row_done, copied, step = columns.landed, sem("row"), [sem("copied0"), sem("copied1")], sem("dve")
    plain = gate is None and not add
    if side:
        modulation, side_col = side
        side_slots = modulation.slots(arena, 2)
        side_landed, side_step = [sem("side0"), sem("side1")], sem("side_step")
        STEPS, LANDED = modulation.STEPS, modulation.LANDED

    def both(eng, first, body):
        if N // 2 > first:
            with eng.Fori(first, N // 2) as i:
                for u in range(2):
                    body(i * 2 + u, i, u)
        if N % 2 and N // 2 >= first:
            body(N - 1, N // 2, 0)

    with nc.Block() as block:
        @block.sync
        def _(sp):
            def load_side(b, i, u, first=False):
                if side:
                    if not first:
                        sp.wait_ge(side_step, i * (2 * STEPS) + STEPS * (u - 1))
                    modulation.load(sp, side_slots, u, b * MB + side_col, side_landed[u])

            def later(b, i, u):
                sp.wait_ge(row_done, i * 2 + (u - 1))
                columns.load(sp, b, u)
                load_side(b, i, u)
            if first:
                first(sp)
            for u in range(min(2, N)):
                load_side(u, 0, u, True)
            both(sp, 1, later)
            if ahead:
                ahead(sp)

        @block.tensor
        def _(pe):
            def body(b, i, u):
                pe.wait_ge(landed[u], i * 16 + 16)
                for t in range(TILES):
                    pe.wait_ge(copied[t], i * 2 + (u + 1))
                    for k in range(kc):
                        m = nc.tensor.matmul(banks[2 * u + t][:, 0:width], inT[:, k, t * P:(t + 1) * P], wt[:, u, k, :],
                                             start=(k == 0), stop=(k == kc - 1))
                m.then_inc(row_done, 1)
            both(pe, 0, body)

        def at(ap, t, b):
            return ap[:, t, bass.ds(b * width, width)] if not isinstance(b, int) else ap[:, t, b * width:(b + 1) * width]

        @block.scalar
        def _(act):
            if plain:
                act.sem_inc(copied[1], 2)

                def body(b, i, u):
                    act.wait_ge(row_done, i * 2 + (u + 1))
                    nc.scalar.copy(at(out, 1, b), banks[2 * u + 1][:, 0:width]).then_inc(copied[1], 1)
                both(act, 0, body)

        @block.vector
        def _(dve):
            dve.sem_inc(copied[0], 2)
            if plain:
                def body(b, i, u):
                    dve.wait_ge(row_done, i * 2 + (u + 1))
                    nc.vector.tensor_copy(at(out, 0, b), banks[2 * u][:, 0:width]).then_inc(copied[0], 1)
                    if side:
                        dve.wait_ge(side_landed[u], i * LANDED + LANDED)
                        modulation.accumulate(dve, side_slots, u, modulation.mod[:, bass.ds(b * MB + side_col, MB)], side_step,
                                              i * (2 * STEPS) + STEPS * u)
            else:
                dve.sem_inc(copied[1], 2)

                def body(b, i, u):
                    dve.wait_ge(row_done, i * 2 + (u + 1))
                    for t in range(TILES):
                        o, src = at(out, t, b), banks[2 * u + t][:, 0:width]
                        if gate is not None and not add:
                            nc.vector.tensor_tensor(o, src, at(gate, t, b), ALU.mult).then_inc(copied[t], 1)
                        elif gate is None:
                            nc.vector.tensor_tensor(o, src, o, ALU.add).then_inc(copied[t], 1)
                        else:
                            nc.vector.tensor_tensor(tmp[:, t], src, at(gate, t, b), ALU.mult).then_inc(step, 1)
                            dve.wait_ge(step, i * 4 + (u * 2 + t + 1))
                            nc.vector.tensor_tensor(o, tmp[:, t], o, ALU.add).then_inc(copied[t], 1)
            both(dve, 0, body)
    stage.close()
    arena.at = mark


def head_norm_stage(nc, tag, jobs, arena, finish=None, loads=None, gated=None):
    stage = Stage(nc, tag)
    sem = stage.sem
    mark = arena.at
    parts = [(rows[:, t, :], n, w, k) for k, (rows, n, w, _) in enumerate(jobs) for t in range(TILES)]
    most = max(n * w for _, n, w, _ in jobs)
    total = sum(n for _, n, _, _ in jobs) * TILES
    sq, ss, rs = arena.take([2, most]), arena.take([total]), arena.take([total])
    ws = [arena.take([w]) for _, _, w, _ in jobs]
    landed, root_asked, root_done, step = sem("w"), sem("ask"), sem("root"), sem("dve")
    squared, summed, silu_done = sem("squared"), sem("summed"), sem("silu")
    fin = finish and finish(stage)
    with nc.Block() as block:
        @block.sync
        def _(sp):
            for (_, _, _, w_row), w in zip(jobs, ws):
                sp.dma_start(w, w_row.partition_broadcast(P)).then_inc(landed, 16)
            if loads:
                loads(sp)

        @block.tensor
        def _(pe):
            if fin:
                fin.tensor(pe)

        @block.scalar
        def _(act):
            for i, (r, n, w, _) in enumerate(parts):
                if i >= 2:
                    act.wait_ge(summed, i - 1)
                nc.scalar.activation(sq[:, i % 2, 0:n * w], r, ACT.Square).then_inc(squared, 1)
            act.wait_ge(root_asked, 1)
            nc.scalar.activation(rs, ss, ACT.Sqrt).then_inc(root_done, 1)
            if gated:
                nc.scalar.activation(gated[0], gated[0], ACT.Silu).then_inc(silu_done, 1)
            if fin:
                fin.scalar(act)

        @block.vector
        def _(dve):
            link = Chain(dve, step)
            at, places = 0, []
            for i, (r, n, w, _) in enumerate(parts):
                dve.wait_ge(squared, i + 1)
                nc.vector.tensor_reduce(ss[:, at:at + n], sq[:, i % 2, 0:n * w].rearrange("p (n w) -> p n w", w=w),
                                        AX.X, ALU.add).then_inc(summed, 1)
                dve.wait_ge(summed, i + 1)
                link(nc.vector.tensor_scalar(ss[:, at:at + n], ss[:, at:at + n], 1.0 / w, EPS, ALU.mult, ALU.add))
                places.append(at)
                at += n
            dve.sem_inc(root_asked, 1)
            dve.wait_ge(root_done, 1)
            link(nc.vector.reciprocal(rs, rs))
            dve.wait_ge(landed, 16 * len(jobs))
            for (r, n, w, k), a in zip(parts, places):
                r = r.rearrange("p (n w) -> p n w", w=w)
                link(nc.vector.tensor_tensor(r, r, rs[:, a:a + n].unsqueeze(2).to_broadcast([P, n, w]), ALU.mult))
                link(nc.vector.tensor_tensor(r, r, ws[k].unsqueeze(1).to_broadcast([P, n, w]), ALU.mult))
            if gated:
                dve.wait_ge(silu_done, 1)
                z, out = gated
                link(nc.vector.tensor_tensor(out, jobs[0][0], z, ALU.mult))
    stage.close()
    arena.at = mark


def attend_stage(nc, tag, jobs, ident, arena, psum, side=None, bias_wait=None):
    stage = Stage(nc, tag)
    sem = stage.sem
    mark = arena.at
    G = HEADS // 2
    units = [(job, t, slice(G * g, G * g + G), job.get("keys") or (t + 1) * P)
             for job in jobs for t in range(TILES) for g in range(2)]
    most = max(nk for *_, nk in units)
    L, PT = arena.take([2, G, most]), arena.take([2, 2 * G, P])
    mx, sm, es, tmp = arena.take([3, G]), arena.take([3, G]), arena.take([3, G]), arena.take([G * max(j["hd"] for j in jobs)])
    names = ("scores", "scaled", "maxed", "probs", "turned", "pt", "outs", "written", "dve", "act")
    scores, scaled, maxed, probs, turned, pt_copied, outs, written, step, astep = (sem(n) for n in names)

    if side:
        modulation, blocks, side_slots = side
        side_landed, side_step = [sem("side0"), sem("side1")], sem("side_step")

    def S(n, nk):
        return psum[:, 1024 * (n % 2):1024 * (n % 2 + 1)].rearrange("p (h n) -> p h n", h=G)[:, :, 0:nk]

    T = psum[:, 2048:3072].rearrange("p (u n) -> p u n", n=P)

    def O(n, hd):
        return psum[:, 3072 + 512 * (n % 2):3072 + 512 * (n % 2) + G * hd]

    with nc.Block() as block:
        @block.tensor
        def _(pe):
            turn_first = len(units) <= 4

            def turn_unit(n):
                job, t, hs, nk = units[n - 1]
                nkt, w = -(-nk // P), min(P, nk)
                pe.wait_ge(probs, n)
                if n >= 2:
                    pe.wait_ge(pt_copied, n - 1)
                for i in range(G):
                    for kt in range(nkt):
                        m = nc.tensor.transpose(T[0:w, i * nkt + kt, :], L[:, (n - 1) % 2, i, kt * P:kt * P + w], ident[:, :])
                m.then_inc(turned, 1)

            def output_unit(n):
                job, t, hs, nk = units[n - 2]
                hd, nkt, w = job["hd"], -(-nk // P), min(P, nk)
                pe.wait_ge(pt_copied, n - 1)
                if n >= 4:
                    pe.wait_ge(written, n - 3)
                for i, h in enumerate(range(hs.start, hs.stop)):
                    for kt in range(nkt):
                        m = nc.tensor.matmul(O(n - 2, hd)[:, i * hd:(i + 1) * hd], PT[0:w, (n - 2) % 2, i * nkt + kt, :],
                                             job["v"](kt, job["kv_of"](h)), start=(kt == 0), stop=(kt == nkt - 1))
                m.then_inc(outs, 1)

            for n in range(len(units) + 2):
                if n < len(units):
                    job, t, hs, nk = units[n]
                    if n >= 2:
                        pe.wait_ge(scaled, n - 1)
                    for i, h in enumerate(range(hs.start, hs.stop)):
                        m = nc.tensor.matmul(S(n, nk)[:, i, :], job["qT"][:, h, t * P:(t + 1) * P],
                                             job["kT"][:, job["kv_of"](h), 0:nk], start=True, stop=True)
                    m.then_inc(scores, 1)
                if turn_first and 0 <= n - 1 < len(units):
                    turn_unit(n)
                if n >= 2:
                    output_unit(n)
                if not turn_first and 0 <= n - 1 < len(units):
                    turn_unit(n)

        @block.scalar
        def _(act):
            for n in range(len(units) + 1):
                if n < len(units):
                    job, t, hs, nk = units[n]
                    act.wait_ge(maxed, n + 1)
                    for i in range(G):
                        m = nc.scalar.activation(L[:, n % 2, i, 0:nk], L[:, n % 2, i, 0:nk], ACT.Exp, bias=mx[:, n % 3, i:i + 1],
                                                 accum_out=sm[:, n % 3, i:i + 1])
                    if job.get("sinks") is not None:
                        m = nc.scalar.activation(es[:, n % 3], es[:, n % 3], ACT.Exp)
                    m.then_inc(probs, 1)
                if n:
                    job, t, hs, nk = units[n - 1]
                    k, w = G * -(-nk // P), min(P, nk)
                    act.wait_ge(turned, n)
                    if n >= 3:
                        act.wait_ge(outs, n - 2)
                    nc.scalar.copy(PT[0:w, (n - 1) % 2, 0:k, :], T[0:w, 0:k, :]).then_inc(pt_copied, 1)

        @block.vector
        def _(dve):
            link = Chain(dve, step)
            if bias_wait:
                bias_wait(dve)
            for n in range(len(units) + 2):
                if n < len(units):
                    job, t, hs, nk = units[n]
                    u = n % 2
                    dve.wait_ge(scores, n + 1)
                    if n >= 2:
                        dve.wait_ge(turned, n - 1)
                    nc.vector.scalar_tensor_tensor(L[:, u, :, 0:nk], S(n, nk), job["scale"], job["bias"](t, hs, nk),
                                                   ALU.mult, ALU.add).then_inc(scaled, 1)
                    dve.wait_ge(scaled, n + 1)
                    if job.get("sinks") is None:
                        nc.vector.tensor_reduce(mx[:, n % 3], L[:, u, :, 0:nk], AX.X, ALU.max, negate=True).then_inc(maxed, 1)
                    else:
                        link(nc.vector.tensor_reduce(mx[:, n % 3], L[:, u, :, 0:nk], AX.X, ALU.max))
                        link(nc.vector.tensor_tensor(mx[:, n % 3], mx[:, n % 3], job["sinks"][:, hs], ALU.max))
                        link(nc.vector.tensor_tensor(es[:, n % 3], job["sinks"][:, hs], mx[:, n % 3], ALU.subtract))
                        nc.vector.tensor_scalar(mx[:, n % 3], mx[:, n % 3], -1.0, None, ALU.mult).then_inc(maxed, 1)
                if n >= 2:
                    job, t, hs, nk = units[n - 2]
                    u, hd = n % 2, job["hd"]
                    dve.wait_ge(probs, n - 1)
                    dve.wait_ge(outs, n - 1)
                    if job.get("sinks") is not None:
                        link(nc.vector.tensor_tensor(sm[:, (n - 2) % 3], sm[:, (n - 2) % 3], es[:, (n - 2) % 3], ALU.add))
                    link(nc.vector.reciprocal(sm[:, (n - 2) % 3], sm[:, (n - 2) % 3]))
                    for f in job.get("factors", ()):
                        link(nc.vector.tensor_tensor(sm[:, (n - 2) % 3], sm[:, (n - 2) % 3], f(t, hs), ALU.mult))
                    out = job["out"][:, t, hs.start * hd:hs.stop * hd].rearrange("p (h w) -> p h w", h=G)
                    dst = tmp[:, 0:G * hd].rearrange("p (h w) -> p h w", h=G) if job.get("add") else out
                    nc.vector.tensor_tensor(dst, O(n - 2, hd).rearrange("p (h w) -> p h w", h=G),
                                            sm[:, (n - 2) % 3].unsqueeze(2).to_broadcast([P, G, hd]), ALU.mult).then_inc(written, 1)
                    dve.wait_ge(written, n - 1)
                    if job.get("add"):
                        link(nc.vector.tensor_tensor(out, out, dst, ALU.add))
                if side and n < len(blocks):
                    dve.wait_ge(side_landed[n % 2], modulation.LANDED * (n // 2 + 1))
                    modulation.accumulate(dve, side_slots, n % 2, modulation.mod[:, blocks[n] * MB:(blocks[n] + 1) * MB], side_step,
                                          modulation.STEPS * n)

        if side:
            @block.sync
            def _(sp):
                for n, j in enumerate(blocks):
                    if n >= 2:
                        sp.wait_ge(side_step, modulation.STEPS * (n - 1))
                    modulation.load(sp, side_slots, n % 2, j * MB, side_landed[n % 2])
    stage.close()
    arena.at = mark


GLA_HEADS, GLA_K, GLA_V, GLA_RANK = 4, 64, 128, 16
HG_HEADS, HG_K, HG_V = 4, 128, 128


def decay_stage(nc, tag, abT, up, brow, landed, g, consts, arena, banks):
    stage = Stage(nc, tag)
    sem = stage.sem
    mark = arena.at
    W = GLA_HEADS * GLA_K
    z, e = arena.take([TILES, W]), arena.take([TILES, W])
    made, absolute, logged, step, astep = (sem(n) for n in ("z", "abs", "log", "dve", "act"))
    with nc.Block() as block:
        @block.tensor
        def _(pe):
            pe.wait_ge(landed, 32)
            for t in range(TILES):
                nc.tensor.matmul(banks[0][:, t * W:(t + 1) * W], abT[:, 0, t * P:(t + 1) * P], up, start=True, stop=False)
                m = nc.tensor.matmul(banks[0][:, t * W:(t + 1) * W], consts["ones"][0:1, :], brow, start=False, stop=True)
            m.then_inc(made, 1)

        @block.scalar
        def _(act):
            link = Chain(act, astep)
            act.wait_ge(absolute, 1)
            link(nc.scalar.activation(e, e, ACT.Exp, scale=-1.0))
            nc.scalar.activation(e, e, ACT.Ln, bias=1.0).then_inc(logged, 1)

        @block.vector
        def _(dve):
            link = Chain(dve, step)
            dve.wait_ge(made, 1)
            link(nc.vector.tensor_copy(z, banks[0][:, 0:TILES * W].rearrange("p (t n) -> p t n", t=TILES)))
            link(nc.vector.scalar_tensor_tensor(e, z, -1.0, z, ALU.mult, ALU.max))
            dve.sem_inc(absolute, 1)
            link(nc.vector.tensor_scalar(z, z, 0.0, None, ALU.min))
            dve.wait_ge(logged, 1)
            link(nc.vector.tensor_tensor(z, z, e, ALU.subtract))
            link(nc.vector.tensor_scalar(g, z, 1.0 / 16.0, None, ALU.mult))
    stage.close()
    arena.at = mark


def gla_stage(nc, tag, g, qT, kT, k, v, out, consts, arena, psum, banks):
    stage = Stage(nc, tag)
    sem = stage.sem
    mark = arena.at
    FC = GLA_HEADS * GLA_K // P
    W = GLA_HEADS * GLA_K
    eb, ei = arena.take([FC, TOK]), arena.take([FC, TOK])
    er = arena.take([TILES, W])
    AT = arena.take([2, 4, P])
    St = arena.take([CHUNKS - 1, FC, GLA_V])
    sums, exps, decayed, attn, masked, upd, states, outs, step = (
        sem(n) for n in ("sums", "exps", "decayed", "attn", "masked", "upd", "states", "outs", "dve"))
    Bs, Rs = banks[0][:, :].rearrange("p (f n) -> p f n", f=FC), banks[1][:, :].rearrange("p (t n) -> p t n", t=TILES)

    def U(c, rows, f):
        at = (c // 2) * FC * GLA_V + f * GLA_V
        return banks[4 + c % 2][rows, at:at + GLA_V]

    with nc.Block() as block:
        @block.tensor
        def _(pe):
            for f in range(FC):
                for t in range(TILES):
                    nc.tensor.matmul(Bs[:, f, t * P:(t + 1) * P], g[:, t, f * P:(f + 1) * P], consts["upto"][:, :], start=True, stop=True)
            for t in range(TILES):
                m = nc.tensor.matmul(Rs[:, t, :], consts["after"][:, :], g[:, t, :], start=True, stop=True)
            m.then_inc(sums, 1)
            pe.wait_ge(decayed, 1)
            for h in range(GLA_HEADS):
                rows = slice(64 * (h % 2), 64 * (h % 2) + 64)
                for t in range(TILES):
                    n = (h // 2) * TILES + t
                    m = nc.tensor.matmul(banks[2 + h % 2][:, n * P:(n + 1) * P], ei[rows, h // 2, t * P:(t + 1) * P],
                                         eb[rows, h // 2, t * P:(t + 1) * P], start=True, stop=True)
            m.then_inc(attn, 1)
            for c in range(CHUNKS - 1):
                rows, t = slice(64 * (c % 2), 64 * (c % 2) + 64), c // 2
                for h in range(GLA_HEADS):
                    m = nc.tensor.matmul(U(c, slice(64 * (h % 2), 64 * (h % 2) + 64), h // 2), er[rows, t, h * GLA_K:(h + 1) * GLA_K],
                                         v[rows, t, h * GLA_V:(h + 1) * GLA_V], start=True, stop=True, skip_group_check=True)
            m.then_inc(upd, 1)
            pe.wait_ge(masked, 1)
            pe.wait_ge(states, 1)
            for h in range(GLA_HEADS):
                rows = slice(64 * (h % 2), 64 * (h % 2) + 64)
                for t in range(TILES):
                    n = (h // 2) * TILES + t
                    o = banks[6 + h % 2][:, n * P:(n + 1) * P]
                    m = nc.tensor.matmul(o, AT[:, h % 2, n, :], v[:, t, h * GLA_V:(h + 1) * GLA_V], start=True, stop=False,
                                         skip_group_check=True)
                    for c in (2 * t, 2 * t + 1):
                        if c:
                            half = slice(64 * (c % 2), 64 * (c % 2) + 64)
                            m = nc.tensor.matmul(o[half, :], eb[rows, h // 2, c * CHUNK:(c + 1) * CHUNK], St[rows, c - 1, h // 2, :],
                                                 start=False, stop=True, skip_group_check=True)
            m.then_inc(outs, 1)

        dec = arena.take([FC, CHUNKS])

        @block.scalar
        def _(act):
            act.wait_ge(sums, 1)
            nc.scalar.activation(eb, Bs, ACT.Exp)
            nc.scalar.activation(ei, Bs, ACT.Exp, scale=-1.0)
            nc.scalar.activation(er, Rs, ACT.Exp).then_inc(exps, 1)

        @block.vector
        def _(dve):
            link = Chain(dve, step)
            dve.wait_ge(exps, 1)
            link(nc.vector.tensor_copy(dec, eb.rearrange("p f (c n) -> p f c n", n=CHUNK)[:, :, :, CHUNK - 1]))
            link(nc.vector.scalar_tensor_tensor(eb, qT, GLA_K ** -0.5, eb, ALU.mult, ALU.mult))
            link(nc.vector.tensor_tensor(ei, kT, ei, ALU.mult))
            link(nc.vector.tensor_tensor(er, k, er, ALU.mult))
            dve.sem_inc(decayed, 1)
            dve.wait_ge(attn, 1)
            for par in range(2):
                link(nc.vector.tensor_tensor(AT[:, par], banks[2 + par][:, :].rearrange("p (n k) -> p n k", n=4),
                                             consts["upto"][:, :].unsqueeze(1).to_broadcast([P, 4, P]), ALU.mult))
            dve.sem_inc(masked, 1)
            dve.wait_ge(upd, 1)
            for c in range(CHUNKS - 1):
                for f in range(FC):
                    if c == 0:
                        link(nc.vector.tensor_copy(St[:, 0, f, :], U(c, slice(0, P), f)))
                    else:
                        link(nc.vector.scalar_tensor_tensor(St[:, c, f, :], St[:, c - 1, f, :], dec[:, f, c:c + 1],
                                                            U(c, slice(0, P), f), ALU.mult, ALU.add))
            dve.sem_inc(states, 1)
            dve.wait_ge(outs, 1)
            o5 = out.rearrange("p t (h q v) -> p q h t v", q=2, v=GLA_V)
            for par in range(2):
                for t in range(TILES):
                    link(nc.vector.tensor_copy(o5[:, par, :, t, :], banks[6 + par][:, :].rearrange("p (h t v) -> p h t v", h=2, t=2)[:, :, t, :]))
    stage.close()
    arena.at = mark


class Forget:

    def __init__(self, nc, stage, lb_logits, z, f, k, g, gates, arena):
        W = HG_HEADS * HG_K
        self.nc, self.lb_logits, self.z, self.f, self.k, self.g, self.gates = nc, lb_logits, z, f, k, g, gates
        self.l, self.mx = arena.take([2, W]), arena.take([W])
        self.landed, self.sig, self.asked, self.exped, self.made, self.step = (
            stage.sem(n) for n in ("lb", "sig", "lb_asked", "lb_exp", "f_made", "f_dve"))

    def sync(self, sp):
        for i in range(2):
            sp.dma_start(self.l[:, i], self.lb_logits[i].partition_broadcast(P)).then_inc(self.landed, 16)

    def scalar(self, act):
        nc = self.nc
        nc.scalar.activation(self.f, self.z, ACT.Sigmoid).then_inc(self.sig, 1)
        for gates in self.gates:
            nc.scalar.activation(gates, gates, ACT.Sigmoid)
        act.wait_ge(self.asked, 1)
        nc.scalar.activation(self.l, self.l, ACT.Exp).then_inc(self.exped, 1)
        act.wait_ge(self.made, 1)
        nc.scalar.activation(self.g, self.f, ACT.Ln)

    def vector(self, dve):
        nc, l, mx, f = self.nc, self.l, self.mx, self.f
        link = Chain(dve, self.step)
        dve.wait_ge(self.landed, 32)
        link(nc.vector.tensor_tensor(mx, l[:, 0], l[:, 1], ALU.max))
        link(nc.vector.tensor_tensor(l, l, mx.unsqueeze(1).to_broadcast([P, 2, mx.shape[1]]), ALU.subtract))
        dve.sem_inc(self.asked, 1)
        dve.wait_ge(self.exped, 1)
        link(nc.vector.tensor_tensor(mx, l[:, 0], l[:, 1], ALU.add))
        link(nc.vector.reciprocal(mx, mx))
        link(nc.vector.tensor_tensor(l[:, 0], l[:, 0], mx, ALU.mult))
        link(nc.vector.tensor_scalar(l[:, 1], l[:, 0], -1.0, 1.0, ALU.mult, ALU.add))
        dve.wait_ge(self.sig, 1)
        link(nc.vector.tensor_tensor(f, f, l[:, 1].unsqueeze(1).to_broadcast(list(f.shape)), ALU.mult))
        link(nc.vector.tensor_tensor(f, f, l[:, 0].unsqueeze(1).to_broadcast(list(f.shape)), ALU.add))
        dve.sem_inc(self.made, 1)
        link(nc.vector.tensor_scalar(self.k, f, -1.0, 1.0, ALU.mult, ALU.add))


def hgrn_stage(nc, tag, g, qT, kT, k, v, out, consts, arena, banks):
    stage = Stage(nc, tag)
    sem = stage.sem
    mark = arena.at
    H, W = HG_HEADS, HG_HEADS * HG_K
    U = H * TILES
    b, eb, er = arena.take([H, TOK]), arena.take([H, TOK]), arena.take([TILES, W])
    ex, ql, kl = (arena.take([2, H * TOK]) for _ in range(3))
    A, tmp = arena.take([U, P]), arena.take([U, P])
    St, dec = arena.take([CHUNKS - 1, H, HG_V]), arena.take([H, CHUNKS])
    sums, exps, decayed, upd, asked, exped, split, level, added, states, outs, step = (
        sem(n) for n in ("sums", "exps", "decayed", "upd", "asked", "exped", "split", "level", "added", "states", "outs", "dve"))
    collected = sem("collected")
    flat = lambda ap: ap.rearrange("p h n -> p (h n)")
    with nc.Block() as block:
        @block.tensor
        def _(pe):
            for h in range(H):
                for t in range(TILES):
                    nc.tensor.matmul(banks[h // 2][:, (h % 2) * TOK + t * P:(h % 2) * TOK + (t + 1) * P],
                                     g[:, t, h * P:(h + 1) * P], consts["upto"][:, :], start=True, stop=True)
            for t in range(TILES):
                m = nc.tensor.matmul(banks[2 + t][:, :], consts["after"][:, :], g[:, t, :], start=True, stop=True)
            m.then_inc(sums, 1)
            pe.wait_ge(decayed, 1)
            for c in range(CHUNKS - 1):
                rows = slice(64 * (c % 2), 64 * (c % 2) + 64)
                for h in range(H):
                    m = nc.tensor.matmul(banks[4 + c][:, h * HG_V:(h + 1) * HG_V], er[rows, c // 2, h * P:(h + 1) * P],
                                         v[rows, c // 2, h * HG_V:(h + 1) * HG_V], start=True, stop=True)
            m.then_inc(upd, 1)
            for n in range(len(LEVELS) + 1):
                if n < len(LEVELS):
                    pe.wait_ge(split, n + 1)
                if n >= 2:
                    pe.wait_ge(added, n - 1)
                for u in range(U):
                    s = slice(u * P, (u + 1) * P)
                    kk, qq = (kl[:, n % 2, s], ql[:, n % 2, s]) if n < len(LEVELS) else (flat(kT)[:, s], flat(qT)[:, s])
                    m = nc.tensor.matmul(banks[2 * (n % 2) + u // 4][:, (u % 4) * P:(u % 4 + 1) * P], kk, qq, start=True, stop=True)
                m.then_inc(level, 1)
            pe.wait_ge(states, 1)
            pe.wait_ge(collected, 1)
            for t in range(TILES):
                for h in range(H):
                    o = banks[2 + t][:, h * HG_V:(h + 1) * HG_V]
                    m = nc.tensor.matmul(o, A[:, h * TILES + t, :], v[:, t, h * HG_V:(h + 1) * HG_V], start=True, stop=False,
                                         skip_group_check=True)
                    for c in (2 * t, 2 * t + 1):
                        if c:
                            half = slice(64 * (c % 2), 64 * (c % 2) + 64)
                            m = nc.tensor.matmul(o[half, :], eb[:, h, c * CHUNK:(c + 1) * CHUNK], St[:, c - 1, h, :],
                                                 start=False, stop=True, skip_group_check=True)
            m.then_inc(outs, 1)

        @block.scalar
        def _(act):
            act.wait_ge(sums, 1)
            for i in range(2):
                src = banks[i][:, :].rearrange("p (h n) -> p h n", h=2)
                nc.scalar.activation(eb[:, 2 * i:2 * i + 2, :], src, ACT.Exp)
                nc.scalar.copy(b[:, 2 * i:2 * i + 2, :], src)
            for t in range(TILES):
                m = nc.scalar.activation(er[:, t], banks[2 + t][:, :], ACT.Exp)
            m.then_inc(exps, 1)
            for n in range(len(LEVELS)):
                act.wait_ge(asked, n + 1)
                nc.scalar.activation(ex[:, n % 2], ex[:, n % 2], ACT.Exp).then_inc(exped, 1)

        @block.vector
        def _(dve):
            link = Chain(dve, step)
            link(nc.vector.memset(ql, 0.0))
            link(nc.vector.memset(kl, 0.0))
            dve.wait_ge(exps, 1)
            link(nc.vector.tensor_copy(dec, eb.rearrange("p h (c n) -> p h c n", n=CHUNK)[:, :, :, CHUNK - 1]))
            link(nc.vector.tensor_tensor(eb, eb, qT, ALU.mult))
            link(nc.vector.tensor_tensor(er, er, k, ALU.mult))
            dve.sem_inc(decayed, 1)

            def halves(ap, m):
                v4 = ap.rearrange("p (n two m) -> p n two m", two=2, m=m)
                return v4[:, :, 0, :], v4[:, :, 1, :]

            def exponents(n):
                m = LEVELS[n]
                (b0, b1), (e0, e1) = halves(flat(b), m), halves(ex[:, n % 2], m)
                r = b0[:, :, m - 1:m].to_broadcast([P, H * TOK // (2 * m), m])
                nc.vector.tensor_tensor(e0, r, b0, ALU.subtract)
                link(nc.vector.tensor_tensor(e1, b1, r, ALU.subtract))
                dve.sem_inc(asked, 1)

            def factors(n):
                m = LEVELS[n]
                e0, e1 = halves(ex[:, n % 2], m)
                dve.wait_ge(exped, n + 1)
                nc.vector.tensor_tensor(halves(kl[:, n % 2], m)[0], halves(flat(kT), m)[0], e0, ALU.mult)
                link(nc.vector.tensor_tensor(halves(ql[:, n % 2], m)[1], halves(flat(qT), m)[1], e1, ALU.mult))
                dve.sem_inc(split, 1)

            def collect(n):
                dve.wait_ge(level, n + 1)
                mask = consts["levels"][:, n * P:(n + 1) * P].unsqueeze(1).to_broadcast([P, 4, P])
                dst = tmp if n else A
                for i in range(2):
                    r = nc.vector.tensor_tensor(dst[:, 4 * i:4 * i + 4, :],
                                                banks[2 * (n % 2) + i][:, :].rearrange("p (u k) -> p u k", u=4), mask, ALU.mult)
                link(r)
                dve.sem_inc(added, 1)
                if n:
                    link(nc.vector.tensor_tensor(A, A, tmp, ALU.add))

            def carry():
                dve.wait_ge(upd, 1)
                for c in range(CHUNKS - 1):
                    u3 = banks[4 + c][:, :].rearrange("p (h v) -> p h v", h=H)
                    if c == 0:
                        link(nc.vector.tensor_copy(St[:, 0], u3))
                    else:
                        link(nc.vector.tensor_tensor(St[:, c], St[:, c - 1], dec[:, :, c:c + 1].to_broadcast([P, H, HG_V]), ALU.mult))
                        link(nc.vector.tensor_tensor(St[:, c], u3, St[:, c], ALU.add))

            last = len(LEVELS)
            exponents(0)
            for n in range(last + 2):
                if n + 1 < last:
                    exponents(n + 1)
                if n < last:
                    factors(n)
                if n == 0:
                    carry()
                if n:
                    collect(n - 1)
            dve.sem_inc(collected, 1)
            dve.sem_inc(states, 1)
            dve.wait_ge(outs, 1)
            for t in range(TILES):
                link(nc.vector.tensor_copy(out[:, t, :], banks[2 + t][:, :]))
    stage.close()
    arena.at = mark


def rope_stage(nc, tag, jobs, arena):
    stage = Stage(nc, tag)
    step = stage.sem("dve")
    mark = arena.at
    half = ROPE_DIM // 2
    with nc.Block() as block:
        @block.vector
        def _(dve):
            link = Chain(dve, step)
            tmp = arena.take([4, HEADS, half])
            for rows, cos, sin in jobs:
                np_, n = rows.shape[0], rows.shape[1]
                cb, sb = (a.unsqueeze(1).to_broadcast([np_, n, half]) for a in (cos, sin))
                t1, t2 = rows[:, :, 0:half], rows[:, :, half:ROPE_DIM]
                a, b, c, d = (tmp[0:np_, i, 0:n, :] for i in range(4))
                nc.vector.tensor_tensor(a, t1, cb, ALU.mult)
                nc.vector.tensor_tensor(b, t2, sb, ALU.mult)
                nc.vector.tensor_tensor(c, t2, cb, ALU.mult)
                link(nc.vector.tensor_tensor(d, t1, sb, ALU.mult))
                nc.vector.tensor_tensor(t1, a, b, ALU.subtract)
                link(nc.vector.tensor_tensor(t2, c, d, ALU.add))
    stage.close()
    arena.at = mark


def compress_stage(nc, tag, inT, pos, w_k, w_v, kcT, vc, consts, arena, banks, beside):
    stage = Stage(nc, tag)
    sem = stage.sem
    mark = arena.at
    hd = 64
    prow, posT = arena.take([hd], parts=CMP_LEN), arena.take([CMP_LEN], parts=hd)
    w = arena.take([2, CMP_LEN, hd], parts=hd)
    blk = arena.take([4, CMP_LEN, N_CMP], parts=hd)
    kc, tmp = arena.take([2, hd], parts=N_CMP), arena.take([4, 2, ROPE_DIM // 2], parts=N_CMP)
    landed, turned, added, made, roped, back, step = (sem(n) for n in ("w", "turned", "added", "made", "roped", "back", "dve"))
    other = beside(stage)
    with nc.Block() as block:
        @block.scalar
        def _(act):
            other.scalar(act)

        @block.sync
        def _(sp):
            sp.dma_start(prow, pos).then_inc(landed, 16)
            sp.dma_start(w[:, 0], w_k.rearrange("(l d) o -> d l o", d=hd)).then_inc(landed, 16)
            sp.dma_start(w[:, 1], w_v.rearrange("(l d) o -> d l o", d=hd)).then_inc(landed, 16)
            other.sync(sp)

        @block.tensor
        def _(pe):
            pe.wait_ge(landed, 48)
            nc.tensor.transpose(banks[0][0:hd, 0:CMP_LEN], prow, consts["ident"][0:CMP_LEN, 0:CMP_LEN]).then_inc(turned, 1)
            pe.wait_ge(added, 1)
            for l in range(CMP_LEN):
                for u in range(4):
                    m = nc.tensor.matmul(banks[1][32 * u:32 * u + N_CMP, 0:hd], blk[:, u, l, :], w[:, u // 2, l, :],
                                         start=(l == 0), stop=(l == CMP_LEN - 1), skip_group_check=True)
            m.then_inc(made, 1)
            pe.wait_ge(roped, 1)
            for g in range(2):
                m = nc.tensor.transpose(banks[2][0:hd, g * 64:g * 64 + N_CMP], kc[:, g, :], consts["ident"][0:N_CMP, 0:N_CMP])
            m.then_inc(back, 1)

        @block.vector
        def _(dve):
            link = Chain(dve, step)
            dve.wait_ge(turned, 1)
            link(nc.vector.tensor_copy(posT, banks[0][0:hd, 0:CMP_LEN]))
            for u in range(4):
                src = inT[:, u, :]
                windows = bass.AP(src.tensor, src.offset, [src.ap[0], [1, CMP_LEN], [CMP_STRIDE, N_CMP]])
                link(nc.vector.tensor_tensor(blk[:, u], windows, posT.unsqueeze(2).to_broadcast([hd, CMP_LEN, N_CMP]), ALU.add))
            dve.sem_inc(added, 1)
            other.vector(dve)
            dve.wait_ge(made, 1)
            for u in range(4):
                link(nc.vector.tensor_copy((kc, vc)[u // 2][:, u % 2, :], banks[1][32 * u:32 * u + N_CMP, 0:hd]))
            half = ROPE_DIM // 2
            cs = consts["rope_cmp"]
            cb, sb = (cs[0:N_CMP, i * half:(i + 1) * half].unsqueeze(1).to_broadcast([N_CMP, 2, half]) for i in range(2))
            t1, t2 = kc[:, :, 0:half], kc[:, :, half:ROPE_DIM]
            for i, (x_, y_) in enumerate(((t1, cb), (t2, sb), (t2, cb), (t1, sb))):
                link(nc.vector.tensor_tensor(tmp[:, i], x_, y_, ALU.mult))
            link(nc.vector.tensor_tensor(t1, tmp[:, 0], tmp[:, 1], ALU.subtract))
            link(nc.vector.tensor_tensor(t2, tmp[:, 2], tmp[:, 3], ALU.add))
            dve.sem_inc(roped, 1)
            dve.wait_ge(back, 1)
            link(nc.vector.tensor_copy(kcT, banks[2][0:hd, 0:2 * 64].rearrange("p (g n) -> p g n", g=2)[:, :, 0:N_CMP]))
    stage.close()
    arena.at = mark


def program(nc, ins, const_dram, out, dump=None):
    psum = nc.alloc_psum_tensor("psum", [P, 4096], F32)
    banks = [psum[:, 512 * i:512 * (i + 1)] for i in range(8)]
    x, h, hT = (nc.alloc_sbuf_tensor(n, s, F32)[:, :, :] for n, s in (("x", [P, TILES, D]), ("h", [P, TILES, D]), ("hT", [P, DC, TOK])))
    consts = alloc_consts(nc)
    ident = consts["ident"]
    scratch = nc.dram_tensor("skew_scratch", (2, HEADS, P, SKEW), F32).ap()
    mod_scratch = nc.dram_tensor("mod_scratch", (6 * MB,), F32).ap()
    ccol = nc.alloc_sbuf_tensor("ccol", [P, DC], F32)[:, :]
    norm_tile = nc.alloc_sbuf_tensor("norm_w", [P, D], F32)[:, :]
    norm_sums = nc.alloc_sbuf_tensor("norm_sums", [P, 2, TILES], F32)[:, :, :]
    arena = Arena(nc, (nc.sbuf_usable_end - nc.sbuf_base) // 4 - ARENA_SPARE)
    rows = lambda ap: ap.rearrange("(t p) d -> p t d", p=P)
    whole = Stage(nc, "whole")
    norm_w, skewed = NormWeight(whole, norm_tile, norm_sums), SkewedBias(whole, scratch)

    def experts_of(tag, names, layer):
        stage, mem = Stage(nc, tag), alloc_moe(arena)
        return stage, mem, Experts(stage, mem, extra_slot(arena), *(ins[n][layer] for n in names))

    def moe(plan, gate2, next_norm, after=None):
        stage, mem, experts = plan
        moe_stage(nc, stage, experts, x, h, hT, gate2, consts, mem, banks, lambda sp: norm_w.fetch(sp, next_norm), after)
        arena.top = arena.words

    def normed(tag, scale=None, shift=None, loads=None, ready_too=None):
        norm_stage(nc, tag, x, h, norm_w, scale, shift, hT, ident, banks, loads=loads, ready_too=ready_too)

    def extra_of(plan):
        return lambda sp: plan[2].load_up(sp, 2, 0, 1)

    def ahead_of(plan, w_row):
        def loads(sp):
            norm_w.fetch(sp, w_row)
            plan[2].prefetch(sp)
        return loads

    later = 6
    for layer in range(2):
        L = f"l{layer}"
        mod = arena.take([6 * D])
        modulation = Modulation(nc, ccol, ins["ada_w"][layer], ins["ada_b"][layer], mod)
        if layer == 0:
            load = lambda n: (consts[n][0:const_dram[n].shape[0], :], const_dram[n])
            start_stage(nc, ins["c"][0], ccol, modulation, [0, 1, 2, 3], [load("ones")],
                        [(x[:, :, :], rows(ins["x"][0]))] + [load(n) for n in consts if n != "ones"],
                        (const_dram["hot_window"], const_dram["hot_causal"]), ins["rel_bias"], skewed, norm_w,
                        ins["norm1_w"][0], arena, banks, consts)
        shift1, scale1, gate1, shift2, scale2, gate2 = (mod[:, i * D:(i + 1) * D] for i in range(6))
        mark = arena.at
        arena.take([WEIGHTS])
        w_in = ins[("even_w_in", "odd_w_in")[layer]][0]
        in_columns = Columns(nc, L + "_in", w_in, DC, w_in.shape[1] // (8, 6)[layer], arena, at=mark)
        normed(L + "_norm1", scale1, shift1, loads=in_columns.fetch, ready_too=(mod_back, 16) if layer else None)
        out_columns = Columns(nc, L + "_out", ins[("even_w_out", "odd_w_out")[layer]][0], DC, 512, arena, at=mark)
        o = arena.take([TILES, D])
        bias = arena.take([HEADS, TOK])
        if layer == 0:
            N = ins["even_w_in"].shape[2]
            pr = arena.take([TILES, N])
            project_stage(nc, in_columns, hT, pr, arena, banks,
                          side=(modulation, 4 * MB))
            sinks, sinks_landed = arena.take([HEADS]), whole.sem("sinks")
            up, brow, up_landed = arena.take([256], parts=GLA_RANK), arena.take([256], parts=1), whole.sem("gate_up")

            def small_loads(sp):
                skewed.load(sp, 0, bias)
                sp.dma_start(sinks, ins["a_sinks"][0].partition_broadcast(P)).then_inc(sinks_landed, 16)
                sp.dma_start(up, ins["b_gate_up"][0]).then_inc(up_landed, 16)
                sp.dma_start(brow, ins["b_gate_bias"]).then_inc(up_landed, 16)

            qa, ka, va, qb, kb, vb, rb, ab = (pr[:, :, a:b] for a, b in (
                (0, 512), (512, 640), (640, 768), (768, 1024), (1024, 1280), (1280, 1792), (1792, 2304), (2304, 2320)))
            head_norm_stage(nc, L + "_qknorm", [(qa, 8, 64, ins["a_q_norm"][0]), (ka, 2, 64, ins["a_k_norm"][0])], arena,
                            finish=lambda st: modulation.finisher(st, list(range(4, 12)), banks, consts),
                            loads=small_loads)
            qT, kT = arena.take([HEADS, TOK], parts=64), arena.take([2, TOK], parts=64)
            qbT, kbT, abT = arena.take([2, TOK]), arena.take([2, TOK]), arena.take([1, TOK], parts=16)
            turn_stage(nc, L + "_turn", [(qa, 64, 8, qT), (ka, 64, 2, kT), (qb, P, 2, qbT), (kb, P, 2, kbT), (ab, 16, 1, abT)],
                       ident, banks)
            raw = arena.take([later * MB])
            side_slots = arena.view([2, DC, MB], mark, P), arena.take([2, MB], parts=1)
            following = Modulation(nc, ccol, ins["ada_w"][1], ins["ada_b"][1], raw)
            attend_stage(nc, L + "_swa", [dict(
                qT=qT, kT=kT, v=lambda kt, kv: va[:, kt, kv * 64:(kv + 1) * 64], hd=64, kv_of=lambda hh: hh // 4, scale=64 ** -0.5,
                bias=lambda t, hs, nk: bias[:, hs, TOK - nk:], out=o[:, :, 0:512], sinks=sinks)], ident, arena, psum,
                side=(following, list(range(later)), side_slots), bias_wait=lambda eng: (skewed.wait(eng, 0), eng.wait_ge(sinks_landed, 16)))
            g = arena.take([TILES, 256])
            decay_stage(nc, L + "_decay", abT, up, brow, up_landed, g, consts, arena, banks)
            ob = arena.take([TILES, 512])
            gla_stage(nc, L + "_gla", g, qbT, kbT, kb, vb, ob, consts, arena, psum, banks)
            head_norm_stage(nc, L + "_onorm", [(ob, 4, 128, ins["b_out_norm"][0])], arena,
                            finish=lambda st: following.finisher(st, list(range(later)), banks, consts), loads=out_columns.fetch,
                            gated=(rb, o[:, :, 512:1024]))
            kept, mod_back = whole.sem("kept"), whole.sem("mod_back")
        else:
            pr = arena.take([TILES, 3 * D])
            project_stage(nc, in_columns, hT, pr, arena, banks,
                          side=(modulation, later * MB))
            q, k, v = (pr[:, :, i * D:(i + 1) * D] for i in range(3))
            head_norm_stage(nc, L + "_qknorm", [(q, 8, 128, ins["c_q_norm"][0]), (k, 8, 128, ins["c_k_norm"][0])], arena,
                            finish=lambda st: modulation.finisher(st, list(range(later, 12)), banks, consts),
                            loads=lambda sp: (skewed.load(sp, 1, bias), out_columns.fetch(sp)))
            qT, kT = arena.take([HEADS, TOK]), arena.take([HEADS, TOK])
            turn_stage(nc, L + "_turn", [(q, P, 8, qT), (k, P, 8, kT)], ident, banks)
            attend_stage(nc, L + "_attn", [dict(
                qT=qT, kT=kT, v=lambda kt, kv: v[:, kt, kv * P:(kv + 1) * P], hd=P, kv_of=lambda hh: hh, scale=P ** -0.5,
                bias=lambda t, hs, nk: bias[:, hs, TOK - nk:], out=o)], ident, arena, psum,
                bias_wait=lambda eng: skewed.wait(eng, 1))
        turn_stage(nc, L + "_oturn", [(o, P, DC, hT)], ident, banks)
        arena.at = mark
        def keep(sp):
            sp.dma_start(mod_scratch.unsqueeze(0), raw[0:1, :]).then_inc(kept, 16)
            sp.wait_ge(kept, 16)

        plan = experts_of(L + "_moe", ("moe_w_group", "moe_b_group", "moe_w_expert", "moe_b_expert", "moe_w1", "moe_w3", "moe_w2"), layer)
        gate_both = bass.AP(gate1.tensor, gate1.offset, [gate1.ap[0], [0, TILES], [1, D]])
        project_stage(nc, out_columns, hT, x, arena, banks, gate=gate_both, add=True,
                      ahead=ahead_of(plan, ins["norm2_w"][layer]), first=keep if layer == 0 else None, tmp=h[:, :, 0:512])
        if dump: dump(L + "_mix", x)
        arena.at = mark
        normed(L + "_norm2", scale2, shift2, extra_of(plan))

        def bring_back(sp):
            sp.dma_start(arena.view([later * MB], 0, P), mod_scratch.partition_broadcast(P)).then_inc(mod_back, 16)

        moe(plan, gate2, ins["attn_norm_2"][0] if layer else ins["norm1_w"][1], bring_back if layer == 0 else None)
        if dump: dump(L + "_moe", x)
        arena.at = 0

    mark = arena.at
    arena.take([WEIGHTS])
    N = ins["w_in_2"].shape[2]
    in_columns = Columns(nc, "s_in", ins["w_in_2"][0], DC, N // 12, arena, at=mark)
    normed("s_norm1", loads=in_columns.fetch)
    out_columns = Columns(nc, "s_out", ins["w_out_2"][0], DC, 512, arena, at=mark)
    nsa_columns = Columns(nc, "s_brn", ins["w_br_nsa_2"][0], DC // 2, 512, arena)
    o = arena.take([TILES, D])
    pr = arena.take([TILES, N])
    project_stage(nc, in_columns, hT, pr, arena, banks)
    kv = pr[:, :, 512:1280].rearrange("p t (s g d) -> p t s g d", s=6, g=2)
    hk, g = arena.take([TILES, 512]), arena.take([TILES, 512])
    mark2 = arena.at
    half = ROPE_DIM // 2
    rope = consts["rope"][:, :].rearrange("p (t n) -> p t n", t=TILES)
    heads = lambda ap: ap.rearrange("p (n d) -> p n d", d=64)
    jobs = []
    for t in range(TILES):
        cs = (rope[:, t, 0:half], rope[:, t, half:])
        jobs += [(heads(pr[:, t, 0:512]), *cs), (kv[:, t, 2], *cs), (kv[:, t, 4], *cs)]
    rope_stage(nc, "s_rope", jobs, arena)
    qT, cT = arena.take([HEADS, TOK], parts=64), arena.take([4, TOK], parts=64)
    ksT, kwT = arena.take([2, TOK], parts=64), arena.take([2, TOK], parts=64)
    turn_stage(nc, "s_turn", [(pr[:, :, 0:512], 64, 8, qT), (pr[:, :, 512:768], 64, 4, cT), (pr[:, :, 768:896], 64, 2, ksT),
                              (pr[:, :, 1024:1152], 64, 2, kwT)], ident, banks)
    kcT, vc = arena.take([2, N_CMP], parts=64), arena.take([2, 64], parts=N_CMP)
    hq, hf, hi, hg = (pr[:, :, 1304 + i * 512:1304 + (i + 1) * 512] for i in range(4))
    compress_stage(nc, "s_cmp", cT, ins["cmp_pos_2"][0], ins["w_cmp_k_2"][0], ins["w_cmp_v_2"][0], kcT, vc, consts, arena, banks,
                   beside=lambda st: Forget(nc, st, ins["hg_lb_logits_2"], hf, hf, hk, g, (pr[:, :, 1280:1304], pr[:, :, 3352:]),
                                            arena))
    gates = pr[:, :, 1280:1304].rearrange("p t (h i) -> p i t h", i=3)
    cb = consts["cmp_bias"][:, :].rearrange("p (t n) -> p t n", t=TILES)
    cm = consts["cmp_mask"][:, :].rearrange("p (t n) -> p t n", t=TILES)
    o_nsa = o[:, :, 0:512]
    nsa = dict(qT=qT, hd=64, kv_of=lambda hh: hh // 4, scale=64 ** -0.5, out=o_nsa)
    some = cm[:, :, 0:1]
    attentions = [dict(nsa, kT=kcT, v=lambda kt, g_: vc[:, g_, :], keys=N_CMP,
                       bias=lambda t, hs, nk: cb[:, t, :].unsqueeze(1).to_broadcast([P, HEADS // 2, N_CMP]),
                       factors=[lambda t, hs: gates[:, 0, t, hs], lambda t, hs: some[:, t, :].to_broadcast([P, HEADS // 2])])]
    for i, (kk, s) in enumerate(((ksT, 3), (kwT, 5))):
        attentions.append(dict(nsa, kT=kk, v=lambda kt, g_, s=s: kv[:, kt, s, g_, :], add=True,
                               bias=lambda t, hs, nk: consts["causal"][:, TOK - nk:].unsqueeze(1).to_broadcast([P, HEADS // 2, nk]),
                               factors=[lambda t, hs, i=i: gates[:, i + 1, t, hs]]))
    attend_stage(nc, "s_attn", attentions, ident, arena, psum)
    if dump: dump("s_nsa", o)
    arena.at = mark2
    hqT, hkT = arena.take([HG_HEADS, TOK]), arena.take([HG_HEADS, TOK])
    turn_stage(nc, "s_hturn", [(hq, P, 4, hqT), (hk, P, 4, hkT)], ident, banks)
    o_hg = o[:, :, 512:1024]
    hgrn_stage(nc, "s_hgrn", g, hqT, hkT, hk, hi, o_hg, consts, arena, banks)
    head_norm_stage(nc, "s_hnorm", [(o_hg, 4, 128, ins["hg_norm_2"][0])], arena,
                    loads=lambda sp: (nsa_columns.fetch(sp), out_columns.fetch(sp)), gated=(hg, o_hg))
    arena.at = mark2 - 2 * TILES * 512
    turn_stage(nc, "s_oturn", [(o, P, DC, hT)], ident, banks)
    mixed = arena.take([TILES, D])
    hg_columns = Columns(nc, "s_brh", ins["w_br_hg_2"][0], DC // 2, 512, arena)
    tmp = arena.take([TILES, 512])
    project_stage(nc, nsa_columns, hT[:, 0:4, :], mixed, arena, banks, gate=pr[:, :, 3352:3352 + D], ahead=hg_columns.fetch)
    project_stage(nc, hg_columns, hT[:, 4:8, :], mixed, arena, banks, tmp=tmp, gate=pr[:, :, 3352 + D:], add=True)
    turn_stage(nc, "s_mturn", [(mixed, P, DC, hT)], ident, banks)
    arena.at = mark
    plan = experts_of("s_moe", ("w_grp_2", "b_grp_2", "w_rtr_2", "b_rtr_2", "w_gate_2", "w_up_2", "w_down_2"), 0)
    project_stage(nc, out_columns, hT, x, arena, banks, add=True,
                  ahead=ahead_of(plan, ins["ffn_norm_2"][0]))
    if dump: dump("s_mix", x)
    arena.at = mark
    normed("s_norm2", loads=extra_of(plan))
    moe(plan, None, ins["final_norm_2"])
    norm_stage(nc, "final", x, h, norm_w, None, None, store=rows(out[0]))
    whole.close()


ARENA_SPARE = 32
WEIGHTS = 2 * DC * 512


def extra_slot(arena):
    size = DC * FF
    assert 6 * D + 2 * size <= arena.top and (FF // P) * D <= 5 * D
    return arena.view([DC, FF], 6 * D, P), arena.view([DC, FF], 6 * D + size, P), arena.view([FF // P, D], 0, P)


def alloc_moe(arena):
    W = ROUNDS * E + 4
    shapes = dict(
        w1b=[2, DC, FF], w3b=[2, DC, FF], w2b=[2, FF // P, D], rt=[DC, 36], rb=[36], lg=[TILES, 36], small=[8, 64],
        mask=[TILES, E], slots=[TILES, W], comb=[TILES, W], nsteps=[1], sel=[TILES, P], selw=[TILES, P], selT=[TILES, P],
        xg=[DC, P], hm=[256], sil=[256], hTs=[2, P], y=[2, 512])
    mem = {n: arena.reserve(shape) for n, shape in shapes.items()}
    mem["nsteps"] = mem["nsteps"].bitcast(I32)
    return mem


def kernel(**inputs):
    import numpy as _np
    import concourse.bacc as _bacc
    from concourse import mybir as _mybir
    from concourse.bass_utils import run_bass_kernel_spmd as _run

    nc = _bacc.Bacc("TRN2", target_bir_lowering=False, num_devices=1)
    arrays, ins, consts = {}, {}, {}
    for name, a in inputs.items():
        a = _np.ascontiguousarray(a)
        arrays[f"in_{name}_dram"] = a
        ins[name] = nc.dram_tensor(f"in_{name}_dram", a.shape, _mybir.dt.from_np(a.dtype), kind="ExternalInput").ap()
    for name, a in host_constants().items():
        arrays[f"const_{name}_dram"] = a
        consts[name] = nc.dram_tensor(f"const_{name}_dram", a.shape, _mybir.dt.from_np(a.dtype), kind="ExternalInput").ap()
    out = nc.dram_tensor("out_dram", inputs["x"].shape, F32, kind="ExternalOutput").ap()
    program(nc, ins, consts, out)
    r = _run(nc, [arrays], core_ids=[0])
    return _np.asarray(r.results[0]["out_dram"])
```
